# Optimizing a Trainium2 kernel written in Bass

```python
import jax, jax.numpy as jnp
from jax import lax
import numpy as np
import math

D_MODEL = 1024
BATCH = 1
SEQ = 512
DEPTH = 2

CHUNK = 64
EPS = 1e-6

HEAD_DIM = 64
ATTN_WIDTH = D_MODEL // 2
ATTN_HEADS = ATTN_WIDTH // HEAD_DIM
ROPE_DIM = HEAD_DIM // 4
ROPE_THETA = 500000.0
IDX_HEADS = 4
IDX_DIM = 64
IDX_SCALE = (IDX_DIM ** -0.5) * (IDX_HEADS ** -0.5)
TOPK_MAX = 256
QBLOCK = 64

CONV_WIDTH = D_MODEL // 2
CONV_GROUPS = 8
CONV_K = 3

N_BRANCH = 2
MLP_HIDDEN = 4 * D_MODEL

PROJ_SIZES = (ATTN_WIDTH, ATTN_WIDTH, ATTN_WIDTH, IDX_HEADS * IDX_DIM, IDX_DIM, IDX_HEADS,
              CONV_WIDTH, CONV_WIDTH, CONV_WIDTH, N_BRANCH * D_MODEL)
IN_COLS = sum(PROJ_SIZES)


def rmsnorm(x, g):
    xf = x.astype(jnp.float32)
    y = xf * lax.rsqrt(jnp.mean(xf * xf, axis=-1, keepdims=True) + EPS)
    return (y * g.astype(jnp.float32)).astype(x.dtype)

def rope_tables(T):
    inv = 1.0 / (ROPE_THETA ** (jnp.arange(0, ROPE_DIM, 2, dtype=jnp.float32) / ROPE_DIM))
    ang = jnp.arange(T, dtype=jnp.float32)[:, None] * inv[None, :]
    return jnp.cos(ang), jnp.sin(ang)

def apply_partial_rope(x, cos, sin):
    half = ROPE_DIM // 2
    xr = x[..., :ROPE_DIM].astype(jnp.float32)
    x1, x2 = xr[..., :half], xr[..., half:]
    c = cos[None, :, None, :]
    s = sin[None, :, None, :]
    rot = jnp.concatenate([x1 * c - x2 * s, x2 * c + x1 * s], axis=-1)
    return jnp.concatenate([rot.astype(x.dtype), x[..., ROPE_DIM:]], axis=-1)

def dsa_attention(q, k, v, iq, ik, iw):
    B, T, H, Dh = q.shape
    topk = min(TOPK_MAX, T // 4)
    nblk = T // QBLOCK
    key_pos = jnp.arange(T)
    scale = Dh ** -0.5
    ikf = ik.astype(jnp.float32)

    def block(i):
        t0 = i * QBLOCK
        qb = lax.dynamic_slice_in_dim(q, t0, QBLOCK, axis=1)
        iqb = lax.dynamic_slice_in_dim(iq, t0, QBLOCK, axis=1).astype(jnp.float32)
        iwb = lax.dynamic_slice_in_dim(iw, t0, QBLOCK, axis=1).astype(jnp.float32)
        tpos = t0 + jnp.arange(QBLOCK)
        limit = (tpos // CHUNK + 1) * CHUNK
        admissible = key_pos[None, :] < limit[:, None]
        logits = jnp.einsum('bthd,bsd->bths', iqb, ikf)
        score = jnp.einsum('bths,bth->bts', jax.nn.relu(logits), iwb) * IDX_SCALE
        score = jnp.where(admissible[None], score, -jnp.inf)
        _, idx = lax.top_k(score, topk)
        valid = idx < limit[None, :, None]
        kg = jax.vmap(lambda kk, ii: kk[ii])(k, idx)
        vg = jax.vmap(lambda vv, ii: vv[ii])(v, idx)
        s = jnp.einsum('bthd,btkhd->bthk', qb, kg).astype(jnp.float32) * scale
        s = jnp.where(valid[:, :, None, :], s, -jnp.inf)
        p = jax.nn.softmax(s, axis=-1).astype(v.dtype)
        return jnp.einsum('bthk,btkhd->bthd', p, vg)

    out = lax.map(block, jnp.arange(nblk))
    return out.transpose(1, 0, 2, 3, 4).reshape(B, T, H * Dh)

def short_conv(xc, conv_w):
    T = xc.shape[1]
    xp = jnp.pad(xc, ((0, 0), (CONV_K - 1, 0), (0, 0)))
    out = xp[:, 0:T] * conv_w[0]
    for j in range(1, CONV_K):
        out = out + xp[:, j:j + T] * conv_w[j]
    return out

def first_inputs(seed: int = 0) -> dict:
    key = jax.random.key(seed)
    ks = jax.random.split(key, 12)
    f32 = jnp.float32
    x = jax.random.normal(ks[0], (BATCH, SEQ, D_MODEL), f32)
    norm_mix = 1.0 + 0.02 * jax.random.normal(ks[1], (DEPTH, D_MODEL), f32)
    w_in = jax.random.normal(ks[2], (DEPTH, D_MODEL, IN_COLS), f32) * D_MODEL ** -0.5
    conv_w = jax.random.normal(ks[3], (DEPTH, CONV_K, CONV_WIDTH), f32) * CONV_K ** -0.5
    w_attn_out = jax.random.normal(ks[4], (DEPTH, ATTN_WIDTH, D_MODEL), f32) * ATTN_WIDTH ** -0.5
    w_conv_out = jax.random.normal(ks[5], (DEPTH, CONV_WIDTH, D_MODEL), f32) * CONV_WIDTH ** -0.5
    w_mix_out = jax.random.normal(ks[6], (DEPTH, D_MODEL, D_MODEL), f32) * D_MODEL ** -0.5
    norm_mlp = 1.0 + 0.02 * jax.random.normal(ks[7], (DEPTH, D_MODEL), f32)
    w_mlp_up = jax.random.normal(ks[8], (DEPTH, D_MODEL, MLP_HIDDEN), f32) * D_MODEL ** -0.5
    w_mlp_down = jax.random.normal(ks[9], (DEPTH, MLP_HIDDEN, D_MODEL), f32) * MLP_HIDDEN ** -0.5
    norm_final = 1.0 + 0.02 * jax.random.normal(ks[10], (D_MODEL,), f32)
    return {"x": x, "norm_mix": norm_mix, "w_in": w_in, "conv_w": conv_w,
            "w_attn_out": w_attn_out, "w_conv_out": w_conv_out, "w_mix_out": w_mix_out,
            "norm_mlp": norm_mlp, "w_mlp_up": w_mlp_up, "w_mlp_down": w_mlp_down,
            "norm_final": norm_final}

def first_block(x, norm_mix, w_in, conv_w, w_attn_out, w_conv_out, w_mix_out,
              norm_mlp, w_mlp_up, w_mlp_down, norm_final):
    B, T, D = x.shape
    cos, sin = rope_tables(T)
    offsets = np.cumsum(PROJ_SIZES)[:-1].tolist()
    for l in range(DEPTH):
        u = rmsnorm(x, norm_mix[l])
        proj = u @ w_in[l]
        q, k, v, iq, ik, iw, cB, cC, ch, g = jnp.split(proj, offsets, axis=-1)
        q = apply_partial_rope(q.reshape(B, T, ATTN_HEADS, HEAD_DIM), cos, sin)
        k = apply_partial_rope(k.reshape(B, T, ATTN_HEADS, HEAD_DIM), cos, sin)
        v = v.reshape(B, T, ATTN_HEADS, HEAD_DIM)
        iq = apply_partial_rope(iq.reshape(B, T, IDX_HEADS, IDX_DIM), cos, sin)
        ik = apply_partial_rope(ik[:, :, None, :], cos, sin)[:, :, 0, :]
        y_attn = dsa_attention(q, k, v, iq, ik, iw) @ w_attn_out[l]
        y_conv = (cB * short_conv(cC * ch, conv_w[l])) @ w_conv_out[l]
        gates = jax.nn.sigmoid(g.reshape(B, T, N_BRANCH, D))
        merged = gates[:, :, 0] * y_attn + gates[:, :, 1] * y_conv
        x = x + merged @ w_mix_out[l]
        u = rmsnorm(x, norm_mlp[l])
        x = x + jnp.square(jax.nn.relu(u @ w_mlp_up[l])) @ w_mlp_down[l]
    return rmsnorm(x, norm_final)


DEPTH_2 = 1

ATTN_WIDTH_2 = D_MODEL // 2
ATTN_HEAD_DIM = 64
N_ATTN_HEADS = ATTN_WIDTH_2 // ATTN_HEAD_DIM
MLSTM_WIDTH = D_MODEL - ATTN_WIDTH_2
N_MLSTM_HEADS = 4
MLSTM_HEAD_DIM = MLSTM_WIDTH // N_MLSTM_HEADS
MLSTM_CHUNK = 64
CONV_WIDTH_2 = 4
DILATED_PATTERNS = ((128, 1), (512, 4), (2048, 16))
ATTN_BLOCK = 128
ATTN_SCALE = ATTN_HEAD_DIM ** -0.5
D_FF = ((8 * D_MODEL // 3 + 255) // 256) * 256
N_MOD = 6
RMS_EPS = 1e-6
IN_SPLITS = (ATTN_WIDTH_2, ATTN_WIDTH_2, ATTN_WIDTH_2,
             MLSTM_WIDTH, MLSTM_WIDTH, MLSTM_WIDTH,
             MLSTM_WIDTH,
             N_MLSTM_HEADS, N_MLSTM_HEADS)
IN_COLS_2 = sum(IN_SPLITS)


def rms_norm(x, g):
    xf = x.astype(jnp.float32)
    y = xf * lax.rsqrt(jnp.mean(xf * xf, axis=-1, keepdims=True) + RMS_EPS)
    return (y * g.astype(jnp.float32)).astype(x.dtype)

def modulate(h, shift, scale):
    return h * (1 + scale[:, None, :]) + shift[:, None, :]

def causal_short_conv(x, w, b):
    S = x.shape[1]
    xp = jnp.pad(x, ((0, 0), (CONV_WIDTH_2 - 1, 0), (0, 0)))
    y = b
    for j in range(CONV_WIDTH_2):
        y = y + xp[:, j:j + S] * w[j]
    return y

def dilated_branch(q, k, v, window, dilation):
    B, S, H, Dh = q.shape
    n_back = window // dilation
    assert n_back <= ATTN_BLOCK and S % dilation == 0
    L = S // dilation
    nb = -(-L // ATTN_BLOCK)
    Lp = nb * ATTN_BLOCK

    def to_sub(t):
        t = t.reshape(B, L, dilation, H, Dh).transpose(0, 2, 1, 3, 4)
        t = jnp.pad(t, ((0, 0), (0, 0), (0, Lp - L), (0, 0), (0, 0)))
        return t.reshape(B, dilation, nb, ATTN_BLOCK, H, Dh)

    def with_prev(t):
        prev = jnp.pad(t, ((0, 0), (0, 0), (1, 0), (0, 0), (0, 0), (0, 0)))[:, :, :-1]
        return jnp.concatenate([prev, t], axis=3)

    qb = to_sub(q)
    kb = with_prev(to_sub(k))
    vb = with_prev(to_sub(v))
    s = jnp.einsum('brnqhd,brnkhd->brnhqk', qb, kb).astype(jnp.float32)
    qi = jnp.arange(ATTN_BLOCK)[:, None] + ATTN_BLOCK
    kj = jnp.arange(2 * ATTN_BLOCK)[None, :]
    rel = qi - kj
    band = (rel >= 0) & (rel <= n_back)
    valid = band[None] & ((jnp.arange(nb)[:, None, None] > 0) | (kj[None] >= ATTN_BLOCK))
    s = jnp.where(valid[None, None, :, None], s, -jnp.inf)
    lse = jax.nn.logsumexp(s, axis=-1)
    p = jnp.exp(s - lse[..., None])
    o = jnp.einsum('brnhqk,brnkhd->brnqhd', p.astype(v.dtype), vb)
    o = o.reshape(B, dilation, Lp, H, Dh)[:, :, :L]
    o = o.transpose(0, 2, 1, 3, 4).reshape(B, S, H, Dh)
    lse = lse.transpose(0, 1, 2, 4, 3).reshape(B, dilation, Lp, H)[:, :, :L]
    lse = lse.transpose(0, 2, 1, 3).reshape(B, S, H)
    return o, lse

def dilated_attention(q, k, v):
    outs, lses = [], []
    for window, dilation in DILATED_PATTERNS:
        o, lse = dilated_branch(q, k, v, window, dilation)
        outs.append(o)
        lses.append(lse)
    w = jax.nn.softmax(jnp.stack(lses, axis=0), axis=0)
    return jnp.einsum('pbsh,pbshd->bshd', w.astype(v.dtype), jnp.stack(outs, axis=0))

def mlstm_chunkwise(q, k, v, log_i, log_f):
    B, NH, S, D = q.shape
    L = MLSTM_CHUNK
    NC = S // L
    k = k * (D ** -0.5)

    def to_chunks(t):
        return jnp.moveaxis(t.reshape(B, NH, NC, L, *t.shape[3:]), 2, 0)

    xs = (to_chunks(q), to_chunks(k), to_chunks(v), to_chunks(log_i), to_chunks(log_f))
    causal = jnp.tril(jnp.ones((L, L), dtype=bool))

    def step(carry, inp):
        C, n, m = carry
        qc, kc, vc, ic, fc = inp
        b = jnp.cumsum(fc, axis=-1)
        log_d = b[..., :, None] - b[..., None, :] + ic[..., None, :]
        log_d = jnp.where(causal, log_d, -jnp.inf)
        m_inter = b + m[..., None]
        m_t = jnp.maximum(m_inter, jnp.max(log_d, axis=-1))
        d_mat = jnp.exp(log_d - m_t[..., None])
        inter = jnp.exp(m_inter - m_t)
        s_qk = jnp.einsum('bhtd,bhsd->bhts', qc, kc) * d_mat
        num = inter[..., None] * jnp.einsum('bhtd,bhde->bhte', qc, C) + jnp.einsum('bhts,bhse->bhte', s_qk, vc)
        nq = inter * jnp.einsum('bhtd,bhd->bht', qc, n) + jnp.sum(s_qk, axis=-1)
        h = num / jnp.maximum(jnp.abs(nq), jnp.exp(-m_t))[..., None]
        b_last = b[..., -1]
        w_log = b_last[..., None] - b + ic
        m_new = jnp.maximum(b_last + m, jnp.max(w_log, axis=-1))
        w = jnp.exp(w_log - m_new[..., None])
        decay = jnp.exp(b_last + m - m_new)
        C_new = decay[..., None, None] * C + jnp.einsum('bhs,bhsd,bhse->bhde', w, kc, vc)
        n_new = decay[..., None] * n + jnp.einsum('bhs,bhsd->bhd', w, kc)
        return (C_new, n_new, m_new), h

    init = (jnp.zeros((B, NH, D, D), jnp.float32),
            jnp.zeros((B, NH, D), jnp.float32),
            jnp.zeros((B, NH), jnp.float32))
    _, h = lax.scan(step, init, xs)
    return jnp.moveaxis(h, 0, 2).reshape(B, NH, S, D)

def token_mixer(h, w_in, w_conv, b_conv, b_igate, b_fgate, q_norm_g, k_norm_g, mlstm_norm_g, w_out):
    B, S, _ = h.shape
    xin = h @ w_in
    cuts = list(np.cumsum(IN_SPLITS)[:-1])
    qa, ka, va, qm, km, vm, og, ig, fg = jnp.split(xin, cuts, axis=-1)
    qa = rms_norm(qa.reshape(B, S, N_ATTN_HEADS, ATTN_HEAD_DIM), q_norm_g) * ATTN_SCALE
    ka = rms_norm(ka.reshape(B, S, N_ATTN_HEADS, ATTN_HEAD_DIM), k_norm_g)
    va = va.reshape(B, S, N_ATTN_HEADS, ATTN_HEAD_DIM)
    attn = dilated_attention(qa, ka, va).reshape(B, S, ATTN_WIDTH_2)
    qkm = jax.nn.silu(causal_short_conv(jnp.concatenate([qm, km], axis=-1), w_conv, b_conv))
    qm, km = jnp.split(qkm, 2, axis=-1)

    def heads(t):
        return t.reshape(B, S, N_MLSTM_HEADS, MLSTM_HEAD_DIM).transpose(0, 2, 1, 3).astype(jnp.float32)

    log_i = (ig + b_igate).astype(jnp.float32).transpose(0, 2, 1)
    log_f = jax.nn.log_sigmoid((fg + b_fgate).astype(jnp.float32)).transpose(0, 2, 1)
    hm = mlstm_chunkwise(heads(qm), heads(km), heads(vm), log_i, log_f)
    hm = hm.transpose(0, 2, 1, 3).astype(h.dtype)
    hm = rms_norm(hm, mlstm_norm_g.reshape(N_MLSTM_HEADS, MLSTM_HEAD_DIM)).reshape(B, S, MLSTM_WIDTH)
    hm = jax.nn.sigmoid(og) * hm
    return jnp.concatenate([attn, hm], axis=-1) @ w_out

def swiglu(h, w_gate, w_up, w_down):
    return (jax.nn.silu(h @ w_gate) * (h @ w_up)) @ w_down

def second_inputs(seed: int = 0) -> dict:
    key = jax.random.key(seed)
    ks = jax.random.split(key, 20)
    f32 = jnp.float32
    D = D_MODEL

    def nrm(k, shape, scale):
        return jax.random.normal(k, shape, f32) * scale

    b_ada = nrm(ks[15], (DEPTH_2, N_MOD * D), 0.02)
    gate_cols = jnp.zeros((N_MOD, D), f32).at[2].set(1.0).at[5].set(1.0).reshape(-1)
    b_ada = b_ada + gate_cols
    f_bias = jnp.linspace(3.0, 6.0, N_MLSTM_HEADS, dtype=f32)[None, :]
    return {
        "x": nrm(ks[0], (BATCH, SEQ, D), 1.0),
        "c": nrm(ks[1], (BATCH, D), 1.0),
        "g_mix": 1.0 + nrm(ks[2], (DEPTH_2, D), 0.02),
        "w_in": nrm(ks[3], (DEPTH_2, D, IN_COLS_2), D ** -0.5),
        "w_conv": nrm(ks[4], (DEPTH_2, CONV_WIDTH_2, 2 * MLSTM_WIDTH), CONV_WIDTH_2 ** -0.5),
        "b_conv": nrm(ks[5], (DEPTH_2, 2 * MLSTM_WIDTH), 0.02),
        "b_igate": nrm(ks[6], (DEPTH_2, N_MLSTM_HEADS), 0.1),
        "b_fgate": f_bias + nrm(ks[7], (DEPTH_2, N_MLSTM_HEADS), 0.1),
        "q_norm_g": 1.0 + nrm(ks[8], (DEPTH_2, ATTN_HEAD_DIM), 0.02),
        "k_norm_g": 1.0 + nrm(ks[9], (DEPTH_2, ATTN_HEAD_DIM), 0.02),
        "mlstm_norm_g": 1.0 + nrm(ks[10], (DEPTH_2, MLSTM_WIDTH), 0.02),
        "w_out": nrm(ks[11], (DEPTH_2, D, D), D ** -0.5),
        "g_ffn": 1.0 + nrm(ks[12], (DEPTH_2, D), 0.02),
        "w_gate": nrm(ks[13], (DEPTH_2, D, D_FF), D ** -0.5),
        "w_up": nrm(ks[14], (DEPTH_2, D, D_FF), D ** -0.5),
        "w_down": nrm(ks[16], (DEPTH_2, D_FF, D), D_FF ** -0.5),
        "w_ada": nrm(ks[17], (DEPTH_2, D, N_MOD * D), 0.1 * D ** -0.5),
        "b_ada": b_ada,
    }

def second_block(x, c, g_mix, w_in, w_conv, b_conv, b_igate, b_fgate, q_norm_g, k_norm_g,
              mlstm_norm_g, w_out, g_ffn, w_gate, w_up, w_down, w_ada, b_ada):
    for l in range(DEPTH_2):
        mod = jax.nn.silu(c) @ w_ada[l] + b_ada[l]
        sh_m, sc_m, gt_m, sh_f, sc_f, gt_f = jnp.split(mod, N_MOD, axis=-1)
        h = modulate(rms_norm(x, g_mix[l]), sh_m, sc_m)
        y = token_mixer(h, w_in[l], w_conv[l], b_conv[l], b_igate[l], b_fgate[l],
                        q_norm_g[l], k_norm_g[l], mlstm_norm_g[l], w_out[l])
        x = x + gt_m[:, None, :] * y
        h = modulate(rms_norm(x, g_ffn[l]), sh_f, sc_f)
        x = x + gt_f[:, None, :] * swiglu(h, w_gate[l], w_up[l], w_down[l])
    return x


def setup_inputs(seed=0):
    out = dict(first_inputs(seed))
    for name, value in second_inputs(seed + 1).items():
        if name != "x":
            out[name + "_2"] = value
    return out


def reference(
    x, norm_mix, w_in, conv_w, w_attn_out, w_conv_out, w_mix_out, norm_mlp, w_mlp_up,
    w_mlp_down, norm_final, c_2, g_mix_2, w_in_2, w_conv_2, b_conv_2, b_igate_2, b_fgate_2,
    q_norm_g_2, k_norm_g_2, mlstm_norm_g_2, w_out_2, g_ffn_2, w_gate_2, w_up_2, w_down_2,
    w_ada_2, b_ada_2,
):
    x = first_block(
        x, norm_mix, w_in, conv_w, w_attn_out, w_conv_out, w_mix_out, norm_mlp, w_mlp_up,
        w_mlp_down, norm_final,
    )
    return second_block(
        x, c_2, g_mix_2, w_in_2, w_conv_2, b_conv_2, b_igate_2, b_fgate_2, q_norm_g_2,
        k_norm_g_2, mlstm_norm_g_2, w_out_2, g_ffn_2, w_gate_2, w_up_2, w_down_2, w_ada_2,
        b_ada_2,
    )


_drawn_inputs = setup_inputs


def setup_inputs(seed=0):
    import zlib

    import numpy as np

    out = dict(_drawn_inputs(seed))
    spreads = {}
    factors = {'g_mix_2': 5.21,
     'b_conv_2': 64.0,
     'b_igate_2': 64.0,
     'q_norm_g_2': 8.0,
     'k_norm_g_2': 8.0,
     'mlstm_norm_g_2': 22.047,
     'g_ffn_2': 11.193}
    for name, (base, spread) in spreads.items():
        noise = np.random.default_rng([zlib.crc32(name.encode()), seed]).standard_normal(out[name].shape)
        drawn = base * np.exp(spread * noise) if base else spread * noise
        out[name] = __import__('jax').numpy.asarray(drawn.astype(out[name].dtype))
    for name, factor in factors.items():
        out[name] = (out[name] * factor).astype(out[name].dtype)
    return out
```

```python
import numpy as np
from contextlib import ExitStack

import concourse.bass as bass
from concourse import mybir

F32 = mybir.dt.float32
F32R = mybir.dt.float32r
ALU = mybir.AluOpType
ACT = mybir.ActivationFunctionType
AX_X = mybir.AxisListType.X

P = 128
S = 512
D = 1024
KT = D // P
LAYERS = 2
HEADS, HD = 8, 64
IDX_HEADS = 4
TOPK = min(256, S // 4)
ATT = HEADS * HD
AT = ATT // P
TT = S // P
MH = 4
CHUNKS = 4
D_FF = 2816
FF_TILES = [8, 8, 6]
EPS = 1e-6
NEG = -1.0e30
OUTSIDE = -2.0e38
TAKEN = -3.0e38

BLK = 2048
B_IQ, B_IK, B_Q, B_K, B_V, B_CONV, B_YCONV, B_G1, B_G0, B_YATT, B_MIX, B_MLP = 0, 1, 2, 4, 6, 8, 14, 16, 20, 24, 26, 30
LAYER_BLOCKS = B_MLP + 8 * CHUNKS
C_QA, C_KA, C_VA, C_QM, C_KM, C_VM, C_OG, C_IF, C_OUT, C_FF = 0, 2, 4, 6, 8, 10, 12, 14, 15, 19
SECOND_BLOCKS = C_FF + sum(n + 4 for n in FF_TILES)
BLOCKS = LAYERS * LAYER_BLOCKS + SECOND_BLOCKS


def first_tile(j):
    return 2 * j + 2 * min(max(j - B_YCONV, 0), 2) + 2 * min(max(j - B_YATT, 0), 2)


LAYER_TILES = first_tile(LAYER_BLOCKS)
TRI = [0, 128, 384, 768, 1280]
TRT = [0, 512, 896, 1152, 1280]

ROPE_SLOT = [0, 1, 2, 4, 5, 6, 7, 8, 9, 10, 11]
LOGIT_SLOT = 5
TOPK_SLOT, TOPK_STEPS = 9, 4
HEAD_SLOT = 21
Y_SLOT = [33, 34, 40, 46]

K_ROT, K_ID, K_ONES, K_HALF, K_N = 0, 128, 256, 384, 512
LP_GMLP, LP_CONV, LP_GNEXT, LP_N = 0, 8, 20, 28
SP_GMIX, SP_GFFN, SP_GFIN, SP_BCONV, SP_WCONV, SP_QG, SP_KG, SP_MG, SP_BADA, SP_C, SP_BI, SP_BF, SP_G0, SP_N = (
    0, 8, 16, 24, 32, 64, 65, 66, 70, 118, 126, 127, 128, 136)


def nth(layer, per_layer, k, step=1):
    return layer * (per_layer * step) + k * step + step


def two_blocks(nc, weights, ada, consts, rope, tri_bias, mult_bias, tri_mask, layer_params, params, x_in, selectors, out):
    with ExitStack() as ctx:
        def sb(name, shape, dt=F32, scope=ctx):
            return scope.enter_context(nc.sbuf_tensor(name, shape, dt))

        x = sb("x", [P, KT, S])
        a_hi = sb("a_hi", [P, KT, S], F32R)
        a_lo = sb("a_lo", [P, KT, S], F32R)
        w_raw = sb("w_raw", [P, 2, BLK])
        w_hi = sb("w_hi", [P, 2, BLK], F32R)
        w_lo = sb("w_lo", [P, 2, BLK], F32R)
        v = sb("v", [P, TT, ATT])
        y_hi = sb("y_hi", [P, AT, S], F32R)
        y_lo = sb("y_lo", [P, AT, S], F32R)
        yc = sb("yc", [P, KT, S])
        g = sb("g", [P, KT, S])
        bias = sb("bias", [P, TRI[TT]])
        cs_rope = sb("cs_rope", [P, 2, S])
        cs_tok = sb("cs_tok", [P, 2, S])
        kc = sb("kc", [P, K_N])
        rms = sb("rms", [P, S])
        rms_col = sb("rms_col", [P, 3 * TT])
        lp = sb("lp", [P, LP_N])
        sp = sb("sp", [P, SP_N])
        mod = sb("mod", [P, 48])
        gs = sb("gs", [P, 2 * KT])
        cs = sb("cs", [P, KT])
        iw = sb("iw", [P, TT, IDX_HEADS])
        top = sb("top", [P, 8])
        peak = sb("peak", [P, 4 * TT])
        nudge = sb("nudge", [P, 1])
        acol = sb("acol", [P, TT, MH])
        one = ExitStack()
        q = sb("q", [P, AT, S], F32, one)
        k = sb("k", [P, AT, S], F32, one)
        iq = sb("iq", [P, 2, S], F32, one)
        ik = sb("ik", [P, 1, S], F32, one)
        pr = sb("pr", [P, TRI[TT]], F32, one)
        pt = sb("pt", [P, TRT[TT]], F32, one)
        one.close()
        two = ExitStack()
        b_hi = sb("b_hi", [P, KT, S], F32R, two)
        b_lo = sb("b_lo", [P, KT, S], F32R, two)
        two.close()
        one.enter_context(nc.sbuf_tensor("region_1", [P, 2 * KT * S], F32))
        ctx.enter_context(one)

        ps = [ctx.enter_context(nc.psum_tensor(f"ps{b}", [P, S], F32)) for b in range(8)]

        def sem(name):
            return ctx.enter_context(nc.semaphore(name))

        setup_loaded = sem("setup_loaded")
        w_loaded = [sem(f"w_loaded{s}") for s in range(2)]
        w_hi_ready = sem("w_hi_ready")
        w_lo_ready = sem("w_lo_ready")
        tile_done = sem("tile_done")
        bank_free = [sem(f"bank_free{b}") for b in range(4)]
        lp_loaded = sem("lp_loaded")
        x_ready = sem("x_ready")
        x_hi = sem("x_hi")
        x_sq = sem("x_sq")
        x_split = sem("x_split")
        sq_used = sem("sq_used")
        sq_summed = sem("sq_summed")
        ss_done = sem("ss_done")
        ms_ready = sem("ms_ready")
        root_ready = sem("root_ready")
        rms_ready = sem("rms_ready")
        raw_ready = sem("raw_ready")
        rot_done = sem("rot_done")
        roped = sem("roped")
        logits_done = sem("logits_done")
        logits_used = sem("logits_used")
        v_ready = sem("v_ready")
        cy_ready = sem("cy_ready")
        cy_hi = sem("cy_hi")
        cy_split = sem("cy_split")
        gate_ready = sem("gate_ready")
        gate_exp = sem("gate_exp")
        yc_ready = sem("yc_ready")
        scores_done = sem("scores_done")
        masked = sem("masked")
        exps_done = sem("exps_done")
        probs_ready = sem("probs_ready")
        probs_turned = sem("probs_turned")
        pt_ready = sem("pt_ready")
        head_done = sem("head_done")
        head_copied = sem("head_copied")
        y_hi_ready = sem("y_hi_ready")
        y_split = sem("y_split")
        merged_ready = sem("merged_ready")
        merged_hi = sem("merged_hi")
        merged_split = sem("merged_split")
        h_ready = sem("h_ready")
        h_hi = sem("h_hi")
        h_split = sem("h_split")
        ada_loaded = sem("ada_loaded")
        ada_used = sem("ada_used")
        ada_summed = sem("ada_summed")
        ada_done = sem("ada_done")
        ada_taken = sem("ada_taken")
        c_silu = sem("c_silu")
        second_loaded = sem("second_loaded")
        xm_ready = sem("xm_ready")
        xm_hi = sem("xm_hi")
        xm_split = sem("xm_split")
        qn_sq = sem("qn_sq")
        qn_ss = sem("qn_ss")
        qn_ms = sem("qn_ms")
        qn_root = sem("qn_root")
        qk_normed = sem("qk_normed")
        v2_ready = sem("v2_ready")
        mc_ready = sem("mc_ready")
        mc_silu = sem("mc_silu")
        mv_ready = sem("mv_ready")
        og_ready = sem("og_ready")
        f_ready = sem("f_ready")
        f_log = sem("f_log")
        m_rows = sem("m_rows")
        m_exp = sem("m_exp")
        a_turned = sem("a_turned")
        a_cols = sem("a_cols")
        m_bc = sem("m_bc")
        m_scores = sem("m_scores")
        m_gap = sem("m_gap")
        m_decay = sem("m_decay")
        m_probs = sem("m_probs")
        m_num = sem("m_num")
        m_h = sem("m_h")
        m_sq = sem("m_sq")
        m_ss = sem("m_ss")
        m_ms = sem("m_ms")
        m_root = sem("m_root")
        m_out = sem("m_out")
        m_hi = sem("m_hi")
        m_split = sem("m_split")
        silu_done = sem("silu_done")
        x_final = sem("x_final")
        stored = sem("stored")

        block = ctx.enter_context(nc.Block())

        def wcols(t, slot, deep, kt, c0, n):
            return t[:, slot, :].rearrange("p (k c) -> p k c", k=deep)[:, kt, c0:c0 + n]

        rot_m, ident, ones, half = (kc[:, c:c + P] for c in (K_ROT, K_ID, K_ONES, K_HALF))
        acc = yc[:, KT - 1, :]
        nms, nroot, ntmp = g[:, 2, :], g[:, 3, :], g[:, 6, :]
        ada_w = v
        ada_p = yc[:, 0:4, :].rearrange("p a b -> p (a b)")
        ada_s = yc[:, 4, 0:256]
        mq, mk, mv = yc[:, 4:8, :], g[:, 0:4, :], yc[:, 0:4, :]
        og = [iq[:, 0, :], iq[:, 1, :], ik[:, 0, :], cs_rope[:, 0, :]]
        tri = cs_rope[:, 1, 0:P]
        sel = cs_tok[0:MH, 0, :]
        row_a, row_b, row_e, row_g = g[0:MH, 6, :], g[0:MH, 7, :], cs_tok[0:MH, 1, :], rms[0:MH, :]
        key_bank = (ps[4][:, :], ps[5][:, 0:384], ps[6][:, 0:256], ps[5][:, 384:512])
        query_bank = (ps[5][:, 384:512], ps[6][:, 0:256], ps[5][:, 0:384], ps[4][:, :])

        def f32(ap):
            return ap.bitcast(F32)

        @block.sync
        def _(sync):
            for s in range(2):
                sync.dma_start(w_raw[:, s, :], weights[s]).then_inc(w_loaded[s], 16)
            with sync.Fori(1, BLOCKS // 2) as pair:
                for s in range(2):
                    sync.wait_ge(w_lo_ready, pair * 2 + (s - 1))
                    sync.dma_start(w_raw[:, s, :], weights[bass.ds(pair * 2 + s, 1)].rearrange("a p n -> p (a n)")
                                   ).then_inc(w_loaded[s], 16)
            sync.wait_ge(w_lo_ready, BLOCKS - 2)
            sync.dma_start(w_raw[:, 0, :], weights[BLOCKS - 1]).then_inc(w_loaded[0], 16)
            for n in range(KT):
                sync.wait_ge(x_final, n + 1)
                sync.dma_start(out[n * P:(n + 1) * P, :], x[:, n, :]).then_inc(stored, 16)
            sync.wait_ge(stored, 16 * KT)

        @block.gpsimd
        def _(pool):
            def split(n, s):
                pool.wait_ge(w_hi_ready, n + 1)
                nc.gpsimd.tensor_tensor(w_lo[:, s, :], w_raw[:, s, :], f32(w_hi[:, s, :]), ALU.subtract
                                        ).then_inc(w_lo_ready, 1)

            with pool.Fori(0, BLOCKS // 2) as pair:
                for s in range(2):
                    split(pair * 2 + s, s)
            split(BLOCKS - 1, (BLOCKS - 1) % 2)

        @block.tensor
        def _(pe):
            def product(o, s, deep, depth, c0, m, hi, lo, ready=None):
                for kt in range(depth):
                    if ready is not None:
                        ready(kt)
                    wh, wl = wcols(w_hi, s, deep, kt, c0, m), wcols(w_lo, s, deep, kt, c0, m)
                    nc.tensor.matmul(o, wh, hi(kt), start=kt == 0, stop=False)
                    nc.tensor.matmul(o, wh, lo(kt), start=False, stop=False)
                    last = nc.tensor.matmul(o, wl, hi(kt), start=False, stop=kt == depth - 1)
                last.then_inc(tile_done, 1)

            def tile(L, t, s, deep, c0, hi, lo, m=P, depth=None, ready=None):
                pe.wait_ge(bank_free[t % 4], nth(L, LAYER_TILES // 4, t // 4))
                product(ps[t % 4][0:m, :], s, deep, depth or deep, c0, m,
                        lambda kt: hi[:, kt, :], lambda kt: lo[:, kt, :], ready)

            def token_tile(L, t, s, parts, c0, n):
                pe.wait_ge(bank_free[t % 4], nth(L, LAYER_TILES // 4, t // 4))
                for tt, col in parts:
                    o = ps[t % 4][:, col:col + n]
                    for kt in range(KT):
                        ah, al = (m[:, kt, tt * P:(tt + 1) * P] for m in (a_hi, a_lo))
                        wh, wl = wcols(w_hi, s, KT, kt, c0, n), wcols(w_lo, s, KT, kt, c0, n)
                        nc.tensor.matmul(o, ah, wh, start=kt == 0, stop=False)
                        nc.tensor.matmul(o, ah, wl, start=False, stop=False)
                        last = nc.tensor.matmul(o, al, wh, start=False, stop=kt == KT - 1)
                last.then_inc(tile_done, 1)

            def sum_squares(L, which, cols=False):
                pe.wait_ge(sq_summed, nth(L, 2, which))
                last = nc.tensor.matmul(ps[7][:, :], ones, acc, start=True, stop=True)
                if cols:
                    for tt in range(TT):
                        last = nc.tensor.matmul(ps[6][:, tt:tt + 1], acc[:, tt * P:(tt + 1) * P], ones[:, 0:1],
                                                start=True, stop=True)
                last.then_inc(ss_done, 1)

            def scores(L, h):
                rows = slice(HD * (h % 2), HD * (h % 2) + HD)
                for i in range(TT):
                    last = nc.tensor.matmul(query_bank[i], q[rows, h // 2, i * P:(i + 1) * P],
                                            k[rows, h // 2, 0:(i + 1) * P], start=True, stop=True)
                last.then_inc(scores_done, 1)

            def transposes(L, h):
                pe.wait_ge(probs_ready, nth(L, HEADS, h))
                for j in range(TT):
                    for i in range(j, TT):
                        last = nc.tensor.transpose(key_bank[j][:, (i - j) * P:(i - j + 1) * P],
                                                   pr[:, TRI[i] + j * P:TRI[i] + (j + 1) * P], ident)
                last.then_inc(probs_turned, 1)

            def values(L, h):
                pe.wait_ge(pt_ready, nth(L, HEADS, h))
                if h > 0:
                    pe.wait_ge(head_copied, nth(L, HEADS, h - 1))
                rows = slice(HD * (h % 2), HD * (h % 2) + HD)
                for j in range(TT):
                    last = nc.tensor.matmul(ps[7][rows, j * P:], v[:, j, h * HD:(h + 1) * HD],
                                            pt[:, TRT[j]:TRT[j + 1]], start=j == 0, stop=j == TT - 1)
                last.then_inc(head_done, 1)

            def beside(L, s):
                if s == 0:
                    sum_squares(L, 0, True)
                for r, rs in enumerate(ROPE_SLOT):
                    if s == rs + 1:
                        pe.wait_ge(raw_ready, nth(L, 11, r))
                        if r > 0:
                            pe.wait_ge(roped, nth(L, 11, r - 1))
                        else:
                            pe.wait_ge(ms_ready, nth(L, 2, 0))
                        nc.tensor.matmul(ps[7][:, :], rot_m, g[:, 4 + r % 2, :], start=True, stop=True
                                         ).then_inc(rot_done, 1)
                if LOGIT_SLOT <= s < LOGIT_SLOT + IDX_HEADS:
                    h = s - LOGIT_SLOT
                    if h == 0:
                        pe.wait_ge(roped, nth(L, 11, 2))
                        pe.wait_ge(rms_ready, nth(L, 2, 0))
                    else:
                        pe.wait_ge(logits_used, nth(L, IDX_HEADS, h - 1))
                    rows = slice(64 * (h % 2), 64 * (h % 2) + 64)
                    for i in range(1, TT):
                        last = nc.tensor.matmul(query_bank[i], iq[rows, h // 2, i * P:(i + 1) * P],
                                                ik[rows, 0, 0:(i + 1) * P], start=True, stop=True)
                    last.then_inc(logits_done, 1)
                h, part = divmod(s - HEAD_SLOT, 3)
                if part == 2 and 0 <= h < HEADS:
                    transposes(L, h)
                if part == 0 and 1 <= h <= HEADS:
                    if h == 1:
                        pe.wait_ge(v_ready, nth(L, 1, 0))
                    values(L, h - 1)
                if part == 0 and 0 <= h < HEADS:
                    if h == 0:
                        pe.wait_ge(roped, nth(L, 11, 10))
                        pe.wait_ge(logits_used, nth(L, IDX_HEADS, IDX_HEADS - 1))
                    scores(L, h)

            with pe.Fori(0, LAYERS) as L:
                for j in range(B_MLP):
                    s, t = j % 2, first_tile(j)
                    pe.wait_ge(w_lo_ready, nth(L, LAYER_BLOCKS, j))
                    if j == B_IK:
                        tile(L, t, s, KT, 0, a_hi, a_lo)
                        beside(L, t)
                        token_tile(L, t + 1, s, [(tt, IDX_HEADS * tt) for tt in range(TT)], P, IDX_HEADS)
                        beside(L, t + 1)
                    elif B_V <= j < B_CONV:
                        for u in range(2):
                            token_tile(L, t + u, s, [(2 * u, 0), (2 * u + 1, 256)], 0, 256)
                            beside(L, t + u)
                    elif B_YCONV <= j < B_G1 or B_YATT <= j < B_MIX:
                        if j == B_YCONV:
                            pe.wait_ge(cy_split, nth(L, AT, AT - 1))
                        if j == B_YATT:
                            pe.wait_ge(y_split, nth(L, AT, AT - 1))
                        for u in range(4):
                            tile(L, t + u, s, AT, u * P, y_hi, y_lo)
                            if u % 2 and j < B_G1:
                                beside(L, 2 * j + u // 2)
                    else:
                        src = (b_hi, b_lo) if j >= B_MIX else (a_hi, a_lo)
                        for u in range(2):
                            ready = None
                            if j == B_IQ and u == 0:
                                def ready(kt):
                                    pe.wait_ge(x_split, nth(L, 2 * KT, kt))
                            if j == B_MIX and u == 0:
                                def ready(kt):
                                    pe.wait_ge(merged_split, nth(L, KT, kt))
                            tile(L, t + u, s, KT, u * P, *src, ready=ready)
                            if j < B_YATT:
                                beside(L, 2 * j + u)
                sum_squares(L, 1)
                with pe.Fori(0, CHUNKS) as c:
                    for b in range(8):
                        pe.wait_ge(w_lo_ready, nth(L, LAYER_BLOCKS, c * 8 + (B_MLP + b)))
                        for u in range(2):
                            n = 2 * b + u
                            pe.wait_ge(bank_free[n % 4], nth(L, LAYER_TILES // 4, c * 4 + (first_tile(B_MLP) + n) // 4))
                            src = (a_hi, a_lo) if b < 4 else (b_hi, b_lo)
                            ready = None
                            if n == 0:
                                def ready(kt):
                                    pe.wait_ge(x_split, nth(L, 2 * KT, KT + kt))
                            if n == 8:
                                def ready(kt):
                                    pe.wait_ge(h_split, nth(L, 8 * CHUNKS, c * 8 + kt))
                            product(ps[n % 4][:, :], b % 2, KT, KT, u * P, P,
                                    lambda kt: src[0][:, kt, :], lambda kt: src[1][:, kt, :], ready)
                            if n in (10, 12, 14):
                                p = (n - 10) // 2
                                pe.wait_ge(ada_summed, nth(L, 12, c * 3 + p))
                                pe.wait_ge(ada_taken, nth(L, 12, c * 3 + p))
                                for e in range(2):
                                    last = nc.tensor.matmul(ps[7][:, e:e + 1], ada_s[:, e * P:(e + 1) * P],
                                                            ones[:, 0:1], start=True, stop=True)
                                last.then_inc(ada_done, 1)

            L = LAYERS
            sum_squares(L, 0)
            sum_squares(L, 1)

            def qk_sums(r):
                pe.wait_ge(qn_sq, r + 1)
                if r > 0:
                    pe.wait_ge(qn_ms, r - 1 + 1)
                nc.tensor.matmul(ps[7][:, :], half, g[:, r % 2, :], start=True, stop=True).then_inc(qn_ss, 1)

            for j in range(C_OUT):
                s, t = j % 2, 2 * j
                pe.wait_ge(w_lo_ready, nth(L, LAYER_BLOCKS, j))
                for u in range(2):
                    if C_VA <= j < C_QM or C_VM <= j < C_OG:
                        token_tile(L, t + u, s, [(2 * u, 0), (2 * u + 1, 256)], 0, 256)
                    elif j == C_IF:
                        tile(L, t + u, s, KT, u * MH, a_hi, a_lo, m=MH)
                    else:
                        ready = None
                        if t + u == 0:
                            def ready(kt):
                                pe.wait_ge(xm_split, kt + 1)
                        tile(L, t + u, s, KT, u * P, a_hi, a_lo, ready=ready)
                    if 1 <= t + u <= 8:
                        qk_sums(t + u - 1)
                h = j - C_QM
                if h == 0:
                    pe.wait_ge(qk_normed, 8)
                    pe.wait_ge(v2_ready, 1)
                if 1 <= h <= HEADS:
                    transposes(L, h - 1)
                    values(L, h - 1)
                if 0 <= h < HEADS:
                    scores(L, h)

            pe.wait_ge(m_rows, 1)
            for tt in range(TT):
                last = nc.tensor.transpose(ps[4][:, MH * tt:MH * tt + MH], row_a[:, tt * P:(tt + 1) * P],
                                           ident[0:MH, 0:MH])
            last.then_inc(a_turned, 1)
            for h in range(MH):
                if h == 0:
                    pe.wait_ge(a_cols, 1)
                    pe.wait_ge(mc_silu, 2 * MH - 1 + 1)
                    pe.wait_ge(mv_ready, 1)
                    pe.wait_ge(m_exp, 1)
                    pe.wait_ge(head_copied, nth(L, HEADS, HEADS - 1))
                    for b in range(4):
                        pe.wait_ge(bank_free[b], nth(L, LAYER_TILES // 4, 2 * C_OUT // 4 + (b < 2 * C_OUT % 4)))
                else:
                    pe.wait_ge(m_split, h - 1 + 1)
                one_head = sel[:, h * P:(h + 1) * P]
                nc.tensor.matmul(ps[7][:, :], one_head, row_g, start=True, stop=True)
                nc.tensor.matmul(ps[3][:, :], one_head, row_e, start=True, stop=True).then_inc(m_bc, 1)
                for i in range(TT):
                    last = nc.tensor.matmul(key_bank[i], mk[:, h, i * P:(i + 1) * P], mq[:, h, i * P:],
                                            start=True, stop=True)
                last.then_inc(m_scores, 1)
                pe.wait_ge(m_probs, h + 1)
                for i in range(TT):
                    nc.tensor.matmul(ps[0][:, i * P:], mv[:, i, h * P:(h + 1) * P], pt[:, TRT[i]:TRT[i + 1]],
                                     start=i == 0, stop=i == TT - 1)
                for i in range(TT):
                    last = nc.tensor.matmul(ps[1][:, i * P:], ones, pt[:, TRT[i]:TRT[i + 1]],
                                            start=i == 0, stop=i == TT - 1)
                last.then_inc(m_num, 1)
                pe.wait_ge(m_sq, h + 1)
                nc.tensor.matmul(ps[2][:, :], ones, pr[:, 0:S], start=True, stop=True).then_inc(m_ss, 1)

            pe.wait_ge(m_split, MH - 1 + 1)
            pe.wait_ge(y_split, nth(L, AT, AT - 1))
            for j in range(C_OUT, C_FF):
                pe.wait_ge(w_lo_ready, nth(L, LAYER_BLOCKS, j))
                for u in range(2):
                    t = 2 * j + u
                    pe.wait_ge(bank_free[t % 4], nth(L, LAYER_TILES // 4, t // 4))
                    product(ps[t % 4][:, :], j % 2, KT, KT, u * P, P,
                            lambda kt: y_hi[:, kt, :] if kt < AT else a_hi[:, kt - AT, :],
                            lambda kt: y_lo[:, kt, :] if kt < AT else a_lo[:, kt - AT, :])
            sum_squares(L, 2)
            j, hid = C_FF, 0
            for nt in FF_TILES:
                for b in range(nt):
                    pe.wait_ge(w_lo_ready, nth(L, LAYER_BLOCKS, j))
                    for u in range(2):
                        ready = None
                        if j == C_FF and u == 0:
                            def ready(kt):
                                pe.wait_ge(xm_split, KT + kt + 1)
                        tile(L, 2 * j + u, j % 2, KT, u * P, a_hi, a_lo, ready=ready)
                    j += 1
                for b in range(4):
                    pe.wait_ge(w_lo_ready, nth(L, LAYER_BLOCKS, j))
                    for u in range(2):
                        ready = None
                        if b + u == 0:
                            def ready(kt):
                                pe.wait_ge(h_split, nth(L, 8 * CHUNKS, hid + kt))
                        tile(L, 2 * j + u, j % 2, KT, u * P, b_hi, b_lo, depth=nt, ready=ready)
                    j += 1
                hid += nt

        @block.scalar
        def _(act):
            def w_split(L, n, at=0):
                act.wait_ge(w_loaded[n % 2], nth(L, LAYER_BLOCKS // 2, at * 4 + n // 2, 16))
                nc.scalar.activation(w_hi[:, n % 2, :], w_raw[:, n % 2, :], ACT.Copy).then_inc(w_hi_ready, 1)

            def x_parts(n, gain):
                nc.scalar.activation(a_hi[:, n, :], x[:, n, :], ACT.Copy, scale=gain).then_inc(x_hi, 1)
                nc.scalar.activation(g[:, n % 2, :], x[:, n, :], ACT.Square).then_inc(x_sq, 1)

            def root(L, which, cols=False):
                act.wait_ge(ms_ready, nth(L, 2, which))
                if cols:
                    nc.scalar.activation(rms_col[:, 8:12], rms_col[:, 4:8], ACT.Sqrt)
                nc.scalar.activation(nroot, nms, ACT.Sqrt).then_inc(root_ready, 1)

            def exps(L, h):
                act.wait_ge(masked, nth(L, HEADS, h))
                for i in range(TT):
                    nc.scalar.activation(pr[:, TRI[i]:TRI[i + 1]], pr[:, TRI[i]:TRI[i + 1]], ACT.Exp,
                                         bias=peak[:, 4 + i:5 + i], accum_out=peak[:, 8 + i:9 + i])
                act.drain().then_inc(exps_done, 1)

            def turned(L, h):
                act.wait_ge(probs_turned, nth(L, HEADS, h))
                nc.scalar.activation(pt[:, TRT[0]:TRT[1]], ps[4][:, :], ACT.Copy)
                nc.scalar.activation(pt[:, TRT[1]:TRT[2]], ps[5][:, 0:384], ACT.Copy)
                nc.scalar.activation(pt[:, TRT[3]:TRT[4]], ps[5][:, 384:512], ACT.Copy)
                nc.scalar.activation(pt[:, TRT[2]:TRT[3]], ps[6][:, 0:256], ACT.Copy)
                act.drain().then_inc(pt_ready, 1)

            def head_out(L, h):
                act.wait_ge(head_done, nth(L, HEADS, h))
                rows = slice(HD * (h % 2), HD * (h % 2) + HD)
                nc.scalar.activation(q[rows, h // 2, :], ps[7][rows, :], ACT.Copy).then_inc(head_copied, 1)

            def y_high(L, i):
                act.wait_ge(head_copied, nth(L, HEADS, 2 * i + 1))
                nc.scalar.activation(y_hi[:, i, :], q[:, i, :], ACT.Copy).then_inc(y_hi_ready, 1)

            setup = [(kc[:, :], consts), (cs_rope[:, :, :], rope), (bias[:, 0:P], tri_bias), (sp[:, :], params),
                     (x[:, :, :], x_in.rearrange("(n p) t -> p n t", p=P))]
            for dst, src in setup:
                act.dma_start(dst, src).then_inc(setup_loaded, 16)
            act.wait_ge(setup_loaded, 16 * len(setup))
            nc.scalar.activation(cs[:, :], sp[:, SP_C:SP_C + KT], ACT.Silu).then_inc(c_silu, 1)
            for n in range(KT):
                if n >= 2:
                    act.wait_ge(sq_used, n - 2 + 1)
                x_parts(n, sp[:, SP_G0 + n:SP_G0 + n + 1])
            for n in range(2):
                w_split(0, n)

            def beside(L, s, t):
                b = t % 4
                if s in ROPE_SLOT:
                    r = ROPE_SLOT.index(s)
                    if r >= 2:
                        act.wait_ge(roped, nth(L, 11, r - 2))
                    nc.scalar.activation(g[:, 4 + r % 2, :], ps[b][:, :], ACT.Copy).then_inc(raw_ready, 1)
                    act.drain().then_inc(bank_free[b], 1)
                if s == 0:
                    act.wait_ge(x_split, nth(L, 2 * KT, KT - 1))
                    act.dma_start(lp[:, :], layer_params[bass.ds(L, 1)].rearrange("a p n -> p (a n)")
                                  ).then_inc(lp_loaded, 16)
                    root(L, 0, True)
                if 2 * B_V <= s < 2 * B_CONV:
                    if s == 2 * B_V:
                        act.wait_ge(rms_ready, nth(L, 2, 0))
                    col, u = (s - 2 * B_V) // 2 * 256, s % 2
                    for e in range(2):
                        last = nc.scalar.activation(v[:, 2 * u + e, col:col + 256], ps[b][:, 256 * e:256 * e + 256],
                                                    ACT.Copy, scale=rms_col[:, 2 * u + e:2 * u + e + 1])
                    last.then_inc(bank_free[b], 1)
                    if s == 2 * B_CONV - 1:
                        act.drain().then_inc(v_ready, 1)
                if 2 * B_CONV <= s < 2 * B_YCONV and (s - 2 * B_CONV) % 6 >= 4:
                    i = 2 * ((s - 2 * B_CONV) // 6) + s % 2
                    act.wait_ge(cy_ready, nth(L, AT, i))
                    nc.scalar.activation(y_hi[:, i, :], g[:, 6 + s % 2, :], ACT.Copy).then_inc(cy_hi, 1)
                h, part = divmod(s - HEAD_SLOT, 3)
                if part == 2 and 0 <= h < HEADS:
                    turned(L, h)
                if part == 0 and 1 <= h <= HEADS:
                    head_out(L, h - 1)
                if part == 0 and 0 <= h < HEADS:
                    exps(L, h)
                if s in Y_SLOT:
                    y_high(L, Y_SLOT.index(s))
                if 2 * B_G1 <= s < 2 * B_YATT:
                    i = s - 2 * B_G1
                    act.wait_ge(gate_ready, nth(L, 2 * KT, i))
                    nc.scalar.activation(g[:, i % 8, :], g[:, i % 8, :], ACT.Exp, scale=-1.0).then_inc(gate_exp, 1)

            with act.Fori(0, LAYERS) as L:
                for j in range(B_MLP):
                    t0, t1 = first_tile(j), first_tile(j + 1)
                    for t in range(t0, t1):
                        act.wait_ge(tile_done, nth(L, LAYER_TILES, t))
                        if t == t1 - 1:
                            w_split(L, j + 2)
                        if j < B_YCONV or B_G1 <= j < B_YATT:
                            beside(L, 2 * j + t - t0, t)
                        elif j < B_G1:
                            n = t - first_tile(B_YCONV)
                            nc.scalar.activation(yc[:, n, :], ps[t % 4][:, :], ACT.Copy
                                                 ).then_inc(bank_free[t % 4], 1)
                            if n == KT - 1:
                                act.drain().then_inc(yc_ready, 1)
                            if (t - t0) % 2:
                                beside(L, 2 * j + (t - t0) // 2, t)
                        elif j < B_MIX:
                            n = t - first_tile(B_YATT)
                            act.wait_ge(merged_ready, nth(L, KT, n))
                            nc.scalar.activation(b_hi[:, n, :], g[:, n, :], ACT.Copy).then_inc(merged_hi, 1)
                        else:
                            n = t - first_tile(B_MIX)
                            if n == 0:
                                act.wait_ge(lp_loaded, nth(L, 1, 0, 16))
                            act.wait_ge(x_ready, nth(L, 2 * KT, n))
                            x_parts(n, lp[:, LP_GMLP + n:LP_GMLP + n + 1])
                root(L, 1)

                def chunk(c, last):
                    for n in range(16):
                        act.wait_ge(tile_done, nth(L, LAYER_TILES, c * 16 + (first_tile(B_MLP) + n)))
                        if n % 2:
                            w_split(L, B_MLP + n // 2 + 2, c)
                        if n in (0, 9, 11):
                            p = (0, 9, 11).index(n)
                            act.wait_ge(ada_used, nth(L, 12, c * 3 + p))
                            act.dma_start(ada_w[:, :, :], ada[bass.ds(L * 12 + c * 3 + p, 1)].rearrange(
                                "a p (k n) -> p (a k) n", k=TT)).then_inc(ada_loaded, 16)
                        if n < 8:
                            act.wait_ge(h_ready, nth(L, 8 * CHUNKS, c * 8 + n))
                            nc.scalar.activation(b_hi[:, n, :], g[:, 6 + n % 2, :], ACT.Copy).then_inc(h_hi, 1)
                        elif last:
                            act.wait_ge(x_ready, nth(L, 2 * KT, n))
                            x_parts(n - 8, lp[:, LP_GNEXT + n - 8:LP_GNEXT + n - 7])

                with act.Fori(0, CHUNKS - 1) as c:
                    chunk(c, False)
                chunk(CHUNKS - 1, True)

            L = LAYERS
            second = [(bias[:, :], mult_bias), (tri, tri_mask), (sel, selectors)]
            for dst, src in second:
                act.dma_start(dst, src).then_inc(second_loaded, 16)
            root(L, 0)
            for n in range(KT):
                act.wait_ge(x_ready, nth(L, 2 * KT, n))
                nc.scalar.activation(g[:, n % 2, :], x[:, n, :], ACT.Square).then_inc(x_sq, 1)
            root(L, 1)

            def modulated(base, shift):
                for n in range(KT):
                    act.wait_ge(xm_ready, base + n + 1)
                    nc.scalar.activation(a_hi[:, n, :], g[:, 4 + n % 2, :], ACT.Identity,
                                         bias=mod[:, shift + n:shift + n + 1]).then_inc(xm_hi, 1)

            modulated(0, 0)

            def qk_root(r):
                act.wait_ge(qn_ms, r + 1)
                nc.scalar.activation(nroot, nms, ACT.Sqrt).then_inc(qn_root, 1)

            for j in range(C_OUT):
                for u in range(2):
                    t = 2 * j + u
                    b = t % 4
                    act.wait_ge(tile_done, nth(L, LAYER_TILES, t))
                    if u:
                        w_split(L, j + 2)
                    if j < C_VA:
                        if t >= 2:
                            act.wait_ge(qk_normed, t - 2 + 1)
                        nc.scalar.activation(g[:, 4 + t % 2, :], ps[b][:, :], ACT.Copy)
                        nc.scalar.activation(g[:, t % 2, :], ps[b][:, :], ACT.Square).then_inc(qn_sq, 1)
                        act.drain().then_inc(bank_free[b], 1)
                    if 1 <= t <= 8:
                        qk_root(t - 1)
                    if C_VA <= j < C_QM or C_VM <= j < C_OG:
                        first = C_VA if j < C_QM else C_VM
                        dst, col = (v, mv)[first == C_VM], (j - first) * 256
                        for e in range(2):
                            last = nc.scalar.activation(dst[:, 2 * u + e, col:col + 256],
                                                        ps[b][:, 256 * e:256 * e + 256], ACT.Copy)
                        last.then_inc(bank_free[b], 1)
                        if t == 2 * first + 3:
                            act.drain().then_inc((v2_ready, mv_ready)[first == C_VM], 1)
                    if C_QM <= j < C_VM:
                        i = t - 2 * C_QM
                        act.wait_ge(mc_ready, i + 1)
                        dst = mq[:, i, :] if i < MH else mk[:, i - MH, :]
                        nc.scalar.activation(dst, g[:, 4 + i % 2, :], ACT.Silu).then_inc(mc_silu, 1)
                    if C_OG <= j < C_IF:
                        i = t - 2 * C_OG
                        nc.scalar.activation(og[i], ps[b][:, :], ACT.Sigmoid).then_inc(bank_free[b], 1)
                        if i == MH - 1:
                            act.drain().then_inc(og_ready, 1)
                h = j - C_QM
                if 1 <= h <= HEADS:
                    turned(L, h - 1)
                    head_out(L, h - 1)
                    if h % 2 == 0:
                        y_high(L, h // 2 - 1)
                if 0 <= h < HEADS:
                    exps(L, h)

            act.wait_ge(f_ready, 1)
            nc.scalar.activation(row_e, row_b, ACT.Abs)
            act.drain()
            nc.scalar.activation(row_e, row_e, ACT.Exp, scale=-1.0)
            act.drain()
            nc.scalar.activation(row_e, row_e, ACT.Ln, bias=1.0).then_inc(f_log, 1)
            act.wait_ge(m_rows, 1)
            nc.scalar.activation(row_e, row_b, ACT.Exp, scale=-1.0).then_inc(m_exp, 1)
            for h in range(MH):
                act.wait_ge(m_gap, h + 1)
                nc.scalar.activation(pr[:, :], pr[:, :], ACT.Exp, scale=-1.0).then_inc(m_decay, 1)
                act.wait_ge(m_h, h + 1)
                nc.scalar.activation(pr[:, 0:S], g[:, 5, :], ACT.Square).then_inc(m_sq, 1)
                act.wait_ge(m_ms, h + 1)
                nc.scalar.activation(pr[:, S:2 * S], g[:, 4, :], ACT.Sqrt).then_inc(m_root, 1)
                act.wait_ge(m_out, h + 1)
                nc.scalar.activation(a_hi[:, h, :], g[:, 5, :], ACT.Copy).then_inc(m_hi, 1)

            for j in range(C_OUT, C_FF):
                for u in range(2):
                    t = 2 * j + u
                    act.wait_ge(tile_done, nth(L, LAYER_TILES, t))
                    if u:
                        w_split(L, j + 2)
                    n = t - 2 * C_OUT
                    act.wait_ge(x_ready, nth(L, 2 * KT, KT + n))
                    nc.scalar.activation(g[:, n % 2, :], x[:, n, :], ACT.Square).then_inc(x_sq, 1)
            root(L, 2)
            modulated(KT, 3 * KT)
            j, hid = C_FF, 0
            for nt in FF_TILES:
                for b in range(nt + 4):
                    for u in range(2):
                        act.wait_ge(tile_done, nth(L, LAYER_TILES, 2 * j + u))
                        if u and j + 2 < SECOND_BLOCKS:
                            w_split(L, j + 2)
                        if b < nt and b % 2 == 0:
                            n = hid + b + u
                            if n >= 2:
                                act.wait_ge(h_ready, nth(L, 8 * CHUNKS, n - 2))
                            nc.scalar.activation(g[:, 4 + u, :], ps[(2 * j + u) % 4][:, :], ACT.Silu
                                                 ).then_inc(silu_done, 1)
                            act.drain().then_inc(bank_free[(2 * j + u) % 4], 1)
                        elif b < nt:
                            n = hid + b - 1 + u
                            act.wait_ge(h_ready, nth(L, 8 * CHUNKS, n))
                            nc.scalar.activation(b_hi[:, n - hid, :], g[:, 6 + u, :], ACT.Copy).then_inc(h_hi, 1)
                    j += 1
                hid += nt

        @block.vector
        def _(dve):
            def tt(out_, a, b_, op):
                return nc.vector.tensor_tensor(out_, a, b_, op)

            def take(L, t, out_, scale):
                dve.wait_ge(tile_done, nth(L, LAYER_TILES, t))
                tt(out_, ps[t % 4][:, :], scale, ALU.mult).then_inc(bank_free[t % 4], 1)

            def refine(y, root_, mean, tmp, out_sem=None):
                nc.vector.reciprocal(y, root_)
                dve.drain()
                tt(tmp, y, y, ALU.mult)
                dve.drain()
                tt(tmp, tmp, mean, ALU.mult)
                dve.drain()
                nc.vector.tensor_scalar(tmp, tmp, -0.5, 1.5, ALU.mult, ALU.add)
                dve.drain()
                last = tt(y, y, tmp, ALU.mult)
                if out_sem is not None:
                    last.then_inc(out_sem, 1)

            def norm(L, which, cols=False):
                dve.wait_ge(ss_done, nth(L, 2, which))
                if cols:
                    nc.vector.tensor_scalar(rms_col[:, 4:8], ps[6][:, 0:TT], 1.0 / D, EPS, ALU.mult, ALU.add)
                nc.vector.tensor_scalar(nms, ps[7][:, :], 1.0 / D, EPS, ALU.mult, ALU.add).then_inc(ms_ready, 1)
                dve.wait_ge(root_ready, nth(L, 2, which))
                if cols:
                    refine(rms_col[:, 0:4], rms_col[:, 8:12], rms_col[:, 4:8], rms_col[:, 8:12])
                refine(rms[:, :], nroot, nms, ntmp, rms_ready)
                dve.drain()

            def low(L, n, k_, gain):
                dve.wait_ge(x_hi, nth(L, 2 * KT, k_))
                nc.vector.scalar_tensor_tensor(a_lo[:, n, :], x[:, n, :], gain, f32(a_hi[:, n, :]), ALU.mult,
                                               ALU.subtract).then_inc(x_split, 1)
                squares(L, n, k_)

            def squares(L, n, k_):
                dve.drain()
                dve.wait_ge(x_sq, nth(L, 2 * KT, k_))
                if n == 0:
                    last = nc.vector.tensor_copy(acc, g[:, 0, :])
                else:
                    last = tt(acc, acc, g[:, n % 2, :], ALU.add)
                if n == KT - 1:
                    last.then_inc(sq_summed, 1)

            for b in range(4):
                nc.vector.memset(top[:, b:b + 1], 0.0).then_inc(bank_free[b], 1)
            nc.vector.memset(top[:, 4:5], 0.0).then_inc(ada_used, 1)
            nc.vector.memset(top[:, 5:6], 0.0).then_inc(ada_taken, 1)
            dve.wait_ge(setup_loaded, 16 * 5)
            for n in range(KT):
                dve.wait_ge(x_hi, n + 1)
                gain = sp[:, SP_G0 + n:SP_G0 + n + 1]
                nc.vector.scalar_tensor_tensor(a_lo[:, n, :], x[:, n, :], gain, f32(a_hi[:, n, :]), ALU.mult,
                                               ALU.subtract).then_inc(x_split, 1)
                dve.wait_ge(x_sq, n + 1)
                if n == 0:
                    last = nc.vector.tensor_copy(acc, g[:, 0, :])
                else:
                    last = tt(acc, acc, g[:, n % 2, :], ALU.add)
                last.then_inc(sq_used, 1)
                dve.drain()
            nc.vector.memset(top[:, 6:7], 0.0).then_inc(sq_summed, 1)
            dve.wait_ge(c_silu, 1)

            rounds = [i for i in range(1, TT) for _ in range(TOPK // 8)]

            def mask_scores(L, h, scale):
                dve.wait_ge(scores_done, nth(L, HEADS, h))
                nc.vector.memset(nudge[:, :], 0.0)
                for i in range(TT):
                    nc.vector.tensor_tensor_reduce(out=pr[:, TRI[i]:TRI[i + 1]], in0=query_bank[i],
                                                   in1=bias[:, TRI[i]:TRI[i + 1]], scale=scale, scalar=-3.0e38,
                                                   op0=ALU.add, op1=ALU.max, accum_out=peak[:, i:i + 1])
                dve.drain()
                nc.vector.tensor_scalar(peak[:, 4:8], peak[:, 0:4], -1.0, None, ALU.mult).then_inc(masked, 1)

            def normalise(L, h):
                dve.wait_ge(exps_done, nth(L, HEADS, h))
                nc.vector.reciprocal(peak[:, 12:16], peak[:, 8:12])
                dve.drain()
                for i in range(TT):
                    last = nc.vector.tensor_scalar(pr[:, TRI[i]:TRI[i + 1]], pr[:, TRI[i]:TRI[i + 1]],
                                                   peak[:, 12 + i:13 + i], None, ALU.mult)
                dve.drain().then_inc(probs_ready, 1)

            def y_low(L, i):
                dve.wait_ge(y_hi_ready, nth(L, AT, i))
                tt(y_lo[:, i, :], q[:, i, :], f32(y_hi[:, i, :]), ALU.subtract).then_inc(y_split, 1)

            def gate_finish(L, i):
                dve.wait_ge(gate_exp, nth(L, 2 * KT, i))
                gi = g[:, i % 8, :]
                nc.vector.tensor_scalar(gi, gi, 1.0, None, ALU.add)
                dve.drain()
                nc.vector.reciprocal(gi, gi)
                dve.drain()
                if i < KT:
                    if i == 0:
                        dve.wait_ge(yc_ready, nth(L, 1, 0))
                    tt(yc[:, i, :], yc[:, i, :], gi, ALU.mult)
                    dve.drain()

            def convolve(L, s):
                pair, kind, e = (s - 2 * B_CONV) // 6, (s - 2 * B_CONV) % 6 // 2, s % 2
                i = 2 * pair + e
                first, second = g[:, 6 + e, :], g[:, 4 + e, :]
                if kind == 0:
                    take(L, s, first, rms[:, :])
                elif kind == 1:
                    take(L, s, second, rms[:, :])
                    dve.drain()
                    tt(first, first, second, ALU.mult)
                    dve.drain()
                    w = [lp[:, LP_CONV + 4 * tap + i:LP_CONV + 4 * tap + i + 1] for tap in range(3)]
                    nc.vector.tensor_scalar(second, first, w[2], None, ALU.mult)
                    for back in (1, 2):
                        dve.drain()
                        nc.vector.scalar_tensor_tensor(second[:, back:], first[:, 0:S - back], w[2 - back],
                                                       second[:, back:], ALU.mult, ALU.add)
                    dve.drain()
                else:
                    take(L, s, first, rms[:, :])
                    dve.drain()
                    tt(first, first, second, ALU.mult).then_inc(cy_ready, 1)
                    dve.wait_ge(cy_hi, nth(L, AT, i))
                    tt(y_lo[:, i, :], first, f32(y_hi[:, i, :]), ALU.subtract).then_inc(cy_split, 1)
                    dve.drain()

            def beside(L, s, t):
                if s == 0:
                    norm(L, 0, True)
                    for e in range(2):
                        tt(cs_tok[:, e, :], cs_rope[:, e, :], rms[:, :], ALU.mult)
                    dve.drain()
                for r, rs in enumerate(ROPE_SLOT):
                    if s == rs + 1:
                        dst = (iq[:, 0, :], iq[:, 1, :], ik[:, 0, :], *(q[:, i, :] for i in range(4)),
                               *(k[:, i, :] for i in range(4)))[r]
                        dve.wait_ge(raw_ready, nth(L, 11, r))
                        tt(dst, g[:, 4 + r % 2, :], cs_tok[:, 0, :], ALU.mult)
                        dve.wait_ge(rot_done, nth(L, 11, r))
                        tt(g[:, 7, :], ps[7][:, :], cs_tok[:, 1, :], ALU.mult)
                        dve.drain()
                        tt(dst, dst, g[:, 7, :], ALU.add).then_inc(roped, 1)
                if s == 3:
                    dve.wait_ge(tile_done, nth(L, LAYER_TILES, 3))
                    for i in range(TT):
                        last = nc.vector.tensor_scalar(iw[:, i, :], ps[3][:, IDX_HEADS * i:IDX_HEADS * (i + 1)],
                                                       rms_col[:, i:i + 1], (64 ** -0.5) * (IDX_HEADS ** -0.5),
                                                       ALU.mult, ALU.mult)
                    last.then_inc(bank_free[3], 1)
                if LOGIT_SLOT <= s < LOGIT_SLOT + IDX_HEADS:
                    h = s - LOGIT_SLOT
                    dve.drain()
                    dve.wait_ge(logits_done, nth(L, IDX_HEADS, h))
                    for i in range(1, TT):
                        to = (bias if h == 0 else pr)[:, TRI[i]:TRI[i + 1]]
                        last = nc.vector.tensor_scalar(to, query_bank[i], 0.0, iw[:, i, h:h + 1], ALU.max, ALU.mult)
                    last.then_inc(logits_used, 1)
                    dve.drain()
                    if h > 0:
                        tt(bias[:, TRI[1]:], bias[:, TRI[1]:], pr[:, TRI[1]:], ALU.add)
                        dve.drain()
                    if h == IDX_HEADS - 1:
                        for i in range(1, TT):
                            nc.vector.memset(bias[0:64, TRI[i + 1] - 64:TRI[i + 1]], OUTSIDE)
                        dve.drain()
                if TOPK_SLOT <= s and TOPK_STEPS * (s - TOPK_SLOT) < len(rounds):
                    done = TOPK_STEPS * (s - TOPK_SLOT)
                    for i in rounds[done:done + TOPK_STEPS]:
                        row = bias[:, TRI[i]:TRI[i + 1]]
                        nc.vector.max(top[:, :], row)
                        dve.drain()
                        nc.vector.match_replace(row, top[:, :], row, TAKEN)
                        dve.drain()
                    if done + TOPK_STEPS >= len(rounds):
                        left = bias[:, TRI[1]:]
                        nc.vector.tensor_scalar(left, left, 0.5 * (TAKEN + OUTSIDE), NEG, ALU.is_gt, ALU.mult)
                        dve.drain()
                if 2 * B_CONV <= s < 2 * B_YCONV:
                    if s == 2 * B_CONV:
                        dve.wait_ge(lp_loaded, nth(L, 1, 0, 16))
                    convolve(L, s)
                if 2 * B_G1 <= s < 2 * B_YATT:
                    i = s - 2 * B_G1
                    if i > 0:
                        gate_finish(L, i - 1)
                    dve.wait_ge(tile_done, nth(L, LAYER_TILES, t))
                    tt(g[:, i % 8, :], ps[t % 4][:, :], rms[:, :], ALU.mult).then_inc(bank_free[t % 4], 1)
                    dve.drain().then_inc(gate_ready, 1)
                h, part = divmod(s - HEAD_SLOT, 3)
                if part == 0 and 0 <= h < HEADS:
                    mask_scores(L, h, HD ** -0.5)
                if part == 1 and 0 <= h < HEADS:
                    normalise(L, h)
                if s in Y_SLOT:
                    y_low(L, Y_SLOT.index(s))

            with dve.Fori(0, LAYERS) as L:
                for j in range(B_YATT):
                    t0, t1 = first_tile(j), first_tile(j + 1)
                    for u in range(2):
                        beside(L, 2 * j + u, t0 + u if t1 - t0 == 2 else t0 + 2 * u + 1)
                gate_finish(L, 2 * KT - 1)

                def merged_low(n):
                    dve.wait_ge(merged_hi, nth(L, KT, n))
                    tt(b_lo[:, n, :], g[:, n, :], f32(b_hi[:, n, :]), ALU.subtract).then_inc(merged_split, 1)

                for n in range(KT):
                    take(L, first_tile(B_YATT) + n, g[:, n, :], g[:, n, :])
                    dve.drain()
                    tt(g[:, n, :], g[:, n, :], yc[:, n, :], ALU.add).then_inc(merged_ready, 1)
                    if n > 0:
                        merged_low(n - 1)
                merged_low(KT - 1)

                def x_add(t, n, done):
                    last = tt(x[:, n, :], x[:, n, :], ps[t % 4][:, :], ALU.add)
                    last.then_inc(bank_free[t % 4], 1)
                    if done:
                        dve.drain().then_inc(x_ready, 1)

                for n in range(KT):
                    t = first_tile(B_MIX) + n
                    dve.wait_ge(tile_done, nth(L, LAYER_TILES, t))
                    x_add(t, n, True)
                    if n > 0:
                        low(L, n - 1, KT + n - 1, lp[:, LP_GMLP + n - 1:LP_GMLP + n])
                low(L, KT - 1, 2 * KT - 1, lp[:, LP_GMLP + KT - 1:LP_GMLP + KT])
                norm(L, 1)

                def chunk(c, last_chunk):
                    def h_low(n):
                        dve.wait_ge(h_hi, nth(L, 8 * CHUNKS, c * 8 + n))
                        tt(b_lo[:, n, :], g[:, 6 + n % 2, :], f32(b_hi[:, n, :]), ALU.subtract).then_inc(h_split, 1)
                        dve.drain()

                    for n in range(8):
                        dve.wait_ge(tile_done, nth(L, LAYER_TILES, c * 16 + (first_tile(B_MLP) + n)))
                        t = g[:, 4 + n % 2, :]
                        tt(t, ps[n % 4][:, :], rms[:, :], ALU.mult).then_inc(bank_free[n % 4], 1)
                        dve.drain()
                        nc.vector.scalar_tensor_tensor(g[:, 6 + n % 2, :], t, 0.0, t, ALU.max, ALU.mult
                                                       ).then_inc(h_ready, 1)
                        if n > 0:
                            h_low(n - 1)
                    h_low(7)
                    for n in range(8, 16):
                        dve.wait_ge(tile_done, nth(L, LAYER_TILES, c * 16 + (first_tile(B_MLP) + n)))
                        x_add(n, n - 8, last_chunk)
                        if last_chunk and n > 8:
                            low(L, n - 9, KT + n - 1, lp[:, LP_GNEXT + n - 9:LP_GNEXT + n - 8])
                        p = (n - 8) // 2
                        if n % 2 == 0 and p < 3:
                            dve.drain()
                            dve.wait_ge(ada_loaded, nth(L, 12, c * 3 + p, 16))
                            tt(ada_p.rearrange("p (k n) -> p k n", k=KT),
                               ada_w[:, :, :].rearrange("p a (b n) -> p (a b) n", b=2),
                               cs[:, :].unsqueeze(2).to_broadcast([P, KT, 256]), ALU.mult).then_inc(ada_used, 1)
                            dve.drain()
                            if p > 0:
                                dve.wait_ge(ada_done, nth(L, 12, c * 3 + p - 1))
                            nc.vector.tensor_reduce(out=ada_s, in_=ada_p.rearrange("p (k n) -> p n k", k=KT),
                                                    axis=AX_X, op=ALU.add).then_inc(ada_summed, 1)
                        if n % 2 and 1 <= p <= 3:
                            p -= 1
                            dve.wait_ge(ada_done, nth(L, 12, c * 3 + p))
                            col = (L * 12 + c * 3 + p) * 2
                            tt(mod[:, bass.ds(col, 2)], ps[7][:, 0:2], sp[:, bass.ds(col + SP_BADA, 2)], ALU.add
                               ).then_inc(ada_taken, 1)

                with dve.Fori(0, CHUNKS - 1) as c:
                    chunk(c, False)
                chunk(CHUNKS - 1, True)
                low(L, KT - 1, 3 * KT - 1, lp[:, LP_GNEXT + KT - 1:LP_GNEXT + KT])

            L = LAYERS
            norm(L, 0)
            for n in range(KT):
                nc.vector.scalar_tensor_tensor(x[:, n, :], x[:, n, :], sp[:, SP_GFIN + n:SP_GFIN + n + 1], rms[:, :],
                                               ALU.mult, ALU.mult).then_inc(x_ready, 1)
                if n > 0:
                    squares(L, n - 1, KT + n - 1)
            squares(L, KT - 1, 2 * KT - 1)
            for e, (gain, scale) in enumerate(((SP_GMIX, KT), (SP_GFFN, 4 * KT))):
                nc.vector.scalar_tensor_tensor(gs[:, e * KT:(e + 1) * KT], mod[:, scale:scale + KT], 1.0,
                                               sp[:, gain:gain + KT], ALU.add, ALU.mult)
            dve.drain()
            norm(L, 1)

            def modulated(base, e, shift):
                def xm_low(n):
                    dve.wait_ge(xm_hi, base + n + 1)
                    nc.vector.scalar_tensor_tensor(a_lo[:, n, :], g[:, 4 + n % 2, :], mod[:, shift + n:shift + n + 1],
                                                   f32(a_hi[:, n, :]), ALU.add, ALU.subtract).then_inc(xm_split, 1)
                    dve.drain()

                for n in range(KT):
                    nc.vector.scalar_tensor_tensor(g[:, 4 + n % 2, :], x[:, n, :], gs[:, e * KT + n:e * KT + n + 1],
                                                   rms[:, :], ALU.mult, ALU.mult).then_inc(xm_ready, 1)
                    if n > 0:
                        xm_low(n - 1)
                xm_low(KT - 1)

            modulated(0, 0, 0)

            def qk_norm(r):
                dve.wait_ge(qn_ss, r + 1)
                nc.vector.tensor_scalar(nms, ps[7][:, :], 1.0 / HD, EPS, ALU.mult, ALU.add).then_inc(qn_ms, 1)
                dve.wait_ge(qn_root, r + 1)
                inv = pr[:, 0:S]
                refine(inv, nroot, nms, pr[:, S:2 * S])
                dve.drain()
                dst, gain = (q[:, r, :], SP_QG) if r < AT else (k[:, r - AT, :], SP_KG)
                last = nc.vector.scalar_tensor_tensor(dst, g[:, 4 + r % 2, :], sp[:, gain:gain + 1], inv,
                                                      ALU.mult, ALU.mult)
                last.then_inc(qk_normed, 1)
                dve.drain()

            for j in range(C_OUT):
                for u in range(2):
                    t = 2 * j + u
                    b = t % 4
                    if 1 <= t <= 8:
                        qk_norm(t - 1)
                    if C_QM <= j < C_VM:
                        i = t - 2 * C_QM
                        dve.wait_ge(tile_done, nth(L, LAYER_TILES, t))
                        if i >= 2:
                            dve.wait_ge(mc_silu, i - 2 + 1)
                        o = g[:, 4 + i % 2, :]
                        w = [sp[:, SP_WCONV + 8 * tap + i:SP_WCONV + 8 * tap + i + 1] for tap in range(4)]
                        nc.vector.tensor_scalar(o, ps[b][:, :], w[3], sp[:, SP_BCONV + i:SP_BCONV + i + 1],
                                                ALU.mult, ALU.add)
                        for back in (1, 2, 3):
                            dve.drain()
                            last = nc.vector.scalar_tensor_tensor(o[:, back:], ps[b][:, 0:S - back], w[3 - back],
                                                                  o[:, back:], ALU.mult, ALU.add)
                        last.then_inc(bank_free[b], 1)
                        dve.drain().then_inc(mc_ready, 1)
                    if j == C_IF:
                        dve.wait_ge(tile_done, nth(L, LAYER_TILES, t))
                        row, col = (row_b, SP_BF) if u else (row_a, SP_BI)
                        nc.vector.tensor_scalar(row, ps[b][0:MH, :], sp[0:MH, col:col + 1], None, ALU.add
                                                ).then_inc(bank_free[b], 1)
                h = j - C_QM
                if h == 0:
                    dve.wait_ge(second_loaded, 48)
                if 1 <= h <= HEADS and h % 2 == 0:
                    y_low(L, h // 2 - 1)
                if 0 <= h < HEADS:
                    mask_scores(L, h, HD ** -0.5)
                    normalise(L, h)

            dve.drain().then_inc(f_ready, 1)
            dve.wait_ge(f_log, 1)
            nc.vector.scalar_tensor_tensor(row_g, row_b, 0.0, row_e, ALU.min, ALU.subtract)
            dve.drain()
            nc.vector.memset(row_e, 1.0)
            dve.drain()
            nc.vector.tensor_tensor_scan(row_b, row_e, row_g, 0.0, ALU.mult, ALU.add)
            dve.drain()
            tt(row_a, row_a, row_b, ALU.subtract)
            dve.drain()
            nc.vector.tensor_tensor_scan(row_g, row_a, row_a, 0.0, ALU.max, ALU.max)
            dve.drain()
            tt(row_b, row_b, row_g, ALU.add).then_inc(m_rows, 1)
            dve.wait_ge(a_turned, 1)
            nc.vector.tensor_copy(acol[:, :, :].rearrange("p a b -> p (a b)"), ps[4][:, 0:TT * MH]).then_inc(a_cols, 1)
            dve.drain()
            for h in range(MH):
                dve.wait_ge(m_bc, h + 1)
                for i in range(TT):
                    last = nc.vector.tensor_scalar(pr[:, TRT[i]:TRT[i + 1]], ps[7][:, i * P:], acol[:, i, h:h + 1], 0.0,
                                                   ALU.subtract, ALU.max)
                dve.drain().then_inc(m_gap, 1)
                dve.wait_ge(m_decay, h + 1)
                dve.wait_ge(m_scores, h + 1)
                for i in range(TT):
                    nc.vector.scalar_tensor_tensor(pt[:, TRT[i]:TRT[i + 1]], key_bank[i], P ** -0.5,
                                                   pr[:, TRT[i]:TRT[i + 1]], ALU.mult, ALU.mult)
                dve.drain()
                for i in range(TT):
                    d = pt[:, TRT[i]:TRT[i] + P]
                    tt(d, d, tri, ALU.mult)
                dve.drain().then_inc(m_probs, 1)
                dve.wait_ge(m_num, h + 1)
                den, hh = g[:, 4, :], g[:, 5, :]
                nc.vector.tensor_scalar(den, ps[1][:, :], -1.0, None, ALU.mult)
                dve.drain()
                tt(den, den, ps[1][:, :], ALU.max)
                dve.drain()
                tt(den, den, ps[3][:, :], ALU.max)
                dve.drain()
                nc.vector.reciprocal(den, den)
                dve.drain()
                tt(hh, ps[0][:, :], den, ALU.mult).then_inc(m_h, 1)
                dve.wait_ge(m_ss, h + 1)
                dve.drain()
                nc.vector.tensor_scalar(den, ps[2][:, :], 1.0 / P, EPS, ALU.mult, ALU.add).then_inc(m_ms, 1)
                dve.wait_ge(m_root, h + 1)
                refine(pr[:, 0:S], pr[:, S:2 * S], den, pr[:, S:2 * S])
                dve.drain()
                nc.vector.scalar_tensor_tensor(hh, hh, sp[:, SP_MG + h:SP_MG + h + 1], pr[:, 0:S], ALU.mult, ALU.mult)
                if h == 0:
                    dve.wait_ge(og_ready, 1)
                dve.drain()
                tt(hh, hh, og[h], ALU.mult).then_inc(m_out, 1)
                dve.wait_ge(m_hi, h + 1)
                tt(a_lo[:, h, :], hh, f32(a_hi[:, h, :]), ALU.subtract).then_inc(m_split, 1)
                dve.drain()

            for n in range(KT):
                t = 2 * C_OUT + n
                dve.wait_ge(tile_done, nth(L, LAYER_TILES, t))
                nc.vector.scalar_tensor_tensor(x[:, n, :], ps[t % 4][:, :], mod[:, 2 * KT + n:2 * KT + n + 1],
                                               x[:, n, :], ALU.mult, ALU.add).then_inc(bank_free[t % 4], 1)
                dve.drain().then_inc(x_ready, 1)
                if n > 0:
                    squares(L, n - 1, 2 * KT + n - 1)
            squares(L, KT - 1, 3 * KT - 1)
            norm(L, 2)
            modulated(KT, 1, 3 * KT)
            j, hid = C_FF, 0
            for nt in FF_TILES:
                def h_low(n):
                    dve.wait_ge(h_hi, nth(L, 8 * CHUNKS, n))
                    tt(b_lo[:, n - hid, :], g[:, 6 + n % 2, :], f32(b_hi[:, n - hid, :]), ALU.subtract
                       ).then_inc(h_split, 1)

                for b in range(nt):
                    if b % 2:
                        for u in range(2):
                            t, n = 2 * j + u, hid + b - 1 + u
                            dve.wait_ge(tile_done, nth(L, LAYER_TILES, t))
                            dve.wait_ge(silu_done, n + 1)
                            tt(g[:, 6 + u, :], ps[t % 4][:, :], g[:, 4 + u, :], ALU.mult).then_inc(bank_free[t % 4], 1)
                            dve.drain().then_inc(h_ready, 1)
                        for u in range(2):
                            h_low(hid + b - 1 + u)
                        dve.drain()
                    j += 1
                for n in range(KT):
                    t = 2 * j + n
                    dve.wait_ge(tile_done, nth(L, LAYER_TILES, t))
                    last = nc.vector.scalar_tensor_tensor(x[:, n, :], ps[t % 4][:, :],
                                                          mod[:, 5 * KT + n:5 * KT + n + 1], x[:, n, :],
                                                          ALU.mult, ALU.add)
                    last.then_inc(bank_free[t % 4], 1)
                    if nt == FF_TILES[-1]:
                        dve.drain().then_inc(x_final, 1)
                j += 4
                hid += nt


def rope_constants():
    half = HD // 8
    inv = (1.0 / (np.float32(500000.0) ** (np.arange(0, 2 * half, 2, dtype=np.float32) / np.float32(2 * half)))).astype(np.float32)
    ang = np.arange(S, dtype=np.float32)[:, None] * inv[None, :]
    c, s = np.ones((P, 2, S), np.float32), None
    c[:, 1, :] = 0.0
    for f in range(P):
        if f % HD < 2 * half:
            c[f, 0, :] = np.cos(ang[:, f % half])
            c[f, 1, :] = np.sin(ang[:, f % half])
    return c


def constant_matrices():
    half = HD // 8
    m = np.zeros((P, K_N), np.float32)
    for base in (0, HD):
        for i in range(half):
            m[base + half + i, K_ROT + base + i] = -1.0
            m[base + i, K_ROT + base + half + i] = 1.0
        m[base:base + HD, K_HALF + base:K_HALF + base + HD] = 1.0
    m[:, K_ID:K_ID + P] = np.eye(P, dtype=np.float32)
    m[:, K_ONES:K_ONES + P] = 1.0
    return m


def key_biases():
    t = np.arange(P)
    near = np.where(t[None, :] < (t[:, None] // 64 + 1) * 64, 0.0, NEG).astype(np.float32)
    many = np.zeros((P, TRI[TT]), np.float32)
    for i in range(TT):
        rel = (i * P + t[:, None]) - np.arange((i + 1) * P)[None, :]
        n = sum(((rel >= 0) & (rel % d == 0) & (rel <= w)).astype(np.float32) for w, d in ((128, 1), (512, 4), (2048, 16)))
        many[:, TRI[i]:TRI[i + 1]] = np.where(n > 0, 8.0 * np.log(np.maximum(n, 1.0)), NEG)
    return near, many


def kernel(**inputs):
    import concourse.bacc as bacc
    from concourse.bass_utils import run_bass_kernel_spmd

    a = {n: np.asarray(v) for n, v in inputs.items()}

    def blocks(w):
        depth, cols = w.shape
        wide = BLK * P // depth if depth in (512, 1024) else 256
        n = -(-cols // wide)
        full = np.zeros((max(depth, 512) if depth == 512 else 1024, n * wide), w.dtype)
        full[:depth, :cols] = w
        return full.reshape(-1, P, n, wide).transpose(2, 1, 0, 3).reshape(n, P, BLK)

    parts = []
    for l in range(LAYERS):
        w = a["w_in"][l]
        cut = np.split(w, np.cumsum([512, 512, 512, 256, 64, 4, 512, 512, 512, 1024]), axis=1)
        wq, wk, wv, wiq, wik, wiw, wb, wc, wh, wg0, wg1 = cut
        parts += [blocks(wiq), blocks(np.concatenate([wik, wik, wiw], axis=1)), blocks(wq), blocks(wk), blocks(wv)]
        for pair in range(2):
            parts += [blocks(m[:, 256 * pair:256 * pair + 256]) for m in (wc, wh, wb)]
        parts += [blocks(a["w_conv_out"][l]), blocks(wg1), blocks(wg0), blocks(a["w_attn_out"][l]),
                  blocks(a["w_mix_out"][l])]
        for c in range(CHUNKS):
            parts += [blocks(a["w_mlp_up"][l][:, 1024 * c:1024 * c + 1024]),
                      blocks(a["w_mlp_down"][l][1024 * c:1024 * c + 1024])]
    w = a["w_in_2"][0]
    parts += [blocks(w[:, 512 * i:512 * i + 512]) for i in range(7)] + [blocks(w[:, 3584:])]
    parts += [blocks(a["w_out_2"][0])]
    at = 0
    for nt in FF_TILES:
        for i in range(0, nt, 2):
            parts += [blocks(a[m][0][:, at + P * i:at + P * i + 256]) for m in ("w_gate_2", "w_up_2")]
        parts += [blocks(a["w_down_2"][0][at:at + P * nt])]
        at += P * nt
    weights = np.concatenate(parts)
    assert weights.shape[0] == BLOCKS

    def cols(vec):
        return vec.reshape(-1, P).T

    layer_params = np.stack([np.concatenate(
        [cols(a["norm_mlp"][l])] + [cols(a["conv_w"][l][t]) for t in range(3)]
        + [cols(a["norm_mix"][l + 1] if l + 1 < LAYERS else a["norm_final"])], axis=1) for l in range(LAYERS)])

    def rows4(vec):
        full = np.zeros((P, 1), vec.dtype)
        full[:MH, 0] = vec
        return full

    params = np.concatenate(
        [cols(a["g_mix_2"][0]), cols(a["g_ffn_2"][0]), cols(a["norm_final"]), cols(a["b_conv_2"][0])]
        + [cols(a["w_conv_2"][0][t]) for t in range(4)]
        + [np.tile(a["q_norm_g_2"][0], 2)[:, None], np.tile(a["k_norm_g_2"][0], 2)[:, None],
           cols(a["mlstm_norm_g_2"][0]), cols(a["b_ada_2"][0]), cols(a["c_2"][0]),
           rows4(a["b_igate_2"][0]), rows4(a["b_fgate_2"][0]), cols(a["norm_mix"][0])], axis=1)
    near, many = key_biases()
    t = np.arange(P)
    selectors = np.zeros((MH, MH * P), np.float32)
    for h in range(MH):
        selectors[h, h * P:(h + 1) * P] = 1.0
    arrays = {
        "weights": weights,
        "ada": blocks(a["w_ada_2"][0]),
        "consts": constant_matrices(),
        "rope": rope_constants(),
        "tri_bias": near,
        "mult_bias": many,
        "tri_mask": (t[:, None] <= t[None, :]).astype(np.float32),
        "layer_params": layer_params,
        "params": params,
        "x_in": a["x"][0].T,
        "selectors": selectors,
    }
    arrays = {f"in_{n}": np.ascontiguousarray(v) for n, v in arrays.items()}
    nc = bacc.Bacc("TRN2", target_bir_lowering=False, num_devices=1)
    args = [nc.dram_tensor(n, v.shape, mybir.dt.from_np(v.dtype), kind="ExternalInput").ap() for n, v in arrays.items()]
    args.append(nc.dram_tensor("out", (D, S), F32, kind="ExternalOutput").ap())
    two_blocks(nc, *args)
    r = run_bass_kernel_spmd(nc, [arrays], core_ids=[0])
    return np.ascontiguousarray(r.results[0]["out"].T)[None]
```

```python
import numpy as np
from contextlib import ExitStack

import concourse.bass as bass
from concourse import mybir

F32 = mybir.dt.float32
F32R = mybir.dt.float32r
ALU = mybir.AluOpType
ACT = mybir.ActivationFunctionType
AX_X = mybir.AxisListType.X

P = 128
S = 512
D = 1024
KT = D // P
LAYERS = 2
HEADS, HD = 8, 64
IDX_HEADS = 4
TOPK = min(256, S // 4)
ATT = HEADS * HD
AT = ATT // P
TT = S // P
MH = 4
CHUNKS = 4
D_FF = 2816
FF_TILES = [8, 8, 6]
EPS = 1e-6
NEG = -1.0e30
OUTSIDE = -2.0e38
TAKEN = -3.0e38

BLK = 2048
B_IQ, B_IK, B_Q, B_K, B_V, B_CONV, B_YCONV, B_G1, B_G0, B_YATT, B_MIX, B_MLP = 0, 1, 2, 4, 6, 8, 14, 16, 20, 24, 26, 30
LAYER_BLOCKS = B_MLP + 8 * CHUNKS
C_QA, C_KA, C_VA, C_IF, C_QM, C_KM, C_VM, C_OG, C_OUT, C_FF = 0, 2, 4, 6, 7, 9, 11, 13, 15, 19
HEAD2_SLOT = 2 * C_IF
SECOND_BLOCKS = C_FF + sum(n + 4 for n in FF_TILES)
BLOCKS = LAYERS * LAYER_BLOCKS + SECOND_BLOCKS


def first_tile(j):
    return 2 * j + 2 * min(max(j - B_YCONV, 0), 2) + 2 * min(max(j - B_YATT, 0), 2)


LAYER_TILES = first_tile(LAYER_BLOCKS)
TRI = [0, 128, 384, 768, 1280]
TRT = [0, 512, 896, 1152, 1280]

ROPE_SLOT = [0, 1, 2, 4, 5, 6, 7, 8, 9, 10, 11]
LOGIT_SLOT = 5
TOPK_SLOT, TOPK_STEPS = 9, 4
HEAD_SLOT = 21
Y_SLOT = [33, 34, 40, 46]

K_ROT, K_ID, K_ONES, K_HALF, K_N = 0, 128, 256, 384, 512
LP_GMLP, LP_CONV, LP_GNEXT, LP_N = 0, 8, 20, 28
SP_GMIX, SP_GFFN, SP_GFIN, SP_BCONV, SP_WCONV, SP_QG, SP_KG, SP_MG, SP_BADA, SP_C, SP_BI, SP_BF, SP_G0, SP_N = (
    0, 8, 16, 24, 32, 64, 65, 66, 70, 118, 126, 127, 128, 136)


def nth(layer, per_layer, k, step=1):
    return layer * (per_layer * step) + k * step + step


def two_blocks(nc, weights, ada, consts, rope, tri_bias, mult_bias, tri_mask, layer_params, params, x_in, selectors, out):
    with ExitStack() as ctx:
        def sb(name, shape, dt=F32, scope=ctx):
            return scope.enter_context(nc.sbuf_tensor(name, shape, dt))

        x = sb("x", [P, KT, S])
        a_hi = sb("a_hi", [P, KT, S], F32R)
        a_lo = sb("a_lo", [P, KT, S], F32R)
        w_raw = sb("w_raw", [P, 2, BLK])
        w_hi = sb("w_hi", [P, 2, BLK], F32R)
        w_lo = sb("w_lo", [P, 2, BLK], F32R)
        v = sb("v", [P, TT, ATT])
        y_hi = sb("y_hi", [P, AT, S], F32R)
        y_lo = sb("y_lo", [P, AT, S], F32R)
        yc = sb("yc", [P, KT, S])
        g = sb("g", [P, KT, S])
        bias = sb("bias", [P, TRI[TT]])
        cs_rope = sb("cs_rope", [P, 2, S])
        cs_tok = sb("cs_tok", [P, 2, S])
        kc = sb("kc", [P, K_N])
        rms = sb("rms", [P, S])
        rms_col = sb("rms_col", [P, 3 * TT])
        lp = sb("lp", [P, LP_N])
        sp = sb("sp", [P, SP_N])
        mod = sb("mod", [P, 48])
        gs = sb("gs", [P, 2 * KT])
        cs = sb("cs", [P, KT])
        iw = sb("iw", [P, TT, IDX_HEADS])
        top = sb("top", [P, 8])
        peak = sb("peak", [P, 4 * TT])
        nudge = sb("nudge", [P, 1])
        acol = sb("acol", [P, 2, TT, MH])
        qcol = sb("qcol", [P, 3, 32])
        mcol = sb("mcol", [P, 4, TT])
        mt = sb("mt", [P, S])
        one = ExitStack()
        q = sb("q", [P, AT, S], F32, one)
        k = sb("k", [P, AT, S], F32, one)
        iq = sb("iq", [P, 2, S], F32, one)
        ik = sb("ik", [P, 1, S], F32, one)
        pr = sb("pr", [P, TRI[TT]], F32, one)
        pt = sb("pt", [P, TRT[TT]], F32, one)
        one.close()
        two = ExitStack()
        b_hi = sb("b_hi", [P, KT, S], F32R, two)
        b_lo = sb("b_lo", [P, KT, S], F32R, two)
        two.close()
        one.enter_context(nc.sbuf_tensor("region_1", [P, 2 * KT * S], F32))
        ctx.enter_context(one)

        ps = [ctx.enter_context(nc.psum_tensor(f"ps{b}", [P, S], F32)) for b in range(8)]

        def sem(name):
            return ctx.enter_context(nc.semaphore(name))

        params_loaded = sem("params_loaded")
        x_loaded = [sem(f"x_loaded{e}") for e in range(2)]
        setup_loaded = sem("setup_loaded")
        w_loaded = [sem(f"w_loaded{s}") for s in range(2)]
        w_hi_ready = sem("w_hi_ready")
        w_lo_ready = sem("w_lo_ready")
        tile_done = sem("tile_done")
        bank_free = [sem(f"bank_free{b}") for b in range(4)]
        lp_loaded = sem("lp_loaded")
        x_ready = sem("x_ready")
        x_hi = sem("x_hi")
        x_sq = sem("x_sq")
        x_split = sem("x_split")
        sq_used = sem("sq_used")
        sq_summed = sem("sq_summed")
        ss_done = sem("ss_done")
        ms_ready = sem("ms_ready")
        root_ready = sem("root_ready")
        rms_spread = sem("rms_spread")
        rms_turned = sem("rms_turned")
        rms_ready = sem("rms_ready")
        raw_ready = sem("raw_ready")
        rot_done = sem("rot_done")
        roped = sem("roped")
        logits_done = sem("logits_done")
        logits_used = sem("logits_used")
        v_ready = sem("v_ready")
        cy_ready = sem("cy_ready")
        cy_hi = sem("cy_hi")
        cy_split = sem("cy_split")
        gate_ready = sem("gate_ready")
        gate_tanh = sem("gate_tanh")
        yc_ready = sem("yc_ready")
        scores_done = sem("scores_done")
        masked = sem("masked")
        exps_done = sem("exps_done")
        probs_ready = sem("probs_ready")
        probs_turned = sem("probs_turned")
        pt_ready = sem("pt_ready")
        head_done = sem("head_done")
        head_copied = sem("head_copied")
        y_hi_ready = sem("y_hi_ready")
        y_split = sem("y_split")
        merged_ready = sem("merged_ready")
        merged_hi = sem("merged_hi")
        merged_split = sem("merged_split")
        h_ready = sem("h_ready")
        h_hi = sem("h_hi")
        h_split = sem("h_split")
        ada_loaded = sem("ada_loaded")
        ada_used = sem("ada_used")
        ada_summed = sem("ada_summed")
        ada_done = sem("ada_done")
        ada_taken = sem("ada_taken")
        c_silu = sem("c_silu")
        second_loaded = sem("second_loaded")
        xm_ready = sem("xm_ready")
        xm_hi = sem("xm_hi")
        xm_split = sem("xm_split")
        qn_sq = sem("qn_sq")
        qn_ss = sem("qn_ss")
        qn_ms = sem("qn_ms")
        qn_root = sem("qn_root")
        qn_spread = sem("qn_spread")
        qn_turned = sem("qn_turned")
        qk_normed = sem("qk_normed")
        v2_ready = sem("v2_ready")
        mc_first = sem("mc_first")
        mc_ready = sem("mc_ready")
        mc_tanh = sem("mc_tanh")
        mc_silu = sem("mc_silu")
        mv_ready = sem("mv_ready")
        og_ready = sem("og_ready")
        f_ready = sem("f_ready")
        f_log = sem("f_log")
        m_rows = sem("m_rows")
        m_exp = sem("m_exp")
        a_turned = sem("a_turned")
        a_cols = sem("a_cols")
        m_bc = sem("m_bc")
        m_scores = sem("m_scores")
        m_gap = sem("m_gap")
        m_decay = sem("m_decay")
        m_probs = sem("m_probs")
        m_num = sem("m_num")
        m_sq = sem("m_sq")
        m_ss = sem("m_ss")
        m_ms = sem("m_ms")
        m_root = sem("m_root")
        m_spread = sem("m_spread")
        m_turned = sem("m_turned")
        m_out = sem("m_out")
        m_hi = sem("m_hi")
        m_split = sem("m_split")
        silu_done = sem("silu_done")
        x_final = sem("x_final")
        stored = sem("stored")

        block = ctx.enter_context(nc.Block())

        def wcols(t, slot, deep, kt, c0, n):
            return t[:, slot, :].rearrange("p (k c) -> p k c", k=deep)[:, kt, c0:c0 + n]

        rot_m, ident, ones, half = (kc[:, c:c + P] for c in (K_ROT, K_ID, K_ONES, K_HALF))
        acc = yc[:, KT - 1, :]
        nms, nroot, ntmp = g[:, 2, :], g[:, 3, :], g[:, 6, :]
        ada_w = v
        ada_p = yc[:, 0:4, :].rearrange("p a b -> p (a b)")
        ada_s = yc[:, 4, 0:256]
        mq, mk, mv = yc[:, 4:8, :], g[:, 0:4, :], yc[:, 0:4, :]
        og = [iq[:, 0, :], iq[:, 1, :], ik[:, 0, :], cs_rope[:, 0, :]]
        tri = cs_rope[:, 1, 0:P]
        sel = cs_tok[0:MH, 0, :]
        row_a, row_b, row_e, row_g = g[0:MH, 6, :], g[0:MH, 7, :], cs_tok[0:MH, 1, :], rms[0:MH, :]
        key_bank = (ps[4][:, :], ps[5][:, 0:384], ps[6][:, 0:256], ps[5][:, 384:512])
        query_bank = (ps[5][:, 384:512], ps[6][:, 0:256], ps[5][:, 0:384], ps[4][:, :])

        def f32(ap):
            return ap.bitcast(F32)

        @block.sync
        def _(sync):
            sync.dma_start(w_raw[:, 0, :], weights[0]).then_inc(w_loaded[0], 16)
            for e in range(2):
                sync.dma_start(x[:, 4 * e:4 * e + 4, :], x_in[4 * e * P:4 * (e + 1) * P].rearrange("(n p) t -> p n t", p=P)
                               ).then_inc(x_loaded[e], 16)
            sync.dma_start(w_raw[:, 1, :], weights[1]).then_inc(w_loaded[1], 16)
            with sync.Fori(1, BLOCKS // 2) as pair:
                for s in range(2):
                    sync.wait_ge(w_lo_ready, pair * 2 + (s - 1))
                    sync.dma_start(w_raw[:, s, :], weights[bass.ds(pair * 2 + s, 1)].rearrange("a p n -> p (a n)")
                                   ).then_inc(w_loaded[s], 16)
            sync.wait_ge(w_lo_ready, BLOCKS - 2)
            sync.dma_start(w_raw[:, 0, :], weights[BLOCKS - 1]).then_inc(w_loaded[0], 16)
            for n in range(KT):
                sync.wait_ge(x_final, n + 1)
                sync.dma_start(out[n * P:(n + 1) * P, :], x[:, n, :]).then_inc(stored, 16)
            sync.wait_ge(stored, 16 * KT)

        @block.gpsimd
        def _(pool):
            def split(n, s):
                pool.wait_ge(w_hi_ready, n + 1)
                nc.gpsimd.tensor_tensor(w_lo[:, s, :], w_raw[:, s, :], f32(w_hi[:, s, :]), ALU.subtract
                                        ).then_inc(w_lo_ready, 1)

            with pool.Fori(0, BLOCKS // 2) as pair:
                for s in range(2):
                    split(pair * 2 + s, s)
            split(BLOCKS - 1, (BLOCKS - 1) % 2)

        @block.tensor
        def _(pe):
            def product(o, s, deep, depth, c0, m, hi, lo, ready=None):
                for kt in range(depth):
                    if ready is not None:
                        ready(kt)
                    wh, wl = wcols(w_hi, s, deep, kt, c0, m), wcols(w_lo, s, deep, kt, c0, m)
                    nc.tensor.matmul(o, wh, hi(kt), start=kt == 0, stop=False)
                    nc.tensor.matmul(o, wh, lo(kt), start=False, stop=False)
                    last = nc.tensor.matmul(o, wl, hi(kt), start=False, stop=kt == depth - 1)
                last.then_inc(tile_done, 1)

            def tile(L, t, s, deep, c0, hi, lo, m=P, depth=None, ready=None):
                pe.wait_ge(bank_free[t % 4], nth(L, LAYER_TILES // 4, t // 4))
                product(ps[t % 4][0:m, :], s, deep, depth or deep, c0, m,
                        lambda kt: hi[:, kt, :], lambda kt: lo[:, kt, :], ready)

            def tile_pair(o, s, src, ready):
                for kt in range(KT):
                    ready(kt)
                    for u in range(2):
                        wh, wl = wcols(w_hi, s, KT, kt, u * P, P), wcols(w_lo, s, KT, kt, u * P, P)
                        nc.tensor.matmul(o[u], wh, src[0][:, kt, :], start=kt == 0, stop=False)
                        nc.tensor.matmul(o[u], wh, src[1][:, kt, :], start=False, stop=False)
                        last = nc.tensor.matmul(o[u], wl, src[0][:, kt, :], start=False, stop=kt == KT - 1)
                        if kt == KT - 1:
                            last.then_inc(tile_done, 1)

            def token_tile(L, t, s, parts, c0, n):
                pe.wait_ge(bank_free[t % 4], nth(L, LAYER_TILES // 4, t // 4))
                for tt, col in parts:
                    o = ps[t % 4][:, col:col + n]
                    for kt in range(KT):
                        ah, al = (m[:, kt, tt * P:(tt + 1) * P] for m in (a_hi, a_lo))
                        wh, wl = wcols(w_hi, s, KT, kt, c0, n), wcols(w_lo, s, KT, kt, c0, n)
                        nc.tensor.matmul(o, ah, wh, start=kt == 0, stop=False)
                        nc.tensor.matmul(o, ah, wl, start=False, stop=False)
                        last = nc.tensor.matmul(o, al, wh, start=False, stop=kt == KT - 1)
                last.then_inc(tile_done, 1)

            def sum_squares(L, which):
                pe.wait_ge(sq_summed, nth(L, 2, which if which < 2 else 1))
                for tt in range(TT):
                    last = nc.tensor.matmul(ps[6][:, tt:tt + 1], acc[:, tt * P:(tt + 1) * P], ones[:, 0:1],
                                            start=True, stop=True)
                last.then_inc(ss_done, 1)

            def turn_rms(L, which):
                pe.wait_ge(rms_spread, nth(L, 2, which))
                for tt in range(TT):
                    last = nc.tensor.transpose(ps[6][:, tt * P:(tt + 1) * P], g[:, 2, tt * P:(tt + 1) * P], ident)
                last.then_inc(rms_turned, 1)

            def scores(L, h):
                rows = slice(HD * (h % 2), HD * (h % 2) + HD)
                for i in range(TT):
                    last = nc.tensor.matmul(query_bank[i], q[rows, h // 2, i * P:(i + 1) * P],
                                            k[rows, h // 2, 0:(i + 1) * P], start=True, stop=True)
                last.then_inc(scores_done, 1)

            def transposes(L, h):
                pe.wait_ge(probs_ready, nth(L, HEADS, h))
                for j in range(TT):
                    for i in range(j, TT):
                        last = nc.tensor.transpose(key_bank[j][:, (i - j) * P:(i - j + 1) * P],
                                                   pr[:, TRI[i] + j * P:TRI[i] + (j + 1) * P], ident)
                last.then_inc(probs_turned, 1)

            def values(L, h):
                pe.wait_ge(pt_ready, nth(L, HEADS, h))
                if h > 0:
                    pe.wait_ge(head_copied, nth(L, HEADS, h - 1))
                rows = slice(HD * (h % 2), HD * (h % 2) + HD)
                for j in range(TT):
                    last = nc.tensor.matmul(ps[7][rows, j * P:], v[:, j, h * HD:(h + 1) * HD],
                                            pt[:, TRT[j]:TRT[j + 1]], start=j == 0, stop=j == TT - 1)
                last.then_inc(head_done, 1)

            def beside(L, s):
                if s == 0:
                    sum_squares(L, 0)
                if s == 2:
                    turn_rms(L, 0)
                for r, rs in enumerate(ROPE_SLOT):
                    if s == rs + 1:
                        pe.wait_ge(raw_ready, nth(L, 11, r))
                        if r > 0:
                            pe.wait_ge(roped, nth(L, 11, r - 1))
                        nc.tensor.matmul(ps[7][:, :], rot_m, g[:, 4 + r % 2, :], start=True, stop=True
                                         ).then_inc(rot_done, 1)
                if LOGIT_SLOT <= s < LOGIT_SLOT + IDX_HEADS:
                    h = s - LOGIT_SLOT
                    if h == 0:
                        pe.wait_ge(roped, nth(L, 11, 2))
                        pe.wait_ge(rms_ready, nth(L, 2, 0))
                    else:
                        pe.wait_ge(logits_used, nth(L, IDX_HEADS, h - 1))
                    rows = slice(64 * (h % 2), 64 * (h % 2) + 64)
                    for i in range(1, TT):
                        last = nc.tensor.matmul(query_bank[i], iq[rows, h // 2, i * P:(i + 1) * P],
                                                ik[rows, 0, 0:(i + 1) * P], start=True, stop=True)
                    last.then_inc(logits_done, 1)
                h, part = divmod(s - HEAD_SLOT, 3)
                if part == 2 and 0 <= h < HEADS:
                    transposes(L, h)
                if part == 0 and 1 <= h <= HEADS:
                    if h == 1:
                        pe.wait_ge(v_ready, nth(L, 1, 0))
                    values(L, h - 1)
                if part == 0 and 0 <= h < HEADS:
                    if h == 0:
                        pe.wait_ge(roped, nth(L, 11, 10))
                        pe.wait_ge(logits_used, nth(L, IDX_HEADS, IDX_HEADS - 1))
                    scores(L, h)

            with pe.Fori(0, LAYERS) as L:
                for j in range(B_MLP):
                    s, t = j % 2, first_tile(j)
                    pe.wait_ge(w_lo_ready, nth(L, LAYER_BLOCKS, j))
                    if j == B_IK:
                        tile(L, t, s, KT, 0, a_hi, a_lo)
                        beside(L, t)
                        token_tile(L, t + 1, s, [(tt, IDX_HEADS * tt) for tt in range(TT)], P, IDX_HEADS)
                        beside(L, t + 1)
                    elif B_V <= j < B_CONV:
                        for u in range(2):
                            token_tile(L, t + u, s, [(2 * u, 0), (2 * u + 1, 256)], 0, 256)
                            beside(L, t + u)
                    elif B_YCONV <= j < B_G1 or B_YATT <= j < B_MIX:
                        if j == B_YCONV:
                            pe.wait_ge(cy_split, nth(L, AT, AT - 1))
                        if j == B_YATT:
                            pe.wait_ge(y_split, nth(L, AT, AT - 1))
                        for u in range(4):
                            tile(L, t + u, s, AT, u * P, y_hi, y_lo)
                            if u % 2 and j < B_G1:
                                beside(L, 2 * j + u // 2)
                    else:
                        src = (b_hi, b_lo) if j >= B_MIX else (a_hi, a_lo)
                        if j == B_IQ:
                            for u in range(2):
                                pe.wait_ge(bank_free[u], nth(L, LAYER_TILES // 4, 0))
                            tile_pair((ps[0][:, :], ps[1][:, :]), s, src,
                                      lambda kt: pe.wait_ge(x_split, nth(L, 2 * KT, kt)))
                            beside(L, 0)
                            beside(L, 1)
                            continue
                        for u in range(2):
                            ready = None
                            if j == B_MIX and u == 0:
                                def ready(kt):
                                    pe.wait_ge(merged_split, nth(L, KT, kt))
                            tile(L, t + u, s, KT, u * P, *src, ready=ready)
                            if j < B_YATT:
                                beside(L, 2 * j + u)
                def chunk(c, first):
                    for b in range(8):
                        pe.wait_ge(w_lo_ready, nth(L, LAYER_BLOCKS, c * 8 + (B_MLP + b)))
                        if first and b == 0:
                            for u in range(2):
                                pe.wait_ge(bank_free[u], nth(L, LAYER_TILES // 4, first_tile(B_MLP) // 4))
                            tile_pair((ps[0][:, :], ps[1][:, :]), 0, (a_hi, a_lo),
                                      lambda kt: pe.wait_ge(x_split, nth(L, 2 * KT, KT + kt)))
                            sum_squares(L, 1)
                            continue
                        for u in range(2):
                            n = 2 * b + u
                            pe.wait_ge(bank_free[n % 4], nth(L, LAYER_TILES // 4, c * 4 + (first_tile(B_MLP) + n) // 4))
                            src = (a_hi, a_lo) if b < 4 else (b_hi, b_lo)
                            ready = None
                            if n == 8:
                                def ready(kt):
                                    pe.wait_ge(h_split, nth(L, 8 * CHUNKS, c * 8 + kt))
                            product(ps[n % 4][:, :], b % 2, KT, KT, u * P, P,
                                    lambda kt: src[0][:, kt, :], lambda kt: src[1][:, kt, :], ready)
                            if first and n == 2:
                                turn_rms(L, 1)
                            if n in (10, 12, 14):
                                p = (n - 10) // 2
                                pe.wait_ge(ada_summed, nth(L, 12, c * 3 + p))
                                pe.wait_ge(ada_taken, nth(L, 12, c * 3 + p))
                                for e in range(2):
                                    last = nc.tensor.matmul(ps[7][:, e:e + 1], ada_s[:, e * P:(e + 1) * P],
                                                            ones[:, 0:1], start=True, stop=True)
                                last.then_inc(ada_done, 1)

                chunk(0, True)
                with pe.Fori(1, CHUNKS) as c:
                    chunk(c, False)

            L = LAYERS
            sum_squares(L, 0)
            turn_rms(L, 0)
            pe.wait_ge(rms_ready, nth(L, 2, 0))
            for n in range(KT):
                pe.wait_ge(x_sq, nth(L, 2 * KT, KT + n))
                for tt in range(TT):
                    last = nc.tensor.matmul(ps[6][:, tt:tt + 1], g[:, n, tt * P:(tt + 1) * P], ones[:, 0:1],
                                            start=n + tt == 0, stop=n == KT - 1, skip_group_check=True)
            last.then_inc(ss_done, 1)
            turn_rms(L, 1)

            def start_pair(t, s, base):
                for u in range(2):
                    pe.wait_ge(bank_free[(t + u) % 4], nth(L, LAYER_TILES // 4, (t + u) // 4))
                tile_pair((ps[t % 4][:, :], ps[t % 4 + 1][:, :]), s, (a_hi, a_lo),
                          lambda kt: pe.wait_ge(xm_split, base + kt + 1))

            def qk_sums(r):
                pe.wait_ge(qn_sq, r + 1)
                if r == AT:
                    pe.wait_ge(qn_ms, 1)
                c = 8 * (r % AT)
                for tt in range(TT):
                    last = nc.tensor.matmul(ps[6][:, c + 2 * tt:c + 2 * tt + 2], g[:, r % 2, tt * P:(tt + 1) * P],
                                            half[:, 0:P:HD], start=True, stop=True)
                last.then_inc(qn_ss, 1)

            def qk_turn(r):
                pe.wait_ge(qn_spread, r + 1)
                if r >= 2:
                    pe.wait_ge(qk_normed, r - 1)
                for tt in range(TT):
                    last = nc.tensor.transpose(ps[4 + r % 2][:, tt * P:(tt + 1) * P],
                                               g[:, 2 + r % AT, tt * P:(tt + 1) * P], ident)
                last.then_inc(qn_turned, 1)

            for j in range(C_OUT):
                s, t = j % 2, 2 * j
                pe.wait_ge(w_lo_ready, nth(L, LAYER_BLOCKS, j))
                if j == 0:
                    start_pair(0, 0, 0)
                for u in range(2):
                    if C_VA <= j < C_IF or C_VM <= j < C_OG:
                        token_tile(L, t + u, s, [(2 * u, 0), (2 * u + 1, 256)], 0, 256)
                    elif j == C_IF:
                        tile(L, t + u, s, KT, u * MH, a_hi, a_lo, m=MH)
                    elif j > 0:
                        tile(L, t + u, s, KT, u * P, a_hi, a_lo)
                    if 1 <= t + u <= 8:
                        qk_sums(t + u - 1)
                    for first in (AT + 1, 2 * AT + 1):
                        if t + u - first in (0, 1):
                            for e in range(2):
                                qk_turn(first - AT - 1 + 2 * (t + u - first) + e)
                    h, part = divmod(t + u - HEAD2_SLOT, 2)
                    if part == 1 and 0 <= h < HEADS:
                        transposes(L, h)
                    if part == 0 and 1 <= h <= HEADS:
                        if h == 1:
                            pe.wait_ge(v2_ready, 1)
                        values(L, h - 1)
                    if part == 0 and 0 <= h < HEADS:
                        if h == 0:
                            pe.wait_ge(qk_normed, 2 * AT)
                        scores(L, h)

            pe.wait_ge(m_exp, 1)
            pe.wait_ge(m_rows, 1)
            for e, rows in enumerate((row_a, row_e)):
                for tt in range(TT):
                    c = MH * (TT * e + tt)
                    last = nc.tensor.transpose(ps[4][:, c:c + MH], rows[:, tt * P:(tt + 1) * P], ident[0:MH, 0:MH])
            last.then_inc(a_turned, 1)

            def m_start(h):
                if h > 0:
                    pe.wait_ge(m_gap, h)
                nc.tensor.matmul(ps[7][:, :], sel[:, h * P:(h + 1) * P], row_g, start=True, stop=True).then_inc(m_bc, 1)
                if h > 0:
                    pe.wait_ge(m_probs, h)
                for i in range(TT):
                    last = nc.tensor.matmul(key_bank[i], mk[:, h, i * P:(i + 1) * P], mq[:, h, i * P:],
                                            start=True, stop=True)
                last.then_inc(m_scores, 1)

            def m_turn(h):
                pe.wait_ge(m_spread, h + 1)
                for tt in range(TT):
                    last = nc.tensor.transpose(ps[2 + h % 2][:, tt * P:(tt + 1) * P],
                                               k[:, h % 2, tt * P:(tt + 1) * P], ident)
                last.then_inc(m_turned, 1)

            for b in range(4):
                pe.wait_ge(bank_free[b], nth(L, LAYER_TILES // 4, (2 * C_OUT - b + 3) // 4))
            pe.wait_ge(head_copied, nth(L, HEADS, HEADS - 1))
            pe.wait_ge(a_cols, 1)
            pe.wait_ge(mc_silu, 2 * MH)
            pe.wait_ge(mv_ready, 1)
            m_start(0)
            for h in range(MH):
                pe.wait_ge(m_probs, h + 1)
                if h >= 2:
                    pe.wait_ge(m_split, h - 1)
                for i in range(TT):
                    nc.tensor.matmul(ps[h % 2][:, i * P:], mv[:, i, h * P:(h + 1) * P], pt[:, TRT[i]:TRT[i + 1]],
                                     start=i == 0, stop=i == TT - 1)
                cols = ps[2 + h % 2]
                for i in range(TT):
                    for e in range(i + 1):
                        last = nc.tensor.matmul(cols[:, i:i + 1], pt[:, TRT[e] + (i - e) * P:TRT[e] + (i - e + 1) * P],
                                                ones[:, 0:1], start=e == 0, stop=e == i)
                last.then_inc(m_num, 1)
                if h + 1 < MH:
                    m_start(h + 1)
                pe.wait_ge(m_sq, h + 1)
                for tt in range(TT):
                    last = nc.tensor.matmul(cols[:, TT + tt:TT + tt + 1], g[:, 6 + h % 2, tt * P:(tt + 1) * P],
                                            ones[:, 0:1], start=True, stop=True)
                last.then_inc(m_ss, 1)
                if h > 0:
                    m_turn(h - 1)
            m_turn(MH - 1)

            pe.wait_ge(m_split, MH - 1 + 1)
            pe.wait_ge(y_split, nth(L, AT, AT - 1))
            for j in range(C_OUT, C_FF):
                pe.wait_ge(w_lo_ready, nth(L, LAYER_BLOCKS, j))
                for u in range(2):
                    t = 2 * j + u
                    pe.wait_ge(bank_free[t % 4], nth(L, LAYER_TILES // 4, t // 4))
                    product(ps[t % 4][:, :], j % 2, KT, KT, u * P, P,
                            lambda kt: y_hi[:, kt, :] if kt < AT else a_hi[:, kt - AT, :],
                            lambda kt: y_lo[:, kt, :] if kt < AT else a_lo[:, kt - AT, :])
            sum_squares(L, 2)
            turn_rms(L, 2)
            j, hid = C_FF, 0
            for nt in FF_TILES:
                for b in range(nt):
                    pe.wait_ge(w_lo_ready, nth(L, LAYER_BLOCKS, j))
                    if j == C_FF:
                        start_pair(2 * j, j % 2, KT)
                        j += 1
                        continue
                    for u in range(2):
                        tile(L, 2 * j + u, j % 2, KT, u * P, a_hi, a_lo)
                    j += 1
                for b in range(4):
                    pe.wait_ge(w_lo_ready, nth(L, LAYER_BLOCKS, j))
                    for u in range(2):
                        ready = None
                        if b + u == 0:
                            def ready(kt):
                                pe.wait_ge(h_split, nth(L, 8 * CHUNKS, hid + kt))
                        tile(L, 2 * j + u, j % 2, KT, u * P, b_hi, b_lo, depth=nt, ready=ready)
                    j += 1
                hid += nt

        @block.scalar
        def _(act):
            def w_split(L, n, at=0):
                act.wait_ge(w_loaded[n % 2], nth(L, LAYER_BLOCKS // 2, at * 4 + n // 2, 16))
                nc.scalar.activation(w_hi[:, n % 2, :], w_raw[:, n % 2, :], ACT.Copy).then_inc(w_hi_ready, 1)

            def x_parts(n, gain):
                nc.scalar.activation(a_hi[:, n, :], x[:, n, :], ACT.Copy, scale=gain).then_inc(x_hi, 1)
                nc.scalar.activation(g[:, n % 2, :], x[:, n, :], ACT.Square).then_inc(x_sq, 1)

            def root(L, which):
                act.wait_ge(ms_ready, nth(L, 2, which))
                nc.scalar.activation(rms_col[:, 8:12], rms_col[:, 4:8], ACT.Sqrt).then_inc(root_ready, 1)

            def exps(L, h):
                act.wait_ge(masked, nth(L, HEADS, h))
                for i in range(TT):
                    nc.scalar.activation(pr[:, TRI[i]:TRI[i + 1]], pr[:, TRI[i]:TRI[i + 1]], ACT.Exp,
                                         bias=peak[:, 4 + i:5 + i], accum_out=peak[:, 8 + i:9 + i])
                act.drain().then_inc(exps_done, 1)

            def turned(L, h):
                act.wait_ge(probs_turned, nth(L, HEADS, h))
                nc.scalar.activation(pt[:, TRT[0]:TRT[1]], ps[4][:, :], ACT.Copy)
                nc.scalar.activation(pt[:, TRT[1]:TRT[2]], ps[5][:, 0:384], ACT.Copy)
                nc.scalar.activation(pt[:, TRT[3]:TRT[4]], ps[5][:, 384:512], ACT.Copy)
                nc.scalar.activation(pt[:, TRT[2]:TRT[3]], ps[6][:, 0:256], ACT.Copy)
                act.drain().then_inc(pt_ready, 1)

            def head_out(L, h):
                act.wait_ge(head_done, nth(L, HEADS, h))
                rows = slice(HD * (h % 2), HD * (h % 2) + HD)
                nc.scalar.activation(q[rows, h // 2, :], ps[7][rows, :], ACT.Copy).then_inc(head_copied, 1)

            def y_high(L, i):
                act.wait_ge(head_copied, nth(L, HEADS, 2 * i + 1))
                nc.scalar.activation(y_hi[:, i, :], q[:, i, :], ACT.Copy).then_inc(y_hi_ready, 1)

            act.dma_start(sp[:, :], params).then_inc(params_loaded, 16)
            act.wait_ge(params_loaded, 16)
            nc.scalar.activation(cs[:, :], sp[:, SP_C:SP_C + KT], ACT.Silu).then_inc(c_silu, 1)
            for dst, src in ((kc[:, :], consts), (cs_rope[:, :, :], rope), (bias[:, 0:P], tri_bias)):
                act.dma_start(dst, src).then_inc(setup_loaded, 16)
            w_split(0, 0)
            for n in range(KT):
                if n % 4 == 0:
                    act.wait_ge(x_loaded[n // 4], 16)
                if n >= 2:
                    act.wait_ge(sq_used, n - 1)
                x_parts(n, sp[:, SP_G0 + n:SP_G0 + n + 1])
            w_split(0, 1)

            def beside(L, s, t):
                b = t % 4
                if s in ROPE_SLOT:
                    r = ROPE_SLOT.index(s)
                    if r >= 2:
                        act.wait_ge(roped, nth(L, 11, r - 2))
                    nc.scalar.activation(g[:, 4 + r % 2, :], ps[b][:, :], ACT.Copy).then_inc(raw_ready, 1)
                    act.drain().then_inc(bank_free[b], 1)
                if s == 0:
                    act.wait_ge(x_split, nth(L, 2 * KT, KT - 1))
                    act.dma_start(lp[:, :], layer_params[bass.ds(L, 1)].rearrange("a p n -> p (a n)")
                                  ).then_inc(lp_loaded, 16)
                    root(L, 0)
                if 2 * B_V <= s < 2 * B_CONV:
                    if s == 2 * B_V:
                        act.wait_ge(rms_ready, nth(L, 2, 0))
                    col, u = (s - 2 * B_V) // 2 * 256, s % 2
                    for e in range(2):
                        last = nc.scalar.activation(v[:, 2 * u + e, col:col + 256], ps[b][:, 256 * e:256 * e + 256],
                                                    ACT.Copy, scale=rms_col[:, 2 * u + e:2 * u + e + 1])
                    last.then_inc(bank_free[b], 1)
                    if s == 2 * B_CONV - 1:
                        act.drain().then_inc(v_ready, 1)
                if 2 * B_CONV <= s < 2 * B_YCONV and (s - 2 * B_CONV) % 6 >= 4:
                    i = 2 * ((s - 2 * B_CONV) // 6) + s % 2
                    act.wait_ge(cy_ready, nth(L, AT, i))
                    nc.scalar.activation(y_hi[:, i, :], g[:, 6 + s % 2, :], ACT.Copy).then_inc(cy_hi, 1)
                h, part = divmod(s - HEAD_SLOT, 3)
                if part == 2 and 0 <= h < HEADS:
                    turned(L, h)
                if part == 0 and 1 <= h <= HEADS:
                    head_out(L, h - 1)
                if part == 0 and 0 <= h < HEADS:
                    exps(L, h)
                if s in Y_SLOT:
                    y_high(L, Y_SLOT.index(s))
                if 2 * B_G1 <= s < 2 * B_YATT:
                    i = s - 2 * B_G1
                    act.wait_ge(gate_ready, nth(L, 2 * KT, i))
                    nc.scalar.activation(g[:, i % 8, :], g[:, i % 8, :], ACT.Tanh, scale=0.5).then_inc(gate_tanh, 1)

            with act.Fori(0, LAYERS) as L:
                for j in range(B_MLP):
                    t0, t1 = first_tile(j), first_tile(j + 1)
                    for t in range(t0, t1):
                        act.wait_ge(tile_done, nth(L, LAYER_TILES, t))
                        if t == t1 - 1:
                            w_split(L, j + 2)
                        if j < B_YCONV or B_G1 <= j < B_YATT:
                            beside(L, 2 * j + t - t0, t)
                        elif j < B_G1:
                            n = t - first_tile(B_YCONV)
                            nc.scalar.activation(yc[:, n, :], ps[t % 4][:, :], ACT.Copy
                                                 ).then_inc(bank_free[t % 4], 1)
                            if n == KT - 1:
                                act.drain().then_inc(yc_ready, 1)
                            if (t - t0) % 2:
                                beside(L, 2 * j + (t - t0) // 2, t)
                        elif j < B_MIX:
                            n = t - first_tile(B_YATT)
                            act.wait_ge(merged_ready, nth(L, KT, n))
                            nc.scalar.activation(b_hi[:, n, :], g[:, n, :], ACT.Copy, scale=0.5).then_inc(merged_hi, 1)
                        else:
                            n = t - first_tile(B_MIX)
                            if n == 0:
                                act.wait_ge(lp_loaded, nth(L, 1, 0, 16))
                            act.wait_ge(x_ready, nth(L, 2 * KT, n))
                            x_parts(n, lp[:, LP_GMLP + n:LP_GMLP + n + 1])
                root(L, 1)

                def chunk(c, last):
                    for n in range(16):
                        act.wait_ge(tile_done, nth(L, LAYER_TILES, c * 16 + (first_tile(B_MLP) + n)))
                        if n % 2:
                            w_split(L, B_MLP + n // 2 + 2, c)
                        if n in (0, 9, 11):
                            p = (0, 9, 11).index(n)
                            act.wait_ge(ada_used, nth(L, 12, c * 3 + p))
                            act.dma_start(ada_w[:, :, :], ada[bass.ds(L * 12 + c * 3 + p, 1)].rearrange(
                                "a p (k n) -> p (a k) n", k=TT)).then_inc(ada_loaded, 16)
                        if n < 8:
                            act.wait_ge(h_ready, nth(L, 8 * CHUNKS, c * 8 + n))
                            nc.scalar.activation(b_hi[:, n, :], g[:, 6 + n % 2, :], ACT.Copy).then_inc(h_hi, 1)
                        elif last:
                            act.wait_ge(x_ready, nth(L, 2 * KT, n))
                            x_parts(n - 8, lp[:, LP_GNEXT + n - 8:LP_GNEXT + n - 7])

                with act.Fori(0, CHUNKS - 1) as c:
                    chunk(c, False)
                chunk(CHUNKS - 1, True)

            L = LAYERS
            second = [(bias[:, :], mult_bias), (tri, tri_mask), (sel, selectors)]
            for dst, src in second:
                act.dma_start(dst, src).then_inc(second_loaded, 16)
            root(L, 0)
            for n in range(KT):
                act.wait_ge(x_ready, nth(L, 2 * KT, n))
                nc.scalar.activation(g[:, n, :], x[:, n, :], ACT.Square).then_inc(x_sq, 1)
            root(L, 1)

            def modulated(base, shift):
                for n in range(KT):
                    act.wait_ge(xm_ready, base + n + 1)
                    nc.scalar.activation(a_hi[:, n, :], g[:, 4 + n % 2, :], ACT.Identity,
                                         bias=mod[:, shift + n:shift + n + 1]).then_inc(xm_hi, 1)

            modulated(0, 0)

            def silu_tanh(i):
                act.wait_ge(mc_ready, i + 1)
                if i > 0:
                    act.wait_ge(mc_silu, i)
                nc.scalar.activation(mt[:, :], g[:, 4 + i % 2, :], ACT.Tanh, scale=0.5
                                     ).then_inc(mc_tanh, 1)

            for j in range(C_OUT):
                for u in range(2):
                    t = 2 * j + u
                    b = t % 4
                    act.wait_ge(tile_done, nth(L, LAYER_TILES, t))
                    if u:
                        w_split(L, j + 2)
                    if j < C_VA:
                        if t >= 2:
                            act.wait_ge(qn_ss, t - 1)
                        dst = q[:, t, :] if t < AT else k[:, t - AT, :]
                        nc.scalar.activation(dst, ps[b][:, :], ACT.Copy)
                        nc.scalar.activation(g[:, t % 2, :], ps[b][:, :], ACT.Square).then_inc(qn_sq, 1)
                        act.drain().then_inc(bank_free[b], 1)
                    if t in (AT, 2 * AT):
                        act.wait_ge(qn_ms, t // AT)
                        nc.scalar.activation(qcol[:, 1, :], qcol[:, 0, :], ACT.Sqrt).then_inc(qn_root, 1)
                    if C_VA <= j < C_IF or C_VM <= j < C_OG:
                        first = C_VA if j < C_IF else C_VM
                        dst, col = (v, mv)[first == C_VM], (j - first) * 256
                        for e in range(2):
                            last = nc.scalar.activation(dst[:, 2 * u + e, col:col + 256],
                                                        ps[b][:, 256 * e:256 * e + 256], ACT.Copy)
                        last.then_inc(bank_free[b], 1)
                        if t == 2 * first + 3:
                            act.drain().then_inc((v2_ready, mv_ready)[first == C_VM], 1)
                    if C_QM <= j < C_VM:
                        i = t - 2 * C_QM
                        if i >= 2:
                            act.wait_ge(mc_silu, i - 1)
                        nc.scalar.activation(g[:, 4 + i % 2, :], ps[b][:, :], ACT.Identity,
                                             scale=sp[:, SP_WCONV + 24 + i:SP_WCONV + 25 + i],
                                             bias=sp[:, SP_BCONV + i:SP_BCONV + i + 1]).then_inc(mc_first, 1)
                        silu_tanh(i)
                    if C_OG <= j:
                        i = t - 2 * C_OG
                        nc.scalar.activation(og[i], ps[b][:, :], ACT.Tanh, scale=0.5).then_inc(bank_free[b], 1)
                        if i == MH - 1:
                            act.drain().then_inc(og_ready, 1)
                    if t == 2 * C_IF + 1:
                        act.wait_ge(f_ready, 1)
                        nc.scalar.activation(row_e, row_b, ACT.Abs)
                        act.drain()
                        nc.scalar.activation(row_e, row_e, ACT.Exp, scale=-1.0)
                        act.drain()
                        nc.scalar.activation(row_e, row_e, ACT.Ln, bias=1.0).then_inc(f_log, 1)
                    h, part = divmod(t - HEAD2_SLOT, 2)
                    if part == 1 and 0 <= h < HEADS:
                        turned(L, h)
                    if part == 0 and 1 <= h <= HEADS:
                        head_out(L, h - 1)
                        if h % 2 == 0:
                            y_high(L, h // 2 - 1)
                    if part == 0 and 0 <= h < HEADS:
                        exps(L, h)

            act.wait_ge(m_rows, 1)
            act.wait_ge(mc_silu, 2 * MH)
            nc.scalar.activation(row_e, row_b, ACT.Exp, scale=-1.0).then_inc(m_exp, 1)

            def m_high(h):
                act.wait_ge(m_out, h + 1)
                nc.scalar.activation(a_hi[:, h, :], g[:, 4 + h % 2, :], ACT.Copy, scale=0.5).then_inc(m_hi, 1)

            act.wait_ge(m_gap, 1)
            nc.scalar.activation(pr[:, :], pr[:, :], ACT.Exp, scale=-1.0).then_inc(m_decay, 1)
            for h in range(MH):
                act.wait_ge(m_num, h + 1)
                if h >= 2:
                    act.wait_ge(m_split, h - 1)
                nc.scalar.activation(g[:, 4 + h % 2, :], ps[h % 2][:, :], ACT.Copy)
                nc.scalar.activation(g[:, 6 + h % 2, :], ps[h % 2][:, :], ACT.Square).then_inc(m_sq, 1)
                if h + 1 < MH:
                    act.wait_ge(m_gap, h + 2)
                    nc.scalar.activation(pr[:, :], pr[:, :], ACT.Exp, scale=-1.0).then_inc(m_decay, 1)
                act.wait_ge(m_ms, h + 1)
                nc.scalar.activation(mcol[:, 2, :], mcol[:, 1, :], ACT.Sqrt).then_inc(m_root, 1)
                if h > 0:
                    m_high(h - 1)
            m_high(MH - 1)

            for j in range(C_OUT, C_FF):
                for u in range(2):
                    t = 2 * j + u
                    act.wait_ge(tile_done, nth(L, LAYER_TILES, t))
                    if u:
                        w_split(L, j + 2)
                    n = t - 2 * C_OUT
                    act.wait_ge(x_ready, nth(L, 2 * KT, KT + n))
                    nc.scalar.activation(g[:, n % 2, :], x[:, n, :], ACT.Square).then_inc(x_sq, 1)
            root(L, 2)
            modulated(KT, 3 * KT)
            j, hid = C_FF, 0
            for nt in FF_TILES:
                for b in range(nt + 4):
                    for u in range(2):
                        act.wait_ge(tile_done, nth(L, LAYER_TILES, 2 * j + u))
                        if u and j + 2 < SECOND_BLOCKS:
                            w_split(L, j + 2)
                        if b < nt and b % 2 == 0:
                            n = hid + b + u
                            if n >= 2:
                                act.wait_ge(h_ready, nth(L, 8 * CHUNKS, n - 2))
                            nc.scalar.activation(g[:, 4 + u, :], ps[(2 * j + u) % 4][:, :], ACT.Silu
                                                 ).then_inc(silu_done, 1)
                            act.drain().then_inc(bank_free[(2 * j + u) % 4], 1)
                        elif b < nt:
                            n = hid + b - 1 + u
                            act.wait_ge(h_ready, nth(L, 8 * CHUNKS, n))
                            nc.scalar.activation(b_hi[:, n - hid, :], g[:, 6 + u, :], ACT.Copy).then_inc(h_hi, 1)
                    j += 1
                hid += nt

        @block.vector
        def _(dve):
            def tt(out_, a, b_, op):
                return nc.vector.tensor_tensor(out_, a, b_, op)

            def take(L, t, out_, scale):
                dve.wait_ge(tile_done, nth(L, LAYER_TILES, t))
                tt(out_, ps[t % 4][:, :], scale, ALU.mult).then_inc(bank_free[t % 4], 1)

            def refine(y, root_, mean, tmp, out_sem=None):
                nc.vector.reciprocal(y, root_)
                dve.drain()
                tt(tmp, y, y, ALU.mult)
                dve.drain()
                tt(tmp, tmp, mean, ALU.mult)
                dve.drain()
                nc.vector.tensor_scalar(tmp, tmp, -0.5, 1.5, ALU.mult, ALU.add)
                dve.drain()
                last = tt(y, y, tmp, ALU.mult)
                if out_sem is not None:
                    last.then_inc(out_sem, 1)

            def norm(L, which):
                dve.wait_ge(ss_done, nth(L, 2, which))
                nc.vector.tensor_scalar(rms_col[:, 4:8], ps[6][:, 0:TT], 1.0 / D, EPS, ALU.mult, ALU.add
                                        ).then_inc(ms_ready, 1)
                dve.wait_ge(root_ready, nth(L, 2, which))
                refine(rms_col[:, 0:4], rms_col[:, 8:12], rms_col[:, 4:8], rms_col[:, 8:12])
                dve.drain()
                nc.vector.tensor_copy(g[:, 2, :].rearrange("p (t c) -> p t c", t=TT),
                                      rms_col[:, 0:TT].unsqueeze(2).to_broadcast([P, TT, P])).then_inc(rms_spread, 1)
                dve.wait_ge(rms_turned, nth(L, 2, which))
                nc.vector.tensor_copy(rms[:, :], ps[6][:, :]).then_inc(rms_ready, 1)
                dve.drain()

            def low(L, n, k_, gain):
                dve.wait_ge(x_hi, nth(L, 2 * KT, k_))
                nc.vector.scalar_tensor_tensor(a_lo[:, n, :], x[:, n, :], gain, f32(a_hi[:, n, :]), ALU.mult,
                                               ALU.subtract).then_inc(x_split, 1)
                squares(L, n, k_)

            def squares(L, n, k_):
                dve.drain()
                dve.wait_ge(x_sq, nth(L, 2 * KT, k_))
                if n == 0:
                    last = nc.vector.tensor_copy(acc, g[:, 0, :])
                else:
                    last = tt(acc, acc, g[:, n % 2, :], ALU.add)
                if n == KT - 1:
                    last.then_inc(sq_summed, 1)

            for b in range(4):
                nc.vector.memset(top[:, b:b + 1], 0.0).then_inc(bank_free[b], 1)
            nc.vector.memset(top[:, 4:5], 0.0).then_inc(ada_used, 1)
            nc.vector.memset(top[:, 5:6], 0.0).then_inc(ada_taken, 1)
            dve.wait_ge(params_loaded, 16)
            for n in range(KT):
                dve.wait_ge(x_loaded[n // 4], 16)
                dve.wait_ge(x_hi, n + 1)
                gain = sp[:, SP_G0 + n:SP_G0 + n + 1]
                nc.vector.scalar_tensor_tensor(a_lo[:, n, :], x[:, n, :], gain, f32(a_hi[:, n, :]), ALU.mult,
                                               ALU.subtract).then_inc(x_split, 1)
                dve.wait_ge(x_sq, n + 1)
                if n == 0:
                    last = nc.vector.tensor_copy(acc, g[:, 0, :])
                else:
                    last = tt(acc, acc, g[:, n % 2, :], ALU.add)
                last.then_inc(sq_used, 1)
                dve.drain()
            dve.wait_ge(setup_loaded, 16 * 3)
            nc.vector.memset(top[:, 6:7], 0.0).then_inc(sq_summed, 1)
            dve.wait_ge(c_silu, 1)

            rounds = [i for i in range(1, TT) for _ in range(TOPK // 8)]

            def mask_scores(L, h, scale):
                dve.wait_ge(scores_done, nth(L, HEADS, h))
                nc.vector.memset(nudge[:, :], 0.0)
                for i in range(TT):
                    nc.vector.tensor_tensor_reduce(out=pr[:, TRI[i]:TRI[i + 1]], in0=query_bank[i],
                                                   in1=bias[:, TRI[i]:TRI[i + 1]], scale=scale, scalar=-3.0e38,
                                                   op0=ALU.add, op1=ALU.max, accum_out=peak[:, i:i + 1])
                dve.drain()
                nc.vector.tensor_scalar(peak[:, 4:8], peak[:, 0:4], -1.0, None, ALU.mult).then_inc(masked, 1)

            def normalise(L, h):
                dve.wait_ge(exps_done, nth(L, HEADS, h))
                nc.vector.reciprocal(peak[:, 12:16], peak[:, 8:12])
                dve.drain()
                for i in range(TT):
                    last = nc.vector.tensor_scalar(pr[:, TRI[i]:TRI[i + 1]], pr[:, TRI[i]:TRI[i + 1]],
                                                   peak[:, 12 + i:13 + i], None, ALU.mult)
                dve.drain().then_inc(probs_ready, 1)

            def y_low(L, i):
                dve.wait_ge(y_hi_ready, nth(L, AT, i))
                tt(y_lo[:, i, :], q[:, i, :], f32(y_hi[:, i, :]), ALU.subtract).then_inc(y_split, 1)

            def gate_finish(L, i):
                dve.wait_ge(gate_tanh, nth(L, 2 * KT, i))
                if i == 0:
                    dve.wait_ge(yc_ready, nth(L, 1, 0))
                nc.vector.scalar_tensor_tensor(yc[:, i, :], g[:, i, :], 1.0, yc[:, i, :], ALU.add, ALU.mult)
                dve.drain()

            def convolve(L, s):
                pair, kind, e = (s - 2 * B_CONV) // 6, (s - 2 * B_CONV) % 6 // 2, s % 2
                i = 2 * pair + e
                first, second = g[:, 6 + e, :], g[:, 4 + e, :]
                if kind == 0:
                    take(L, s, first, rms[:, :])
                elif kind == 1:
                    take(L, s, second, rms[:, :])
                    dve.drain()
                    tt(first, first, second, ALU.mult)
                    dve.drain()
                    w = [lp[:, LP_CONV + 4 * tap + i:LP_CONV + 4 * tap + i + 1] for tap in range(3)]
                    nc.vector.tensor_scalar(second, first, w[2], None, ALU.mult)
                    for back in (1, 2):
                        dve.drain()
                        nc.vector.scalar_tensor_tensor(second[:, back:], first[:, 0:S - back], w[2 - back],
                                                       second[:, back:], ALU.mult, ALU.add)
                    dve.drain()
                else:
                    take(L, s, first, rms[:, :])
                    dve.drain()
                    tt(first, first, second, ALU.mult).then_inc(cy_ready, 1)
                    dve.wait_ge(cy_hi, nth(L, AT, i))
                    tt(y_lo[:, i, :], first, f32(y_hi[:, i, :]), ALU.subtract).then_inc(cy_split, 1)
                    dve.drain()

            def beside(L, s, t):
                if s == 0:
                    norm(L, 0)
                    for e in range(2):
                        tt(cs_tok[:, e, :], cs_rope[:, e, :], rms[:, :], ALU.mult)
                    dve.drain()
                for r, rs in enumerate(ROPE_SLOT):
                    if s == rs + 1:
                        dst = (iq[:, 0, :], iq[:, 1, :], ik[:, 0, :], *(q[:, i, :] for i in range(4)),
                               *(k[:, i, :] for i in range(4)))[r]
                        dve.wait_ge(raw_ready, nth(L, 11, r))
                        tt(dst, g[:, 4 + r % 2, :], cs_tok[:, 0, :], ALU.mult)
                        dve.wait_ge(rot_done, nth(L, 11, r))
                        tt(g[:, 7, :], ps[7][:, :], cs_tok[:, 1, :], ALU.mult)
                        dve.drain()
                        tt(dst, dst, g[:, 7, :], ALU.add).then_inc(roped, 1)
                if s == 3:
                    dve.wait_ge(tile_done, nth(L, LAYER_TILES, 3))
                    for i in range(TT):
                        last = nc.vector.tensor_scalar(iw[:, i, :], ps[3][:, IDX_HEADS * i:IDX_HEADS * (i + 1)],
                                                       rms_col[:, i:i + 1], (64 ** -0.5) * (IDX_HEADS ** -0.5),
                                                       ALU.mult, ALU.mult)
                    last.then_inc(bank_free[3], 1)
                if LOGIT_SLOT <= s < LOGIT_SLOT + IDX_HEADS:
                    h = s - LOGIT_SLOT
                    dve.drain()
                    dve.wait_ge(logits_done, nth(L, IDX_HEADS, h))
                    for i in range(1, TT):
                        to = (bias if h == 0 else pr)[:, TRI[i]:TRI[i + 1]]
                        last = nc.vector.tensor_scalar(to, query_bank[i], 0.0, iw[:, i, h:h + 1], ALU.max, ALU.mult)
                    last.then_inc(logits_used, 1)
                    dve.drain()
                    if h > 0:
                        tt(bias[:, TRI[1]:], bias[:, TRI[1]:], pr[:, TRI[1]:], ALU.add)
                        dve.drain()
                    if h == IDX_HEADS - 1:
                        for i in range(1, TT):
                            nc.vector.memset(bias[0:64, TRI[i + 1] - 64:TRI[i + 1]], OUTSIDE)
                        dve.drain()
                if TOPK_SLOT <= s and TOPK_STEPS * (s - TOPK_SLOT) < len(rounds):
                    done = TOPK_STEPS * (s - TOPK_SLOT)
                    for i in rounds[done:done + TOPK_STEPS]:
                        row = bias[:, TRI[i]:TRI[i + 1]]
                        nc.vector.max(top[:, :], row)
                        dve.drain()
                        nc.vector.match_replace(row, top[:, :], row, TAKEN)
                        dve.drain()
                    if done + TOPK_STEPS >= len(rounds):
                        left = bias[:, TRI[1]:]
                        nc.vector.tensor_scalar(left, left, 0.5 * (TAKEN + OUTSIDE), NEG, ALU.is_gt, ALU.mult)
                        dve.drain()
                if 2 * B_CONV <= s < 2 * B_YCONV:
                    if s == 2 * B_CONV:
                        dve.wait_ge(lp_loaded, nth(L, 1, 0, 16))
                    convolve(L, s)
                if 2 * B_G1 <= s < 2 * B_YATT:
                    i = s - 2 * B_G1
                    if 0 < i <= KT:
                        gate_finish(L, i - 1)
                    dve.wait_ge(tile_done, nth(L, LAYER_TILES, t))
                    tt(g[:, i % 8, :], ps[t % 4][:, :], rms[:, :], ALU.mult).then_inc(bank_free[t % 4], 1)
                    dve.drain().then_inc(gate_ready, 1)
                h, part = divmod(s - HEAD_SLOT, 3)
                if part == 0 and 0 <= h < HEADS:
                    mask_scores(L, h, HD ** -0.5)
                if part == 1 and 0 <= h < HEADS:
                    normalise(L, h)
                if s in Y_SLOT:
                    y_low(L, Y_SLOT.index(s))

            with dve.Fori(0, LAYERS) as L:
                for j in range(B_YATT):
                    t0, t1 = first_tile(j), first_tile(j + 1)
                    for u in range(2):
                        beside(L, 2 * j + u, t0 + u if t1 - t0 == 2 else t0 + 2 * u + 1)
                def merged_low(n):
                    dve.wait_ge(merged_hi, nth(L, KT, n))
                    nc.vector.scalar_tensor_tensor(b_lo[:, n, :], g[:, n, :], 0.5, f32(b_hi[:, n, :]), ALU.mult,
                                                   ALU.subtract).then_inc(merged_split, 1)

                for n in range(KT):
                    t = first_tile(B_YATT) + n
                    dve.wait_ge(gate_tanh, nth(L, 2 * KT, KT + n))
                    dve.wait_ge(tile_done, nth(L, LAYER_TILES, t))
                    nc.vector.scalar_tensor_tensor(g[:, n, :], g[:, n, :], 1.0, ps[t % 4][:, :], ALU.add, ALU.mult
                                                   ).then_inc(bank_free[t % 4], 1)
                    dve.drain()
                    tt(g[:, n, :], g[:, n, :], yc[:, n, :], ALU.add).then_inc(merged_ready, 1)
                    if n > 0:
                        merged_low(n - 1)
                merged_low(KT - 1)

                def x_add(t, n, done):
                    last = tt(x[:, n, :], x[:, n, :], ps[t % 4][:, :], ALU.add)
                    last.then_inc(bank_free[t % 4], 1)
                    if done:
                        dve.drain().then_inc(x_ready, 1)

                for n in range(KT):
                    t = first_tile(B_MIX) + n
                    dve.wait_ge(tile_done, nth(L, LAYER_TILES, t))
                    x_add(t, n, True)
                    if n > 0:
                        low(L, n - 1, KT + n - 1, lp[:, LP_GMLP + n - 1:LP_GMLP + n])
                low(L, KT - 1, 2 * KT - 1, lp[:, LP_GMLP + KT - 1:LP_GMLP + KT])
                norm(L, 1)

                def chunk(c, last_chunk):
                    def h_low(n):
                        dve.wait_ge(h_hi, nth(L, 8 * CHUNKS, c * 8 + n))
                        tt(b_lo[:, n, :], g[:, 6 + n % 2, :], f32(b_hi[:, n, :]), ALU.subtract).then_inc(h_split, 1)
                        dve.drain()

                    for n in range(8):
                        dve.wait_ge(tile_done, nth(L, LAYER_TILES, c * 16 + (first_tile(B_MLP) + n)))
                        t = g[:, 4 + n % 2, :]
                        tt(t, ps[n % 4][:, :], rms[:, :], ALU.mult).then_inc(bank_free[n % 4], 1)
                        dve.drain()
                        nc.vector.scalar_tensor_tensor(g[:, 6 + n % 2, :], t, 0.0, t, ALU.max, ALU.mult
                                                       ).then_inc(h_ready, 1)
                        if n > 0:
                            h_low(n - 1)
                    h_low(7)
                    for n in range(8, 16):
                        dve.wait_ge(tile_done, nth(L, LAYER_TILES, c * 16 + (first_tile(B_MLP) + n)))
                        x_add(n, n - 8, last_chunk)
                        if last_chunk and n > 8:
                            low(L, n - 9, KT + n - 1, lp[:, LP_GNEXT + n - 9:LP_GNEXT + n - 8])
                        p = (n - 8) // 2
                        if n % 2 == 0 and p < 3:
                            dve.drain()
                            dve.wait_ge(ada_loaded, nth(L, 12, c * 3 + p, 16))
                            tt(ada_p.rearrange("p (k n) -> p k n", k=KT),
                               ada_w[:, :, :].rearrange("p a (b n) -> p (a b) n", b=2),
                               cs[:, :].unsqueeze(2).to_broadcast([P, KT, 256]), ALU.mult).then_inc(ada_used, 1)
                            dve.drain()
                            if p > 0:
                                dve.wait_ge(ada_done, nth(L, 12, c * 3 + p - 1))
                            nc.vector.tensor_reduce(out=ada_s, in_=ada_p.rearrange("p (k n) -> p n k", k=KT),
                                                    axis=AX_X, op=ALU.add).then_inc(ada_summed, 1)
                        if n % 2 and 1 <= p <= 3:
                            p -= 1
                            dve.wait_ge(ada_done, nth(L, 12, c * 3 + p))
                            col = (L * 12 + c * 3 + p) * 2
                            tt(mod[:, bass.ds(col, 2)], ps[7][:, 0:2], sp[:, bass.ds(col + SP_BADA, 2)], ALU.add
                               ).then_inc(ada_taken, 1)

                with dve.Fori(0, CHUNKS - 1) as c:
                    chunk(c, False)
                chunk(CHUNKS - 1, True)
                low(L, KT - 1, 3 * KT - 1, lp[:, LP_GNEXT + KT - 1:LP_GNEXT + KT])

            L = LAYERS
            norm(L, 0)
            for n in range(KT):
                nc.vector.scalar_tensor_tensor(x[:, n, :], x[:, n, :], sp[:, SP_GFIN + n:SP_GFIN + n + 1], rms[:, :],
                                               ALU.mult, ALU.mult).then_inc(x_ready, 1)
            for e, (gain, scale) in enumerate(((SP_GMIX, KT), (SP_GFFN, 4 * KT))):
                nc.vector.scalar_tensor_tensor(gs[:, e * KT:(e + 1) * KT], mod[:, scale:scale + KT], 1.0,
                                               sp[:, gain:gain + KT], ALU.add, ALU.mult)
            dve.drain()
            norm(L, 1)

            def modulated(base, e, shift):
                def xm_low(n):
                    dve.wait_ge(xm_hi, base + n + 1)
                    nc.vector.scalar_tensor_tensor(a_lo[:, n, :], g[:, 4 + n % 2, :], mod[:, shift + n:shift + n + 1],
                                                   f32(a_hi[:, n, :]), ALU.add, ALU.subtract).then_inc(xm_split, 1)
                    dve.drain()

                for n in range(KT):
                    nc.vector.scalar_tensor_tensor(g[:, 4 + n % 2, :], x[:, n, :], gs[:, e * KT + n:e * KT + n + 1],
                                                   rms[:, :], ALU.mult, ALU.mult).then_inc(xm_ready, 1)
                    if n > 0:
                        xm_low(n - 1)
                xm_low(KT - 1)

            modulated(0, 0, 0)

            def qk_columns(e):
                dve.wait_ge(qn_ss, AT * (e + 1))
                nc.vector.tensor_scalar(qcol[:, 0, :], ps[6][:, 0:32], 1.0 / HD, EPS, ALU.mult, ALU.add).then_inc(qn_ms, 1)
                dve.wait_ge(qn_root, e + 1)
                refine(qcol[:, 2, :], qcol[:, 1, :], qcol[:, 0, :], qcol[:, 1, :])
                dve.drain()
                for r in range(AT):
                    nc.vector.tensor_copy(g[:, 2 + r, :].rearrange("p (t c) -> p t c", t=2 * TT),
                                          qcol[:, 2, 8 * r:8 * r + 8].unsqueeze(2).to_broadcast([P, 2 * TT, HD])
                                          ).then_inc(qn_spread, 1)

            def qk_norm(r):
                dst, gain = (q[:, r, :], SP_QG) if r < AT else (k[:, r - AT, :], SP_KG)
                dve.wait_ge(qn_turned, r + 1)
                nc.vector.scalar_tensor_tensor(dst, dst, sp[:, gain:gain + 1], ps[4 + r % 2][:, :], ALU.mult, ALU.mult
                                               ).then_inc(qk_normed, 1)

            for j in range(C_OUT):
                for u in range(2):
                    t = 2 * j + u
                    b = t % 4
                    if t in (AT, 2 * AT):
                        qk_columns(t // AT - 1)
                    for first in (AT + 1, 2 * AT + 1):
                        if t - first in (0, 1):
                            for e in range(2):
                                qk_norm(first - AT - 1 + 2 * (t - first) + e)
                            dve.drain()
                    if j == C_IF:
                        dve.wait_ge(tile_done, nth(L, LAYER_TILES, t))
                        row, col = (row_b, SP_BF) if u else (row_a, SP_BI)
                        nc.vector.tensor_scalar(row, ps[b][0:MH, :], sp[0:MH, col:col + 1], None, ALU.add
                                                ).then_inc(bank_free[b], 1)
                        dve.drain().then_inc(f_ready, 1) if u else dve.drain()
                    if t == 2 * C_IF + 2:
                        dve.wait_ge(f_log, 1)
                        nc.vector.scalar_tensor_tensor(row_g, row_b, 0.0, row_e, ALU.min, ALU.subtract)
                        dve.drain()
                        nc.vector.memset(row_e, 1.0)
                        dve.drain()
                        nc.vector.tensor_tensor_scan(row_b, row_e, row_g, 0.0, ALU.mult, ALU.add)
                        dve.drain()
                        tt(row_a, row_a, row_b, ALU.subtract)
                        dve.drain()
                        nc.vector.tensor_tensor_scan(row_g, row_a, row_a, 0.0, ALU.max, ALU.max)
                        dve.drain()
                        tt(row_b, row_b, row_g, ALU.add).then_inc(m_rows, 1)
                    h, part = divmod(t - HEAD2_SLOT, 2)
                    if part == 0 and 0 <= h < HEADS:
                        if h == 0:
                            dve.wait_ge(second_loaded, 48)
                        mask_scores(L, h, HD ** -0.5)
                    if C_QM <= j < C_VM:
                        i = t - 2 * C_QM
                        o = g[:, 4 + i % 2, :]
                        dve.wait_ge(mc_first, i + 1)
                        for back in (1, 2, 3):
                            w = SP_WCONV + 8 * (3 - back) + i
                            last = nc.vector.scalar_tensor_tensor(o[:, back:], ps[b][:, 0:S - back], sp[:, w:w + 1],
                                                                  o[:, back:], ALU.mult, ALU.add)
                            if back < 3:
                                dve.drain()
                        last.then_inc(bank_free[b], 1)
                        dve.drain().then_inc(mc_ready, 1)
                        dve.wait_ge(mc_tanh, i + 1)
                        dst = mq[:, i, :] if i < MH else mk[:, i - MH, :]
                        nc.vector.scalar_tensor_tensor(dst, mt[:, :], 1.0, o, ALU.add, ALU.mult
                                                       ).then_inc(mc_silu, 1)
                    if part == 0 and h >= 0 and 0 <= h < HEADS:
                        normalise(L, h)
                    if part == 0 and 2 <= h <= HEADS and h % 2 == 0:
                        y_low(L, h // 2 - 1)

            dve.wait_ge(a_turned, 1)
            nc.vector.tensor_copy(acol[:, :, :, :].rearrange("p e a b -> p (e a b)"), ps[4][:, 0:2 * TT * MH]
                                  ).then_inc(a_cols, 1)
            dve.drain()
            dve.wait_ge(og_ready, 1)

            def m_gaps(h):
                dve.wait_ge(m_bc, h + 1)
                for i in range(TT):
                    nc.vector.tensor_scalar(pr[:, TRT[i]:TRT[i + 1]], ps[7][:, i * P:], acol[:, 0, i, h:h + 1], 0.0,
                                            ALU.subtract, ALU.max)
                dve.drain().then_inc(m_gap, 1)

            def m_finish(h):
                num = g[:, 4 + h % 2, :]
                dve.wait_ge(m_turned, h + 1)
                nc.vector.scalar_tensor_tensor(num, num, sp[:, SP_MG + h:SP_MG + h + 1], ps[2 + h % 2][:, :],
                                               ALU.mult, ALU.mult)
                dve.drain()
                nc.vector.scalar_tensor_tensor(num, og[h], 1.0, num, ALU.add, ALU.mult).then_inc(m_out, 1)
                dve.wait_ge(m_hi, h + 1)
                nc.vector.scalar_tensor_tensor(a_lo[:, h, :], num, 0.5, f32(a_hi[:, h, :]), ALU.mult, ALU.subtract
                                               ).then_inc(m_split, 1)
                dve.drain()

            m_gaps(0)
            for h in range(MH):
                dve.wait_ge(m_decay, h + 1)
                dve.wait_ge(m_scores, h + 1)
                for i in range(TT):
                    nc.vector.scalar_tensor_tensor(pt[:, TRT[i]:TRT[i + 1]], key_bank[i], 0.25 * P ** -0.5,
                                                   pr[:, TRT[i]:TRT[i + 1]], ALU.mult, ALU.mult)
                dve.drain()
                for i in range(TT):
                    d = pt[:, TRT[i]:TRT[i] + P]
                    tt(d, d, tri, ALU.mult)
                dve.drain().then_inc(m_probs, 1)
                if h + 1 < MH:
                    m_gaps(h + 1)
                cols, den, ms = ps[2 + h % 2], mcol[:, 0, :], mcol[:, 1, :]
                dve.wait_ge(m_ss, h + 1)
                nc.vector.tensor_scalar(ms, cols[:, 0:TT], -1.0, None, ALU.mult)
                dve.drain()
                tt(den, ms, cols[:, 0:TT], ALU.max)
                dve.drain()
                tt(den, den, acol[:, 1, :, h], ALU.max)
                dve.drain()
                nc.vector.scalar_tensor_tensor(den, den, EPS, den, ALU.mult, ALU.mult)
                dve.drain()
                nc.vector.scalar_tensor_tensor(ms, cols[:, TT:2 * TT], 1.0 / P, den, ALU.mult, ALU.add).then_inc(m_ms, 1)
                dve.wait_ge(m_root, h + 1)
                refine(mcol[:, 3, :], mcol[:, 2, :], ms, mcol[:, 2, :])
                dve.drain()
                nc.vector.tensor_copy(k[:, h % 2, :].rearrange("p (t c) -> p t c", t=TT),
                                      mcol[:, 3, :].unsqueeze(2).to_broadcast([P, TT, P])).then_inc(m_spread, 1)
                if h > 0:
                    m_finish(h - 1)
            m_finish(MH - 1)

            for n in range(KT):
                t = 2 * C_OUT + n
                dve.wait_ge(tile_done, nth(L, LAYER_TILES, t))
                nc.vector.scalar_tensor_tensor(x[:, n, :], ps[t % 4][:, :], mod[:, 2 * KT + n:2 * KT + n + 1],
                                               x[:, n, :], ALU.mult, ALU.add).then_inc(bank_free[t % 4], 1)
                dve.drain().then_inc(x_ready, 1)
                if n > 0:
                    squares(L, n - 1, 2 * KT + n - 1)
            squares(L, KT - 1, 3 * KT - 1)
            norm(L, 2)
            modulated(KT, 1, 3 * KT)
            j, hid = C_FF, 0
            for nt in FF_TILES:
                def h_low(n):
                    dve.wait_ge(h_hi, nth(L, 8 * CHUNKS, n))
                    tt(b_lo[:, n - hid, :], g[:, 6 + n % 2, :], f32(b_hi[:, n - hid, :]), ALU.subtract
                       ).then_inc(h_split, 1)

                for b in range(nt):
                    if b % 2:
                        for u in range(2):
                            t, n = 2 * j + u, hid + b - 1 + u
                            dve.wait_ge(tile_done, nth(L, LAYER_TILES, t))
                            dve.wait_ge(silu_done, n + 1)
                            tt(g[:, 6 + u, :], ps[t % 4][:, :], g[:, 4 + u, :], ALU.mult).then_inc(bank_free[t % 4], 1)
                            dve.drain().then_inc(h_ready, 1)
                        for u in range(2):
                            h_low(hid + b - 1 + u)
                        dve.drain()
                    j += 1
                for n in range(KT):
                    t = 2 * j + n
                    dve.wait_ge(tile_done, nth(L, LAYER_TILES, t))
                    last = nc.vector.scalar_tensor_tensor(x[:, n, :], ps[t % 4][:, :],
                                                          mod[:, 5 * KT + n:5 * KT + n + 1], x[:, n, :],
                                                          ALU.mult, ALU.add)
                    last.then_inc(bank_free[t % 4], 1)
                    if nt == FF_TILES[-1]:
                        dve.drain().then_inc(x_final, 1)
                j += 4
                hid += nt


def rope_constants():
    half = HD // 8
    inv = (1.0 / (np.float32(500000.0) ** (np.arange(0, 2 * half, 2, dtype=np.float32) / np.float32(2 * half)))).astype(np.float32)
    ang = np.arange(S, dtype=np.float32)[:, None] * inv[None, :]
    c, s = np.ones((P, 2, S), np.float32), None
    c[:, 1, :] = 0.0
    for f in range(P):
        if f % HD < 2 * half:
            c[f, 0, :] = np.cos(ang[:, f % half])
            c[f, 1, :] = np.sin(ang[:, f % half])
    return c


def constant_matrices():
    half = HD // 8
    m = np.zeros((P, K_N), np.float32)
    for base in (0, HD):
        for i in range(half):
            m[base + half + i, K_ROT + base + i] = -1.0
            m[base + i, K_ROT + base + half + i] = 1.0
        m[base:base + HD, K_HALF + base:K_HALF + base + HD] = 1.0
    m[:, K_ID:K_ID + P] = np.eye(P, dtype=np.float32)
    m[:, K_ONES:K_ONES + P] = 1.0
    return m


def key_biases():
    t = np.arange(P)
    near = np.where(t[None, :] < (t[:, None] // 64 + 1) * 64, 0.0, NEG).astype(np.float32)
    many = np.zeros((P, TRI[TT]), np.float32)
    for i in range(TT):
        rel = (i * P + t[:, None]) - np.arange((i + 1) * P)[None, :]
        n = sum(((rel >= 0) & (rel % d == 0) & (rel <= w)).astype(np.float32) for w, d in ((128, 1), (512, 4), (2048, 16)))
        many[:, TRI[i]:TRI[i + 1]] = np.where(n > 0, 8.0 * np.log(np.maximum(n, 1.0)), NEG)
    return near, many


def kernel(**inputs):
    import concourse.bacc as bacc
    from concourse.bass_utils import run_bass_kernel_spmd

    a = {n: np.asarray(v) for n, v in inputs.items()}

    def blocks(w):
        depth, cols = w.shape
        wide = BLK * P // depth if depth in (512, 1024) else 256
        n = -(-cols // wide)
        full = np.zeros((max(depth, 512) if depth == 512 else 1024, n * wide), w.dtype)
        full[:depth, :cols] = w
        return full.reshape(-1, P, n, wide).transpose(2, 1, 0, 3).reshape(n, P, BLK)

    parts = []
    for l in range(LAYERS):
        w = a["w_in"][l]
        cut = np.split(w, np.cumsum([512, 512, 512, 256, 64, 4, 512, 512, 512, 1024]), axis=1)
        wq, wk, wv, wiq, wik, wiw, wb, wc, wh, wg0, wg1 = cut
        parts += [blocks(wiq), blocks(np.concatenate([wik, wik, wiw], axis=1)), blocks(wq), blocks(wk), blocks(wv)]
        for pair in range(2):
            parts += [blocks(m[:, 256 * pair:256 * pair + 256]) for m in (wc, wh, wb)]
        parts += [blocks(a["w_conv_out"][l]), blocks(wg1), blocks(wg0), blocks(a["w_attn_out"][l]),
                  blocks(a["w_mix_out"][l])]
        for c in range(CHUNKS):
            parts += [blocks(a["w_mlp_up"][l][:, 1024 * c:1024 * c + 1024]),
                      blocks(a["w_mlp_down"][l][1024 * c:1024 * c + 1024])]
    w = a["w_in_2"][0]
    parts += [blocks(w[:, c:d]) for c, d in ((0, 512), (512, 1024), (1024, 1536), (3584, 3592), (1536, 2048), (2048, 2560),
                                             (2560, 3072), (3072, 3584))]
    parts += [blocks(a["w_out_2"][0])]
    at = 0
    for nt in FF_TILES:
        for i in range(0, nt, 2):
            parts += [blocks(a[m][0][:, at + P * i:at + P * i + 256]) for m in ("w_gate_2", "w_up_2")]
        parts += [blocks(a["w_down_2"][0][at:at + P * nt])]
        at += P * nt
    weights = np.concatenate(parts)
    assert weights.shape[0] == BLOCKS

    def cols(vec):
        return vec.reshape(-1, P).T

    layer_params = np.stack([np.concatenate(
        [cols(a["norm_mlp"][l])] + [cols(a["conv_w"][l][t]) for t in range(3)]
        + [cols(a["norm_mix"][l + 1] if l + 1 < LAYERS else a["norm_final"])], axis=1) for l in range(LAYERS)])

    def rows4(vec):
        full = np.zeros((P, 1), vec.dtype)
        full[:MH, 0] = vec
        return full

    params = np.concatenate(
        [cols(a["g_mix_2"][0]), cols(a["g_ffn_2"][0]), cols(a["norm_final"]), cols(a["b_conv_2"][0])]
        + [cols(a["w_conv_2"][0][t]) for t in range(4)]
        + [np.tile(a["q_norm_g_2"][0], 2)[:, None], np.tile(a["k_norm_g_2"][0], 2)[:, None],
           cols(a["mlstm_norm_g_2"][0]), cols(a["b_ada_2"][0]), cols(a["c_2"][0]),
           rows4(a["b_igate_2"][0]), rows4(a["b_fgate_2"][0]), cols(a["norm_mix"][0])], axis=1)
    near, many = key_biases()
    t = np.arange(P)
    selectors = np.zeros((MH, MH * P), np.float32)
    for h in range(MH):
        selectors[h, h * P:(h + 1) * P] = 1.0
    arrays = {
        "weights": weights,
        "ada": blocks(a["w_ada_2"][0]),
        "consts": constant_matrices(),
        "rope": rope_constants(),
        "tri_bias": near,
        "mult_bias": many,
        "tri_mask": (t[:, None] <= t[None, :]).astype(np.float32),
        "layer_params": layer_params,
        "params": params,
        "x_in": a["x"][0].T,
        "selectors": selectors,
    }
    arrays = {f"in_{n}": np.ascontiguousarray(v) for n, v in arrays.items()}
    nc = bacc.Bacc("TRN2", target_bir_lowering=False, num_devices=1)
    args = [nc.dram_tensor(n, v.shape, mybir.dt.from_np(v.dtype), kind="ExternalInput").ap() for n, v in arrays.items()]
    args.append(nc.dram_tensor("out", (D, S), F32, kind="ExternalOutput").ap())
    two_blocks(nc, *args)
    r = run_bass_kernel_spmd(nc, [arrays], core_ids=[0])
    return np.ascontiguousarray(r.results[0]["out"].T)[None]
```

```python
import numpy as np
from contextlib import ExitStack

import concourse.bass as bass
from concourse import mybir

F32 = mybir.dt.float32
F32R = mybir.dt.float32r
ALU = mybir.AluOpType
ACT = mybir.ActivationFunctionType
AX_X = mybir.AxisListType.X

P = 128
S = 512
D = 1024
KT = D // P
LAYERS = 2
HEADS, HD = 8, 64
IDX_HEADS = 4
TOPK = min(256, S // 4)
ATT = HEADS * HD
AT = ATT // P
TT = S // P
MH = 4
CHUNKS = 4
FF_TILES = [8, 8, 6]
EPS = 1e-6
NEG = -1.0e30
OUTSIDE = -2.0e38
TAKEN = -3.0e38

BLK = 2048
B_IQ, B_IK, B_Q, B_K, B_V, B_CONV, B_YCONV, B_G1, B_G0, B_YATT, B_MIX, B_MLP = 0, 1, 2, 4, 6, 8, 14, 16, 20, 24, 26, 30
LAYER_BLOCKS = B_MLP + 8 * CHUNKS
C_QA, C_KA, C_VA, C_IF, C_QM, C_KM, C_VM, C_OG, C_OUT, C_FF = 0, 2, 4, 6, 7, 9, 11, 13, 15, 19
HEAD2_SLOT = 2 * C_IF
SECOND_BLOCKS = C_FF + sum(n + 4 for n in FF_TILES)
BLOCKS = LAYERS * LAYER_BLOCKS + SECOND_BLOCKS


def first_tile(j):
    return 2 * j + 2 * min(max(j - B_YCONV, 0), 2) + 2 * min(max(j - B_YATT, 0), 2)


LAYER_TILES = first_tile(LAYER_BLOCKS)
TRI = [0, 128, 384, 768, 1280]
TRT = [0, 512, 896, 1152, 1280]

ROPE_SLOT = [0, 1, 2, 4, 5, 6, 7, 8, 9, 10, 11]
ROPE_GROUPS = ((0, 3), (3, 7), (7, 11))
ROTARY = HD // 4
ROPES = len(ROPE_SLOT)
LOGIT_SLOT = 7
TOPK_SLOT = [s for s in range(11, 30) if s not in (18, 19, 25)]
HEAD_SLOT = 30
Y_SLOT = [34, 38, 42, 46]

K_ROT, K_ID, K_ONES, K_HALF, K_N = 0, 128, 256, 384, 512
LP_GMLP, LP_CONV, LP_GNEXT, LP_N = 0, 8, 20, 28
SP_GMIX, SP_GFFN, SP_GFIN, SP_BCONV, SP_WCONV, SP_QG, SP_KG, SP_MG, SP_BADA, SP_C, SP_BI, SP_BF, SP_G0, SP_N = (
    0, 8, 16, 24, 32, 64, 65, 66, 70, 118, 126, 127, 128, 136)


def nth(layer, per_layer, k, step=1):
    return layer * (per_layer * step) + k * step + step


def two_blocks(nc, weights, ada, consts, rope, tri_bias, mult_bias, tri_mask, layer_params, params, x_in, selectors, out):
    with ExitStack() as ctx:
        def sb(name, shape, dt=F32, scope=ctx):
            return scope.enter_context(nc.sbuf_tensor(name, shape, dt))

        x = sb("x", [P, KT, S])
        a_hi = sb("a_hi", [P, KT, S], F32R)
        a_lo = sb("a_lo", [P, KT, S], F32R)
        w_raw = sb("w_raw", [P, 2, BLK])
        w_hi = sb("w_hi", [P, 2, BLK], F32R)
        w_lo = sb("w_lo", [P, 2, BLK], F32R)
        v = sb("v", [P, TT, ATT])
        y_hi = sb("y_hi", [P, AT, S], F32R)
        y_lo = sb("y_lo", [P, AT, S], F32R)
        yc = sb("yc", [P, KT, S])
        g = sb("g", [P, KT, S])
        bias = sb("bias", [P, TRI[TT]])
        cs_rope = sb("cs_rope", [P, 2, S])
        mrows = sb("mrows", [MH, 2, S])
        iw_rows = sb("iw_rows", [IDX_HEADS, S])
        kc = sb("kc", [P, K_N])
        rms = sb("rms", [P, S])
        rms_col = sb("rms_col", [P, 3 * TT])
        lp = sb("lp", [P, LP_N])
        sp = sb("sp", [P, SP_N])
        mod = sb("mod", [P, 48])
        gs = sb("gs", [P, 2 * KT])
        cs = sb("cs", [P, KT])
        iw = sb("iw", [P, TT, IDX_HEADS])
        top = sb("top", [P, 3, 8])
        peak = sb("peak", [P, 3 * TT])
        warm = sb("warm", [P, 1])
        nudge = sb("nudge", [P, 1])
        acol = sb("acol", [P, 2, TT, MH])
        qcol = sb("qcol", [P, 3, 32])
        mcol = sb("mcol", [P, 4, MH, TT])
        mt = sb("mt", [P, S])
        one = ExitStack()
        q = sb("q", [P, AT, S], F32, one)
        k = sb("k", [P, AT, S], F32, one)
        iq = sb("iq", [P, 2, S], F32, one)
        ik = sb("ik", [P, 1, S], F32, one)
        pr = sb("pr", [P, TRI[TT]], F32, one)
        pt = sb("pt", [P, TRT[TT]], F32, one)
        one.close()
        two = ExitStack()
        b_hi = sb("b_hi", [P, KT, S], F32R, two)
        b_lo = sb("b_lo", [P, KT, S], F32R, two)
        two.close()
        one.enter_context(nc.sbuf_tensor("region_1", [P, 2 * KT * S], F32))
        ctx.enter_context(one)

        ps = [ctx.enter_context(nc.psum_tensor(f"ps{b}", [P, S], F32)) for b in range(8)]

        def sem(name):
            return ctx.enter_context(nc.semaphore(name))

        params_loaded = sem("params_loaded")
        x_loaded = [sem(f"x_loaded{e}") for e in range(2)]
        setup_loaded = sem("setup_loaded")
        w_loaded = [sem(f"w_loaded{s}") for s in range(2)]
        w_hi_ready = sem("w_hi_ready")
        w_lo_ready = sem("w_lo_ready")
        tile_done = sem("tile_done")
        bank_free = [sem(f"bank_free{b}") for b in range(4)]
        lp_loaded = sem("lp_loaded")
        x_ready = sem("x_ready")
        x_hi = sem("x_hi")
        x_sq = sem("x_sq")
        x_split = sem("x_split")
        sq_used = sem("sq_used")
        sq_summed = sem("sq_summed")
        gained_summed = sem("gained_summed")
        ss_done = sem("ss_done")
        ms_ready = sem("ms_ready")
        root_ready = sem("root_ready")
        rms_spread = sem("rms_spread")
        rms_turned = sem("rms_turned")
        rms_ready = sem("rms_ready")
        qk_ready = sem("qk_ready")
        rope_gathered = [sem(f"rope_gathered{e}") for e in range(3)]
        rot_done = sem("rot_done")
        rope_turned = sem("rope_turned")
        roped = [sem(f"roped{e}") for e in range(3)]
        iw_ready = sem("iw_ready")
        iw_turned = sem("iw_turned")
        logits_done = sem("logits_done")
        logits_used = sem("logits_used")
        v_ready = sem("v_ready")
        cy_ready = sem("cy_ready")
        cy_hi = sem("cy_hi")
        cy_split = sem("cy_split")
        gate_ready = sem("gate_ready")
        gate_tanh = sem("gate_tanh")
        yc_ready = sem("yc_ready")
        scores_done = sem("scores_done")
        masked = sem("masked")
        exps_done = sem("exps_done")
        probs_ready = sem("probs_ready")
        probs_turned = sem("probs_turned")
        pt_ready = sem("pt_ready")
        head_done = sem("head_done")
        head_copied = sem("head_copied")
        y_hi_ready = sem("y_hi_ready")
        y_split = sem("y_split")
        merged_ready = sem("merged_ready")
        merged_hi = sem("merged_hi")
        merged_split = sem("merged_split")
        h_ready = sem("h_ready")
        h_hi = sem("h_hi")
        h_split = sem("h_split")
        ada_loaded = sem("ada_loaded")
        ada_used = sem("ada_used")
        ada_summed = sem("ada_summed")
        ada_done = sem("ada_done")
        ada_taken = sem("ada_taken")
        c_silu = sem("c_silu")
        second_loaded = sem("second_loaded")
        xm_ready = sem("xm_ready")
        xm_hi = sem("xm_hi")
        xm_split = sem("xm_split")
        qn_sq = sem("qn_sq")
        qn_ss = sem("qn_ss")
        qn_ms = sem("qn_ms")
        qn_root = sem("qn_root")
        qn_spread = sem("qn_spread")
        qn_turned = sem("qn_turned")
        qk_normed = sem("qk_normed")
        v2_ready = sem("v2_ready")
        mc_first = sem("mc_first")
        mc_ready = sem("mc_ready")
        mc_tanh = sem("mc_tanh")
        mc_silu = sem("mc_silu")
        mv_ready = sem("mv_ready")
        og_ready = sem("og_ready")
        f_ready = sem("f_ready")
        f_log = sem("f_log")
        m_rows = sem("m_rows")
        m_exp = sem("m_exp")
        a_turned = sem("a_turned")
        a_cols = sem("a_cols")
        m_bc = sem("m_bc")
        m_scores = sem("m_scores")
        m_gap = sem("m_gap")
        m_decay = sem("m_decay")
        m_probs = sem("m_probs")
        m_num = sem("m_num")
        m_sq = sem("m_sq")
        m_ss = sem("m_ss")
        m_ms = sem("m_ms")
        m_root = sem("m_root")
        m_spread = sem("m_spread")
        m_turned = sem("m_turned")
        m_out = sem("m_out")
        m_hi = sem("m_hi")
        m_split = sem("m_split")
        silu_done = sem("silu_done")
        x_final = sem("x_final")
        stored = sem("stored")

        block = ctx.enter_context(nc.Block())

        def wcols(t, slot, deep, kt, c0, n):
            return t[:, slot, :].rearrange("p (k c) -> p k c", k=deep)[:, kt, c0:c0 + n]

        rot_m, ident, ones, half = (kc[:, c:c + P] for c in (K_ROT, K_ID, K_ONES, K_HALF))
        acc = yc[:, KT - 1, :]
        ada_w = v
        ada_p = yc[:, 0:4, :].rearrange("p a b -> p (a b)")
        ada_s = yc[:, 4, 0:256]
        mq, mk, mv = yc[:, 4:8, :], g[:, 0:4, :], yc[:, 0:4, :]
        og = [iq[:, 0, :], iq[:, 1, :], ik[:, 0, :], cs_rope[:, 0, :]]
        tri = cs_rope[:, 1, 0:P]
        sel = mrows[:, 0, :]
        row_a, row_b, row_e, row_g = g[0:MH, 6, :], g[0:MH, 7, :], mrows[:, 1, :], rms[0:MH, :]
        key_bank = (ps[4][:, :], ps[5][:, 0:384], ps[6][:, 0:256], ps[5][:, 384:512])
        query_bank = (ps[5][:, 384:512], ps[6][:, 0:256], ps[5][:, 0:384], ps[4][:, :])

        m_bank, m_pr = (ps[7][:, :], ps[2][:, :]), (pr, bias)
        m_cols = ps[3][:, 0:2 * MH * TT].rearrange("p (h e t) -> p h e t", h=MH, e=2)

        qk_tiles = [q[:, i, :] for i in range(AT)] + [k[:, i, :] for i in range(AT)]
        rope_tiles = [iq[:, 0, :], iq[:, 1, :], ik[:, 0, :]] + qk_tiles
        gained_sq = qk_tiles

        rope_group = [g[:, 4, :], g[:, 5, :], g[:, 6, :]]

        def rotary(r, e):
            group = [r < end for _, end in ROPE_GROUPS].index(True)
            at = ROTARY * (2 * (r - ROPE_GROUPS[group][0]) + e)
            return rope_tiles[r][HD * e:HD * e + ROTARY, :], rope_group[group][at:at + ROTARY, :]

        def f32(ap):
            return ap.bitcast(F32)

        @block.sync
        def _(sync):
            sync.dma_start(w_raw[:, 0, :], weights[0]).then_inc(w_loaded[0], 16)
            for e in range(2):
                sync.dma_start(x[:, 4 * e:4 * e + 4, :], x_in[4 * e * P:4 * (e + 1) * P].rearrange("(n p) t -> p n t", p=P)
                               ).then_inc(x_loaded[e], 16)
            sync.dma_start(w_raw[:, 1, :], weights[1]).then_inc(w_loaded[1], 16)
            with sync.Fori(1, BLOCKS // 2) as pair:
                for s in range(2):
                    sync.wait_ge(w_lo_ready, pair * 2 + (s - 1))
                    sync.dma_start(w_raw[:, s, :], weights[bass.ds(pair * 2 + s, 1)].rearrange("a p n -> p (a n)")
                                   ).then_inc(w_loaded[s], 16)
            sync.wait_ge(w_lo_ready, BLOCKS - 2)
            sync.dma_start(w_raw[:, 0, :], weights[BLOCKS - 1]).then_inc(w_loaded[0], 16)
            for n in range(KT):
                sync.wait_ge(x_final, n + 1)
                sync.dma_start(out[n * P:(n + 1) * P, :], x[:, n, :]).then_inc(stored, 16)
            sync.wait_ge(stored, 16 * KT)

        @block.gpsimd
        def _(pool):
            def split(n, s):
                pool.wait_ge(w_hi_ready, n + 1)
                nc.gpsimd.tensor_tensor(w_lo[:, s, :], w_raw[:, s, :], f32(w_hi[:, s, :]), ALU.subtract
                                        ).then_inc(w_lo_ready, 1)

            with pool.Fori(0, BLOCKS // 2) as pair:
                for s in range(2):
                    split(pair * 2 + s, s)
            split(BLOCKS - 1, (BLOCKS - 1) % 2)

        @block.tensor
        def _(pe):
            def product(o, s, deep, depth, c0, m, hi, lo, ready=None):
                for kt in range(depth):
                    if ready is not None:
                        ready(kt)
                    wh, wl = wcols(w_hi, s, deep, kt, c0, m), wcols(w_lo, s, deep, kt, c0, m)
                    nc.tensor.matmul(o, wh, hi(kt), start=kt == 0, stop=False)
                    nc.tensor.matmul(o, wh, lo(kt), start=False, stop=False)
                    last = nc.tensor.matmul(o, wl, hi(kt), start=False, stop=kt == depth - 1)
                last.then_inc(tile_done, 1)

            def tile(L, t, s, deep, c0, hi, lo, m=P, depth=None, ready=None):
                pe.wait_ge(bank_free[t % 4], nth(L, LAYER_TILES // 4, t // 4))
                product(ps[t % 4][0:m, :], s, deep, depth or deep, c0, m,
                        lambda kt: hi[:, kt, :], lambda kt: lo[:, kt, :], ready)

            def tiles_together(o, s, src, ready, depth=KT):
                for kt in range(depth):
                    ready(kt)
                    for u in range(len(o)):
                        wh, wl = wcols(w_hi, s, depth, kt, u * P, P), wcols(w_lo, s, depth, kt, u * P, P)
                        nc.tensor.matmul(o[u], wh, src[0][:, kt, :], start=kt == 0, stop=False)
                        nc.tensor.matmul(o[u], wh, src[1][:, kt, :], start=False, stop=False)
                        last = nc.tensor.matmul(o[u], wl, src[0][:, kt, :], start=False, stop=kt == depth - 1)
                        if kt == depth - 1:
                            last.then_inc(tile_done, 1)

            def token_tile(L, t, s, parts, c0, n):
                pe.wait_ge(bank_free[t % 4], nth(L, LAYER_TILES // 4, t // 4))
                for tt, col in parts:
                    o = ps[t % 4][:, col:col + n]
                    for kt in range(KT):
                        ah, al = (m[:, kt, tt * P:(tt + 1) * P] for m in (a_hi, a_lo))
                        wh, wl = wcols(w_hi, s, KT, kt, c0, n), wcols(w_lo, s, KT, kt, c0, n)
                        nc.tensor.matmul(o, ah, wh, start=kt == 0, stop=False)
                        nc.tensor.matmul(o, ah, wl, start=False, stop=False)
                        last = nc.tensor.matmul(o, al, wh, start=False, stop=kt == KT - 1)
                last.then_inc(tile_done, 1)

            def sum_squares(L, which):
                pe.wait_ge(sq_summed, nth(L, 2, which))
                for tt in range(TT):
                    last = nc.tensor.matmul(ps[6][:, tt:tt + 1], acc[:, tt * P:(tt + 1) * P], ones[:, 0:1],
                                            start=True, stop=True)
                last.then_inc(ss_done, 1)

            def turn_rms(L, which):
                pe.wait_ge(rms_spread, nth(L, 2, which))
                for tt in range(TT):
                    last = nc.tensor.transpose(ps[6][:, tt * P:(tt + 1) * P], g[:, 2, tt * P:(tt + 1) * P], ident)
                last.then_inc(rms_turned, 1)

            def scores(L, h):
                rows = slice(HD * (h % 2), HD * (h % 2) + HD)
                for i in range(TT):
                    last = nc.tensor.matmul(query_bank[i], q[rows, h // 2, i * P:(i + 1) * P],
                                            k[rows, h // 2, 0:(i + 1) * P], start=True, stop=True)
                last.then_inc(scores_done, 1)

            def transposes(L, h):
                pe.wait_ge(probs_ready, nth(L, HEADS, h))
                for j in range(TT):
                    for i in range(j, TT):
                        last = nc.tensor.transpose(key_bank[j][:, (i - j) * P:(i - j + 1) * P],
                                                   pr[:, TRI[i] + j * P:TRI[i] + (j + 1) * P], ident)
                last.then_inc(probs_turned, 1)

            def values(L, h):
                pe.wait_ge(pt_ready, nth(L, HEADS, h))
                if h > 0:
                    pe.wait_ge(head_copied, nth(L, HEADS, h - 1))
                rows = slice(HD * (h % 2), HD * (h % 2) + HD)
                for j in range(TT):
                    last = nc.tensor.matmul(ps[7][rows, j * P:], v[:, j, h * HD:(h + 1) * HD],
                                            pt[:, TRT[j]:TRT[j + 1]], start=j == 0, stop=j == TT - 1)
                last.then_inc(head_done, 1)

            def beside(L, s):
                if s == 0:
                    sum_squares(L, 0)
                if s == 2:
                    turn_rms(L, 0)
                for group, (r0, r1) in enumerate(ROPE_GROUPS):
                    if s == ROPE_SLOT[r1 - 1] + 2:
                        n = 2 * ROTARY * (r1 - r0)
                        if s == 4:
                            pe.wait_ge(iw_ready, nth(L, 1, 0))
                            pe.wait_ge(rms_ready, nth(L, 2, 0))
                        pe.wait_ge(rope_gathered[group], nth(L, 1, 0, 32 * (r1 - r0)))
                        if group > 0:
                            pe.wait_ge(rope_turned, nth(L, len(ROPE_GROUPS), group - 1))
                        nc.tensor.matmul(ps[7][0:n, :], rot_m[0:n, 0:n], rope_group[group][0:n, :], start=True, stop=True
                                         ).then_inc(rot_done, 1)
                if s == 4:
                    for i in range(TT):
                        last = nc.tensor.transpose(ps[6][:, IDX_HEADS * i:IDX_HEADS * (i + 1)],
                                                   iw_rows[:, i * P:(i + 1) * P], ident[0:IDX_HEADS, 0:IDX_HEADS])
                    last.then_inc(iw_turned, 1)
                if LOGIT_SLOT <= s < LOGIT_SLOT + IDX_HEADS:
                    h = s - LOGIT_SLOT
                    if h == 0:
                        pe.wait_ge(roped[0], nth(L, 1, 0, 32 * 3))
                    else:
                        pe.wait_ge(logits_used, nth(L, IDX_HEADS, h - 1))
                    rows = slice(64 * (h % 2), 64 * (h % 2) + 64)
                    for i in range(1, TT):
                        last = nc.tensor.matmul(query_bank[i], iq[rows, h // 2, i * P:(i + 1) * P],
                                                ik[rows, 0, 0:(i + 1) * P], start=True, stop=True)
                    last.then_inc(logits_done, 1)
                h, part = divmod(s - HEAD_SLOT, 2)
                if part == 1 and 0 <= h < HEADS:
                    transposes(L, h)
                if part == 0 and 1 <= h <= HEADS:
                    if h == 1:
                        pe.wait_ge(v_ready, nth(L, 1, 0))
                    values(L, h - 1)
                if part == 0 and 0 <= h < HEADS:
                    if h == 0:
                        pe.wait_ge(roped[1], nth(L, 1, 0, 32 * AT))
                        pe.wait_ge(roped[2], nth(L, 1, 0, 32 * AT))
                        pe.wait_ge(logits_used, nth(L, IDX_HEADS, IDX_HEADS - 1))
                    scores(L, h)

            with pe.Fori(0, LAYERS) as L:
                for j in range(B_MLP):
                    s, t = j % 2, first_tile(j)
                    pe.wait_ge(w_lo_ready, nth(L, LAYER_BLOCKS, j))
                    if j == B_IK:
                        tile(L, t, s, KT, 0, a_hi, a_lo)
                        beside(L, t)
                        tile(L, t + 1, s, KT, P, a_hi, a_lo, m=IDX_HEADS)
                        beside(L, t + 1)
                    elif B_V <= j < B_CONV:
                        for u in range(2):
                            token_tile(L, t + u, s, [(2 * u, 0), (2 * u + 1, 256)], 0, 256)
                            beside(L, t + u)
                    elif B_YCONV <= j < B_G1 or B_YATT <= j < B_MIX:
                        if j in (B_YCONV, B_YATT):
                            for u in range(4):
                                pe.wait_ge(bank_free[(t + u) % 4], nth(L, LAYER_TILES // 4, (t + u) // 4))
                            split = cy_split if j == B_YCONV else y_split
                            tiles_together([ps[(t + u) % 4][:, :] for u in range(4)], s, (y_hi, y_lo),
                                      lambda kt: pe.wait_ge(split, nth(L, AT, kt)), depth=AT)
                            if j == B_YCONV:
                                beside(L, 2 * j)
                                beside(L, 2 * j + 1)
                            continue
                        for u in range(4):
                            tile(L, t + u, s, AT, u * P, y_hi, y_lo)
                            if u % 2 and j < B_G1:
                                beside(L, 2 * j + u // 2)
                    else:
                        src = (b_hi, b_lo) if j >= B_MIX else (a_hi, a_lo)
                        if j == B_IQ:
                            for u in range(2):
                                pe.wait_ge(bank_free[u], nth(L, LAYER_TILES // 4, 0))
                            tiles_together((ps[0][:, :], ps[1][:, :]), s, src,
                                      lambda kt: pe.wait_ge(x_split, nth(L, 2 * KT, kt)))
                            beside(L, 0)
                            beside(L, 1)
                            continue
                        for u in range(2):
                            ready = None
                            if j == B_MIX and u == 0:
                                def ready(kt):
                                    pe.wait_ge(merged_split, nth(L, KT, kt))
                            tile(L, t + u, s, KT, u * P, *src, ready=ready)
                            if j < B_YATT:
                                beside(L, 2 * j + u)

                def chunk(c, first):
                    for b in range(8):
                        pe.wait_ge(w_lo_ready, nth(L, LAYER_BLOCKS, c * 8 + (B_MLP + b)))
                        if first and b == 0:
                            for u in range(2):
                                pe.wait_ge(bank_free[u], nth(L, LAYER_TILES // 4, first_tile(B_MLP) // 4))
                            tiles_together((ps[0][:, :], ps[1][:, :]), 0, (a_hi, a_lo),
                                      lambda kt: pe.wait_ge(x_split, nth(L, 2 * KT, KT + kt)))
                            sum_squares(L, 1)
                            continue
                        for u in range(2):
                            n = 2 * b + u
                            pe.wait_ge(bank_free[n % 4], nth(L, LAYER_TILES // 4, c * 4 + (first_tile(B_MLP) + n) // 4))
                            src = (a_hi, a_lo) if b < 4 else (b_hi, b_lo)
                            ready = None
                            if n == 8:
                                def ready(kt):
                                    pe.wait_ge(h_split, nth(L, 8 * CHUNKS, c * 8 + kt))
                            product(ps[n % 4][:, :], b % 2, KT, KT, u * P, P,
                                    lambda kt: src[0][:, kt, :], lambda kt: src[1][:, kt, :], ready)
                            if first and n == 2:
                                turn_rms(L, 1)
                            if n in (10, 12, 14):
                                p = (n - 10) // 2
                                pe.wait_ge(ada_summed, nth(L, 12, c * 3 + p))
                                pe.wait_ge(ada_taken, nth(L, 12, c * 3 + p))
                                for e in range(2):
                                    last = nc.tensor.matmul(ps[7][:, e:e + 1], ada_s[:, e * P:(e + 1) * P],
                                                            ones[:, 0:1], start=True, stop=True)
                                last.then_inc(ada_done, 1)

                chunk(0, True)
                with pe.Fori(1, CHUNKS) as c:
                    chunk(c, False)

            L = LAYERS
            pe.wait_ge(sq_summed, nth(L, 2, 0))
            for tt in range(TT):
                nc.tensor.matmul(ps[6][:, tt:tt + 1], acc[:, tt * P:(tt + 1) * P], ones[:, 0:1], start=True, stop=True)
            pe.wait_ge(gained_summed, 1)
            for tt in range(TT):
                last = nc.tensor.matmul(ps[4][:, tt:tt + 1], gained_sq[0][:, tt * P:(tt + 1) * P], ones[:, 0:1],
                                        start=True, stop=True)
            last.then_inc(ss_done, 1)
            pe.wait_ge(rms_spread, nth(L, 2, 0))
            for bank, tile_ in ((6, 2), (4, 3)):
                for tt in range(TT):
                    last = nc.tensor.transpose(ps[bank][:, tt * P:(tt + 1) * P], g[:, tile_, tt * P:(tt + 1) * P], ident)
            last.then_inc(rms_turned, 1)

            def start_pair(t, s, base):
                for u in range(2):
                    pe.wait_ge(bank_free[(t + u) % 4], nth(L, LAYER_TILES // 4, (t + u) // 4))
                tiles_together((ps[t % 4][:, :], ps[t % 4 + 1][:, :]), s, (a_hi, a_lo),
                          lambda kt: pe.wait_ge(xm_split, base + kt + 1))

            def qk_sums(r):
                pe.wait_ge(qn_sq, r + 1)
                if r == AT:
                    pe.wait_ge(qn_ms, 1)
                c = 8 * (r % AT)
                for tt in range(TT):
                    last = nc.tensor.matmul(ps[6][:, c + 2 * tt:c + 2 * tt + 2], g[:, r % 2, tt * P:(tt + 1) * P],
                                            half[:, 0:P:HD], start=True, stop=True)
                last.then_inc(qn_ss, 1)

            def qk_turn(r):
                pe.wait_ge(qn_spread, r + 1)
                if r >= 2:
                    pe.wait_ge(qk_normed, r - 1)
                for tt in range(TT):
                    last = nc.tensor.transpose(ps[4 + r % 2][:, tt * P:(tt + 1) * P],
                                               g[:, 2 + r % AT, tt * P:(tt + 1) * P], ident)
                last.then_inc(qn_turned, 1)

            for j in range(C_OUT):
                s, t = j % 2, 2 * j
                pe.wait_ge(w_lo_ready, nth(L, LAYER_BLOCKS, j))
                if j == 0:
                    start_pair(0, 0, 0)
                for u in range(2):
                    if C_VA <= j < C_IF or C_VM <= j < C_OG:
                        token_tile(L, t + u, s, [(2 * u, 0), (2 * u + 1, 256)], 0, 256)
                    elif j == C_IF:
                        tile(L, t + u, s, KT, u * MH, a_hi, a_lo, m=MH)
                    elif j > 0:
                        tile(L, t + u, s, KT, u * P, a_hi, a_lo)
                    if 1 <= t + u <= 8:
                        qk_sums(t + u - 1)
                    for first in (AT + 1, 2 * AT + 1):
                        if t + u - first in (0, 1):
                            for e in range(2):
                                qk_turn(first - AT - 1 + 2 * (t + u - first) + e)
                    h, part = divmod(t + u - HEAD2_SLOT, 2)
                    if part == 1 and 0 <= h < HEADS:
                        transposes(L, h)
                    if part == 0 and 1 <= h <= HEADS:
                        if h == 1:
                            pe.wait_ge(v2_ready, 1)
                        values(L, h - 1)
                    if part == 0 and 0 <= h < HEADS:
                        if h == 0:
                            pe.wait_ge(qk_normed, 2 * AT)
                        scores(L, h)

            pe.wait_ge(m_exp, 1)
            pe.wait_ge(m_rows, 1)
            for e, rows in enumerate((row_a, row_e)):
                for tt in range(TT):
                    c = MH * (TT * e + tt)
                    last = nc.tensor.transpose(ps[6][:, c:c + MH], rows[:, tt * P:(tt + 1) * P], ident[0:MH, 0:MH])
            last.then_inc(a_turned, 1)

            def m_maxima(h):
                if h >= 2:
                    pe.wait_ge(m_gap, h - 1)
                nc.tensor.matmul(m_bank[h % 2], sel[:, h * P:(h + 1) * P], row_g, start=True, stop=True
                                 ).then_inc(m_bc, 1)

            def m_products(h):
                for i in range(TT):
                    last = nc.tensor.matmul(key_bank[i], mk[:, h, i * P:(i + 1) * P], mq[:, h, i * P:],
                                            start=True, stop=True)
                last.then_inc(m_scores, 1)

            def m_square_sums(h):
                pe.wait_ge(m_sq, h + 1)
                for tt in range(TT):
                    last = nc.tensor.matmul(m_cols[:, h, 1, tt:tt + 1], k[:, h, tt * P:(tt + 1) * P],
                                            ones[:, 0:1], start=True, stop=True)
                last.then_inc(m_ss, 1)

            def m_turn(h):
                pe.wait_ge(m_spread, h + 1)
                for tt in range(TT):
                    last = nc.tensor.transpose(ps[4 + h][:, tt * P:(tt + 1) * P],
                                               k[:, h, tt * P:(tt + 1) * P], ident)
                last.then_inc(m_turned, 1)

            pe.wait_ge(head_copied, nth(L, HEADS, HEADS - 1))
            m_maxima(0)
            pe.wait_ge(mc_silu, 2 * MH)
            pe.wait_ge(mv_ready, 1)
            pe.wait_ge(a_cols, 1)
            m_products(0)
            for b in (2, 3, 0, 1):
                pe.wait_ge(bank_free[b], nth(L, LAYER_TILES // 4, (2 * C_OUT - b + 3) // 4))
                if b == 2:
                    m_maxima(1)
            for h in range(MH):
                if h + 2 < MH:
                    m_maxima(h + 2)
                pe.wait_ge(m_probs, h + 1)
                if h >= 2:
                    pe.wait_ge(m_sq, h - 1)
                for i in range(TT):
                    nc.tensor.matmul(ps[h % 2][:, i * P:], mv[:, i, h * P:(h + 1) * P], pt[:, TRT[i]:TRT[i + 1]],
                                     start=i == 0, stop=i == TT - 1)
                for i in range(TT):
                    for e in range(i + 1):
                        at = TRT[e] + (i - e) * P
                        last = nc.tensor.matmul(m_cols[:, h, 0, i:i + 1], pt[:, at:at + P], ones[:, 0:1],
                                                start=e == 0, stop=e == i)
                last.then_inc(m_num, 1)
                if h + 1 < MH:
                    m_products(h + 1)
                if h > 0:
                    m_square_sums(h - 1)
            m_square_sums(MH - 1)

            pe.wait_ge(y_split, nth(L, AT, AT - 1))
            order = [(kt, j) for kt in range(AT) for j in (C_OUT + 1, C_OUT)]
            order += [(kt, j) for j in (C_OUT, C_OUT + 1) for kt in range(AT, KT)]
            for kt, j in order:
                if kt == 0:
                    pe.wait_ge(w_lo_ready, nth(L, LAYER_BLOCKS, j))
                if kt == 0 and j == C_OUT:
                    pe.wait_ge(m_ms, 1)
                if kt >= AT:
                    pe.wait_ge(m_split, kt - AT + 1)
                hi, lo = (m[:, kt % AT, :] for m in ((y_hi, y_lo) if kt < AT else (a_hi, a_lo)))
                for u in range(2):
                    t = 2 * j + u
                    o, s = ps[t % 4][:, :], j % 2
                    wh, wl = wcols(w_hi, s, KT, kt, u * P, P), wcols(w_lo, s, KT, kt, u * P, P)
                    nc.tensor.matmul(o, wh, hi, start=kt == 0, stop=False)
                    nc.tensor.matmul(o, wh, lo, start=False, stop=False)
                    last = nc.tensor.matmul(o, wl, hi, start=False, stop=kt == KT - 1)
                    if kt == KT - 1:
                        last.then_inc(tile_done, 1)
                if kt == 1 and j == C_OUT:
                    for h in range(MH):
                        m_turn(h)
            for j in range(C_OUT + 2, C_FF):
                pe.wait_ge(w_lo_ready, nth(L, LAYER_BLOCKS, j))
                for u in range(2):
                    t = 2 * j + u
                    pe.wait_ge(bank_free[t % 4], nth(L, LAYER_TILES // 4, t // 4))
                    product(ps[t % 4][:, :], j % 2, KT, KT, u * P, P,
                            lambda kt: y_hi[:, kt, :] if kt < AT else a_hi[:, kt - AT, :],
                            lambda kt: y_lo[:, kt, :] if kt < AT else a_lo[:, kt - AT, :])
            sum_squares(L, 1)
            turn_rms(L, 1)
            j, hid = C_FF, 0
            for nt in FF_TILES:
                for b in range(nt):
                    pe.wait_ge(w_lo_ready, nth(L, LAYER_BLOCKS, j))
                    if j == C_FF:
                        start_pair(2 * j, j % 2, KT)
                        j += 1
                        continue
                    for u in range(2):
                        tile(L, 2 * j + u, j % 2, KT, u * P, a_hi, a_lo)
                    j += 1
                for b in range(4):
                    pe.wait_ge(w_lo_ready, nth(L, LAYER_BLOCKS, j))
                    for u in range(2):
                        ready = None
                        if b + u == 0:
                            def ready(kt):
                                pe.wait_ge(h_split, nth(L, 8 * CHUNKS, hid + kt))
                        tile(L, 2 * j + u, j % 2, KT, u * P, b_hi, b_lo, depth=nt, ready=ready)
                    j += 1
                hid += nt

        @block.scalar
        def _(act):
            def w_split(L, n, at=0):
                act.wait_ge(w_loaded[n % 2], nth(L, LAYER_BLOCKS // 2, at * 4 + n // 2, 16))
                nc.scalar.activation(w_hi[:, n % 2, :], w_raw[:, n % 2, :], ACT.Copy).then_inc(w_hi_ready, 1)

            def x_parts(n, gain):
                nc.scalar.activation(a_hi[:, n, :], x[:, n, :], ACT.Copy, scale=gain).then_inc(x_hi, 1)
                nc.scalar.activation(g[:, n % 2, :], x[:, n, :], ACT.Square).then_inc(x_sq, 1)

            def root(L, which):
                nc.scalar.activation(warm[:, :], ones[:, 0:1], ACT.Sqrt)
                act.wait_ge(ms_ready, nth(L, 2, which))
                nc.scalar.activation(rms_col[:, 8:12], rms_col[:, 4:8], ACT.Sqrt).then_inc(root_ready, 1)

            def exps(L, h):
                for i in range(TT):
                    act.wait_ge(masked, nth(L, TT * HEADS, TT * h + i))
                    nc.scalar.activation(pr[:, TRI[i]:TRI[i + 1]], pr[:, TRI[i]:TRI[i + 1]], ACT.Exp, scale=-1.0,
                                         bias=peak[:, i:i + 1], accum_out=peak[:, 4 + i:5 + i])
                act.drain().then_inc(exps_done, 1)

            def turned(L, h):
                act.wait_ge(probs_turned, nth(L, HEADS, h))
                nc.scalar.activation(pt[:, TRT[0]:TRT[1]], ps[4][:, :], ACT.Copy)
                nc.scalar.activation(pt[:, TRT[1]:TRT[2]], ps[5][:, 0:384], ACT.Copy)
                nc.scalar.activation(pt[:, TRT[3]:TRT[4]], ps[5][:, 384:512], ACT.Copy)
                nc.scalar.activation(pt[:, TRT[2]:TRT[3]], ps[6][:, 0:256], ACT.Copy)
                act.drain().then_inc(pt_ready, 1)

            def head_out(L, h):
                act.wait_ge(head_done, nth(L, HEADS, h))
                rows = slice(HD * (h % 2), HD * (h % 2) + HD)
                nc.scalar.activation(q[rows, h // 2, :], ps[7][rows, :], ACT.Copy).then_inc(head_copied, 1)

            def y_high(L, i):
                act.wait_ge(head_copied, nth(L, HEADS, 2 * i + 1))
                nc.scalar.activation(y_hi[:, i, :], q[:, i, :], ACT.Copy).then_inc(y_hi_ready, 1)

            act.dma_start(sp[:, :], params).then_inc(params_loaded, 16)
            for dst, src in ((kc[:, :], consts), (cs_rope[:, :, :], rope), (bias[:, 0:P], tri_bias)):
                act.dma_start(dst, src).then_inc(setup_loaded, 16)
            w_split(0, 0)
            act.wait_ge(params_loaded, 16)
            for n in range(KT):
                if n % 4 == 0:
                    act.wait_ge(x_loaded[n // 4], 16)
                if n >= 2:
                    act.wait_ge(sq_used, n - 1)
                x_parts(n, sp[:, SP_G0 + n:SP_G0 + n + 1])
            w_split(0, 1)
            nc.scalar.activation(cs[:, :], sp[:, SP_C:SP_C + KT], ACT.Silu).then_inc(c_silu, 1)
            act.wait_ge(setup_loaded, 16 * 3)

            def beside(L, s, t):
                b = t % 4
                if s - 1 in ROPE_SLOT:
                    r = ROPE_SLOT.index(s - 1)
                    group = [r < end for _, end in ROPE_GROUPS].index(True)
                    act.wait_ge(qk_ready, nth(L, ROPES, r))
                    for e in range(2):
                        in_tile, in_group = rotary(r, e)
                        act.dma_start(in_group, in_tile).then_inc(rope_gathered[group], 16)
                for group, (r0, r1) in enumerate(ROPE_GROUPS):
                    if s == ROPE_SLOT[r1 - 1] + 3:
                        act.wait_ge(rope_turned, nth(L, len(ROPE_GROUPS), group))
                        for r in range(r0, r1):
                            for e in range(2):
                                in_tile, in_group = rotary(r, e)
                                act.dma_start(in_tile, in_group).then_inc(roped[group], 16)
                if s == 0:
                    act.wait_ge(x_split, nth(L, 2 * KT, KT - 1))
                    act.dma_start(lp[:, :], layer_params[bass.ds(L, 1)].rearrange("a p n -> p (a n)")
                                  ).then_inc(lp_loaded, 16)
                    root(L, 0)
                if 2 * B_V <= s < 2 * B_CONV:
                    if s == 2 * B_V:
                        act.wait_ge(rms_ready, nth(L, 2, 0))
                    col, u = (s - 2 * B_V) // 2 * 256, s % 2
                    for e in range(2):
                        last = nc.scalar.activation(v[:, 2 * u + e, col:col + 256], ps[b][:, 256 * e:256 * e + 256],
                                                    ACT.Copy, scale=rms_col[:, 2 * u + e:2 * u + e + 1])
                    last.then_inc(bank_free[b], 1)
                    if s == 2 * B_CONV - 1:
                        act.drain().then_inc(v_ready, 1)
                if 2 * B_CONV <= s < 2 * B_YCONV and (s - 2 * B_CONV) % 6 >= 4:
                    i = 2 * ((s - 2 * B_CONV) // 6) + s % 2
                    act.wait_ge(cy_ready, nth(L, AT, i))
                    nc.scalar.activation(y_hi[:, i, :], g[:, 6 + s % 2, :], ACT.Copy).then_inc(cy_hi, 1)
                h, part = divmod(s - HEAD_SLOT, 2)
                if part == 1 and 0 <= h < HEADS:
                    turned(L, h)
                if part == 0 and 1 <= h <= HEADS:
                    head_out(L, h - 1)
                if part == 0 and 0 <= h < HEADS:
                    exps(L, h)
                if s in Y_SLOT:
                    y_high(L, Y_SLOT.index(s))
                if 2 * B_G1 <= s < 2 * B_YATT:
                    i = s - 2 * B_G1
                    act.wait_ge(gate_ready, nth(L, 2 * KT, i))
                    nc.scalar.activation(g[:, i % 8, :], g[:, i % 8, :], ACT.Tanh, scale=0.5).then_inc(gate_tanh, 1)

            with act.Fori(0, LAYERS) as L:
                for j in range(B_MLP):
                    t0, t1 = first_tile(j), first_tile(j + 1)
                    for t in range(t0, t1):
                        act.wait_ge(tile_done, nth(L, LAYER_TILES, t))
                        if t == t1 - 1:
                            w_split(L, j + 2)
                        if j < B_YCONV or B_G1 <= j < B_YATT:
                            beside(L, 2 * j + t - t0, t)
                        elif j < B_G1:
                            n = t - first_tile(B_YCONV)
                            nc.scalar.activation(yc[:, n, :], ps[t % 4][:, :], ACT.Copy
                                                 ).then_inc(bank_free[t % 4], 1)
                            if n == KT - 1:
                                act.drain().then_inc(yc_ready, 1)
                            if (t - t0) % 2:
                                beside(L, 2 * j + (t - t0) // 2, t)
                        elif j < B_MIX:
                            n = t - first_tile(B_YATT)
                            act.wait_ge(merged_ready, nth(L, KT, n))
                            nc.scalar.activation(b_hi[:, n, :], g[:, n, :], ACT.Copy, scale=0.5).then_inc(merged_hi, 1)
                        else:
                            n = t - first_tile(B_MIX)
                            if n == 0:
                                act.wait_ge(lp_loaded, nth(L, 1, 0, 16))
                            act.wait_ge(x_ready, nth(L, 2 * KT, n))
                            x_parts(n, lp[:, LP_GMLP + n:LP_GMLP + n + 1])
                root(L, 1)

                def chunk(c, last):
                    for n in range(16):
                        act.wait_ge(tile_done, nth(L, LAYER_TILES, c * 16 + (first_tile(B_MLP) + n)))
                        if n % 2:
                            w_split(L, B_MLP + n // 2 + 2, c)
                        if n in (0, 9, 11):
                            p = (0, 9, 11).index(n)
                            act.wait_ge(ada_used, nth(L, 12, c * 3 + p))
                            act.dma_start(ada_w[:, :, :], ada[bass.ds(L * 12 + c * 3 + p, 1)].rearrange(
                                "a p (k n) -> p (a k) n", k=TT)).then_inc(ada_loaded, 16)
                        for m in {0: (), 1: (0, 1)}.get(n, (n,) if n < 8 else ()):
                            act.wait_ge(h_ready, nth(L, 8 * CHUNKS, c * 8 + m))
                            nc.scalar.activation(b_hi[:, m, :], g[:, 6 + m % 2, :], ACT.Copy).then_inc(h_hi, 1)
                        if n >= 8 and last:
                            act.wait_ge(x_ready, nth(L, 2 * KT, n))
                            x_parts(n - 8, lp[:, LP_GNEXT + n - 8:LP_GNEXT + n - 7])

                with act.Fori(0, CHUNKS - 1) as c:
                    chunk(c, False)
                chunk(CHUNKS - 1, True)

            L = LAYERS
            second = [(bias[:, :], mult_bias), (tri, tri_mask), (sel, selectors)]
            for dst, src in second:
                act.dma_start(dst, src).then_inc(second_loaded, 16)
            for n in range(KT):
                nc.scalar.activation(gained_sq[n], x[:, n, :], ACT.Square, scale=sp[:, SP_GFIN + n:SP_GFIN + n + 1]
                                     ).then_inc(x_sq, 1)
            nc.scalar.activation(warm[:, :], ones[:, 0:1], ACT.Sqrt)
            act.wait_ge(ms_ready, nth(L, 2, 0))
            nc.scalar.activation(qcol[:, 1, 0:2 * TT], qcol[:, 0, 0:2 * TT], ACT.Sqrt).then_inc(root_ready, 1)

            def modulated(base, shift):
                for n in range(KT):
                    act.wait_ge(xm_ready, base + n + 1)
                    nc.scalar.activation(a_hi[:, n, :], g[:, 4 + n % 2, :], ACT.Identity,
                                         bias=mod[:, shift + n:shift + n + 1]).then_inc(xm_hi, 1)

            modulated(0, 0)

            def silu_tanh(i):
                act.wait_ge(mc_ready, i + 1)
                if i > 0:
                    act.wait_ge(mc_silu, i)
                nc.scalar.activation(mt[:, :], g[:, 4 + i % 2, :], ACT.Tanh, scale=0.5
                                     ).then_inc(mc_tanh, 1)

            for j in range(C_OUT):
                for u in range(2):
                    t = 2 * j + u
                    b = t % 4
                    act.wait_ge(tile_done, nth(L, LAYER_TILES, t))
                    if u:
                        w_split(L, j + 2)
                    if j < C_VA:
                        if t >= 2:
                            act.wait_ge(qn_ss, t - 1)
                        dst = q[:, t, :] if t < AT else k[:, t - AT, :]
                        nc.scalar.activation(dst, ps[b][:, :], ACT.Copy)
                        nc.scalar.activation(g[:, t % 2, :], ps[b][:, :], ACT.Square).then_inc(qn_sq, 1)
                        act.drain().then_inc(bank_free[b], 1)
                    if t in (AT, 2 * AT):
                        act.wait_ge(qn_ms, t // AT)
                        nc.scalar.activation(qcol[:, 1, :], qcol[:, 0, :], ACT.Sqrt).then_inc(qn_root, 1)
                    if C_VA <= j < C_IF or C_VM <= j < C_OG:
                        first = C_VA if j < C_IF else C_VM
                        dst, col = (v, mv)[first == C_VM], (j - first) * 256
                        for e in range(2):
                            last = nc.scalar.activation(dst[:, 2 * u + e, col:col + 256],
                                                        ps[b][:, 256 * e:256 * e + 256], ACT.Copy)
                        last.then_inc(bank_free[b], 1)
                        if t == 2 * first + 3:
                            act.drain().then_inc((v2_ready, mv_ready)[first == C_VM], 1)
                    if C_QM <= j < C_VM:
                        i = t - 2 * C_QM
                        if i >= 2:
                            act.wait_ge(mc_silu, i - 1)
                        nc.scalar.activation(g[:, 4 + i % 2, :], ps[b][:, :], ACT.Identity,
                                             scale=sp[:, SP_WCONV + 24 + i:SP_WCONV + 25 + i],
                                             bias=sp[:, SP_BCONV + i:SP_BCONV + i + 1]).then_inc(mc_first, 1)
                    h, part = divmod(t - HEAD2_SLOT, 2)
                    if part == 0 and 0 <= h < HEADS:
                        exps(L, h)
                    if C_QM <= j < C_VM:
                        silu_tanh(t - 2 * C_QM)
                    if C_OG <= j:
                        i = t - 2 * C_OG
                        nc.scalar.activation(og[i], ps[b][:, :], ACT.Tanh, scale=0.5).then_inc(bank_free[b], 1)
                        if i == MH - 1:
                            act.drain().then_inc(og_ready, 1)
                    if t == 2 * C_VM + 2:
                        act.wait_ge(m_rows, 1)
                        nc.scalar.activation(row_e, row_b, ACT.Exp, scale=-1.0).then_inc(m_exp, 1)
                    if t == 2 * C_IF + 1:
                        act.wait_ge(f_ready, 1)
                        nc.scalar.activation(row_e, row_b, ACT.Abs)
                        act.drain()
                        nc.scalar.activation(row_e, row_e, ACT.Exp, scale=-1.0)
                        act.drain()
                        nc.scalar.activation(row_e, row_e, ACT.Ln, bias=1.0).then_inc(f_log, 1)
                    if part == 1 and 0 <= h < HEADS:
                        turned(L, h)
                    if part == 0 and 1 <= h <= HEADS:
                        head_out(L, h - 1)
                        if h % 2 == 0:
                            y_high(L, h // 2 - 1)

            def m_high(h):
                act.wait_ge(m_out, h + 1)
                nc.scalar.activation(a_hi[:, h, :], g[:, 4 + h, :], ACT.Copy, scale=0.5).then_inc(m_hi, 1)

            for h in range(MH + 2):
                if h < MH:
                    act.wait_ge(m_gap, h + 1)
                    nc.scalar.activation(m_pr[h % 2][:, :], m_pr[h % 2][:, :], ACT.Exp, scale=-1.0).then_inc(m_decay, 1)
                if h >= 2:
                    act.wait_ge(m_num, h - 1)
                    nc.scalar.activation(g[:, 2 + h, :], ps[h % 2][:, :], ACT.Copy)
                    nc.scalar.activation(k[:, h - 2, :], ps[h % 2][:, :], ACT.Square).then_inc(m_sq, 1)
            act.wait_ge(m_ms, 1)
            nc.scalar.activation(mcol[:, 2, :, :], mcol[:, 1, :, :], ACT.Sqrt).then_inc(m_root, 1)
            for h in range(MH):
                m_high(h)

            for j in range(C_OUT, C_FF):
                for u in range(2):
                    t = 2 * j + u
                    act.wait_ge(tile_done, nth(L, LAYER_TILES, t))
                    if u:
                        w_split(L, j + 2)
                    n = t - 2 * C_OUT
                    act.wait_ge(x_ready, nth(L, 2 * KT, n))
                    nc.scalar.activation(g[:, n % 2, :], x[:, n, :], ACT.Square).then_inc(x_sq, 1)
            root(L, 1)
            modulated(KT, 3 * KT)
            j, hid = C_FF, 0
            for nt in FF_TILES:
                for b in range(nt + 4):
                    for u in range(2):
                        act.wait_ge(tile_done, nth(L, LAYER_TILES, 2 * j + u))
                        if u and j + 2 < SECOND_BLOCKS:
                            w_split(L, j + 2)
                        if b < nt and b % 2 == 0:
                            n = hid + b + u
                            if n >= 2:
                                act.wait_ge(h_ready, nth(L, 8 * CHUNKS, n - 2))
                            nc.scalar.activation(g[:, 4 + u, :], ps[(2 * j + u) % 4][:, :], ACT.Silu
                                                 ).then_inc(silu_done, 1)
                            act.drain().then_inc(bank_free[(2 * j + u) % 4], 1)
                        elif b < nt:
                            n = hid + b - 1 + u
                            act.wait_ge(h_ready, nth(L, 8 * CHUNKS, n))
                            nc.scalar.activation(b_hi[:, n - hid, :], g[:, 6 + u, :], ACT.Copy).then_inc(h_hi, 1)
                    j += 1
                hid += nt

        @block.vector
        def _(dve):
            def tt(out_, a, b_, op):
                return nc.vector.tensor_tensor(out_, a, b_, op)

            def take(L, t, out_, scale):
                dve.wait_ge(tile_done, nth(L, LAYER_TILES, t))
                tt(out_, ps[t % 4][:, :], scale, ALU.mult).then_inc(bank_free[t % 4], 1)

            def refine(y, root_, mean, tmp, out_sem=None):
                nc.vector.reciprocal(y, root_)
                dve.drain()
                tt(tmp, y, y, ALU.mult)
                dve.drain()
                tt(tmp, tmp, mean, ALU.mult)
                dve.drain()
                nc.vector.tensor_scalar(tmp, tmp, -0.5, 1.5, ALU.mult, ALU.add)
                dve.drain()
                last = tt(y, y, tmp, ALU.mult)
                if out_sem is not None:
                    last.then_inc(out_sem, 1)

            def norm(L, which, copy=True):
                dve.wait_ge(ss_done, nth(L, 2, which))
                nc.vector.tensor_scalar(rms_col[:, 4:8], ps[6][:, 0:TT], 1.0 / D, EPS, ALU.mult, ALU.add
                                        ).then_inc(ms_ready, 1)
                dve.wait_ge(root_ready, nth(L, 2, which))
                refine(rms_col[:, 0:4], rms_col[:, 8:12], rms_col[:, 4:8], rms_col[:, 8:12])
                dve.drain()
                nc.vector.tensor_copy(g[:, 2, :].rearrange("p (t c) -> p t c", t=TT),
                                      rms_col[:, 0:TT].unsqueeze(2).to_broadcast([P, TT, P])).then_inc(rms_spread, 1)
                dve.wait_ge(rms_turned, nth(L, 2, which))
                if copy:
                    nc.vector.tensor_copy(rms[:, :], ps[6][:, :]).then_inc(rms_ready, 1)
                    dve.drain()

            def low(L, n, k_, gain):
                dve.wait_ge(x_hi, nth(L, 2 * KT, k_))
                nc.vector.scalar_tensor_tensor(a_lo[:, n, :], x[:, n, :], gain, f32(a_hi[:, n, :]), ALU.mult,
                                               ALU.subtract).then_inc(x_split, 1)
                squares(L, n, k_)

            def squares(L, n, k_):
                dve.drain()
                dve.wait_ge(x_sq, nth(L, 2 * KT, k_))
                if n == 0:
                    last = nc.vector.tensor_copy(acc, g[:, 0, :])
                else:
                    last = tt(acc, acc, g[:, n % 2, :], ALU.add)
                if n == KT - 1:
                    last.then_inc(sq_summed, 1)

            for b in range(4):
                nc.vector.memset(top[:, 0, b:b + 1], 0.0).then_inc(bank_free[b], 1)
            nc.vector.memset(top[:, 0, 4:5], 0.0).then_inc(ada_used, 1)
            nc.vector.memset(top[:, 0, 5:6], 0.0).then_inc(ada_taken, 1)
            dve.wait_ge(params_loaded, 16)
            for n in range(KT):
                dve.wait_ge(x_loaded[n // 4], 16)
                dve.wait_ge(x_hi, n + 1)
                gain = sp[:, SP_G0 + n:SP_G0 + n + 1]
                nc.vector.scalar_tensor_tensor(a_lo[:, n, :], x[:, n, :], gain, f32(a_hi[:, n, :]), ALU.mult,
                                               ALU.subtract).then_inc(x_split, 1)
                dve.wait_ge(x_sq, n + 1)
                if n == 0:
                    last = nc.vector.tensor_copy(acc, g[:, 0, :])
                else:
                    last = tt(acc, acc, g[:, n % 2, :], ALU.add)
                last.then_inc(sq_used, 1)
                dve.drain()
            dve.wait_ge(setup_loaded, 16 * 3)
            nc.vector.memset(top[:, 0, 6:7], 0.0).then_inc(sq_summed, 1)
            dve.wait_ge(c_silu, 1)

            def mask_scores(L, h, scale):
                dve.wait_ge(scores_done, nth(L, HEADS, h))
                nc.vector.memset(nudge[:, :], 0.0)
                for i in range(TT):
                    nc.vector.tensor_tensor_reduce(out=pr[:, TRI[i]:TRI[i + 1]], in0=query_bank[i],
                                                   in1=bias[:, TRI[i]:TRI[i + 1]], scale=-scale, scalar=3.0e38,
                                                   op0=ALU.add, op1=ALU.min, accum_out=peak[:, i:i + 1]
                                                   ).then_inc(masked, 1)

            def normalise(L, h):
                dve.wait_ge(exps_done, nth(L, HEADS, h))
                nc.vector.reciprocal(peak[:, 8:12], peak[:, 4:8])
                dve.drain()
                for i in range(TT):
                    last = nc.vector.tensor_scalar(pr[:, TRI[i]:TRI[i + 1]], pr[:, TRI[i]:TRI[i + 1]],
                                                   peak[:, 8 + i:9 + i], None, ALU.mult)
                dve.drain().then_inc(probs_ready, 1)

            def y_low(L, i):
                dve.wait_ge(y_hi_ready, nth(L, AT, i))
                tt(y_lo[:, i, :], q[:, i, :], f32(y_hi[:, i, :]), ALU.subtract).then_inc(y_split, 1)

            def gate_finish(L, i):
                dve.wait_ge(gate_tanh, nth(L, 2 * KT, i))
                if i == 0:
                    dve.wait_ge(yc_ready, nth(L, 1, 0))
                nc.vector.scalar_tensor_tensor(yc[:, i, :], g[:, i, :], 1.0, yc[:, i, :], ALU.add, ALU.mult)
                dve.drain()

            def convolve(L, s):
                pair, kind, e = (s - 2 * B_CONV) // 6, (s - 2 * B_CONV) % 6 // 2, s % 2
                i = 2 * pair + e
                first, second = g[:, 6 + e, :], g[:, 4 + e, :]
                if kind == 0:
                    take(L, s, first, rms[:, :])
                elif kind == 1:
                    take(L, s, second, rms[:, :])
                    dve.drain()
                    tt(first, first, second, ALU.mult)
                    dve.drain()
                    w = [lp[:, LP_CONV + 4 * tap + i:LP_CONV + 4 * tap + i + 1] for tap in range(3)]
                    nc.vector.tensor_scalar(second, first, w[2], None, ALU.mult)
                    for back in (1, 2):
                        dve.drain()
                        nc.vector.scalar_tensor_tensor(second[:, back:], first[:, 0:S - back], w[2 - back],
                                                       second[:, back:], ALU.mult, ALU.add)
                    dve.drain()
                else:
                    take(L, s, first, rms[:, :])
                    dve.drain()
                    tt(first, first, second, ALU.mult).then_inc(cy_ready, 1)

            def beside(L, s, t):
                if s == 0:
                    norm(L, 0)
                if s == 5:
                    dve.wait_ge(iw_turned, nth(L, 1, 0))
                    nc.vector.tensor_copy(iw[:, :, :].rearrange("p a b -> p (a b)"), ps[6][:, 0:TT * IDX_HEADS])
                for group, (r0, r1) in enumerate(ROPE_GROUPS):
                    if s == ROPE_SLOT[r1 - 1] + 3:
                        n = 2 * ROTARY * (r1 - r0)
                        plain, swapped = rope_group[group][0:n, :], g[0:n, 7, :]
                        dve.wait_ge(rot_done, nth(L, len(ROPE_GROUPS), group))
                        tt(plain, plain, cs_rope[0:n, 0, :], ALU.mult)
                        tt(swapped, ps[7][0:n, :], cs_rope[0:n, 1, :], ALU.mult)
                        dve.drain()
                        tt(plain, plain, swapped, ALU.add).then_inc(rope_turned, 1)
                if s in ROPE_SLOT:
                    r = ROPE_SLOT.index(s)
                    take(L, s, rope_tiles[r], rms[:, :])
                    dve.drain().then_inc(qk_ready, 1)
                if s == 3:
                    dve.wait_ge(tile_done, nth(L, LAYER_TILES, 3))
                    nc.vector.scalar_tensor_tensor(iw_rows[:, :], ps[3][0:IDX_HEADS, :], (64 ** -0.5) * (IDX_HEADS ** -0.5),
                                                   rms[0:IDX_HEADS, :], ALU.mult, ALU.mult).then_inc(bank_free[3], 1)
                    dve.drain().then_inc(iw_ready, 1)
                if LOGIT_SLOT <= s < LOGIT_SLOT + IDX_HEADS:
                    h = s - LOGIT_SLOT
                    dve.drain()
                    dve.wait_ge(logits_done, nth(L, IDX_HEADS, h))
                    for i in range(1, TT):
                        to = (bias if h == 0 else pr)[:, TRI[i]:TRI[i + 1]]
                        last = nc.vector.tensor_scalar(to, query_bank[i], 0.0, iw[:, i, h:h + 1], ALU.max, ALU.mult)
                    last.then_inc(logits_used, 1)
                    dve.drain()
                    if h > 0:
                        tt(bias[:, TRI[1]:], bias[:, TRI[1]:], pr[:, TRI[1]:], ALU.add)
                        dve.drain()
                    if h == IDX_HEADS - 1:
                        for i in range(1, TT):
                            nc.vector.memset(bias[0:64, TRI[i + 1] - 64:TRI[i + 1]], OUTSIDE)
                        dve.drain()
                if 2 * B_CONV <= s < 2 * B_YCONV:
                    if s == 2 * B_CONV:
                        dve.wait_ge(lp_loaded, nth(L, 1, 0, 16))
                        for group, (r0, r1) in enumerate(ROPE_GROUPS):
                            dve.wait_ge(roped[group], nth(L, 1, 0, 32 * (r1 - r0)))
                    convolve(L, s)
                if s in TOPK_SLOT:
                    rows = [bias[:, TRI[i]:TRI[i + 1]] for i in range(1, TT)]
                    for i, row in enumerate(rows):
                        nc.vector.max(top[:, i, :], row)
                    dve.drain()
                    for i, row in enumerate(rows):
                        nc.vector.match_replace(row, top[:, i, :], row, TAKEN)
                    dve.drain()
                    if s == TOPK_SLOT[-1]:
                        left = bias[:, TRI[1]:]
                        nc.vector.tensor_scalar(left, left, 0.5 * (TAKEN + OUTSIDE), NEG, ALU.is_gt, ALU.mult)
                        dve.drain()
                if 2 * B_CONV <= s < 2 * B_YCONV and (s - 2 * B_CONV) % 6 >= 4:
                    i = 2 * ((s - 2 * B_CONV) // 6) + s % 2
                    dve.wait_ge(cy_hi, nth(L, AT, i))
                    tt(y_lo[:, i, :], g[:, 6 + s % 2, :], f32(y_hi[:, i, :]), ALU.subtract).then_inc(cy_split, 1)
                    dve.drain()
                h, part = divmod(s - HEAD_SLOT, 2)
                if part == 0 and 0 <= h < HEADS:
                    mask_scores(L, h, HD ** -0.5)
                if 2 * B_G1 <= s < 2 * B_YATT:
                    i = s - 2 * B_G1
                    if 0 < i <= KT:
                        gate_finish(L, i - 1)
                    dve.wait_ge(tile_done, nth(L, LAYER_TILES, t))
                    tt(g[:, i % 8, :], ps[t % 4][:, :], rms[:, :], ALU.mult).then_inc(bank_free[t % 4], 1)
                    dve.drain().then_inc(gate_ready, 1)
                if part == 0 and 0 <= h < HEADS:
                    normalise(L, h)
                if s in Y_SLOT:
                    y_low(L, Y_SLOT.index(s))

            with dve.Fori(0, LAYERS) as L:
                for j in range(B_YATT):
                    t0, t1 = first_tile(j), first_tile(j + 1)
                    for u in range(2):
                        beside(L, 2 * j + u, t0 + u if t1 - t0 == 2 else t0 + 2 * u + 1)

                def merged_low(n):
                    dve.wait_ge(merged_hi, nth(L, KT, n))
                    nc.vector.scalar_tensor_tensor(b_lo[:, n, :], g[:, n, :], 0.5, f32(b_hi[:, n, :]), ALU.mult,
                                                   ALU.subtract).then_inc(merged_split, 1)

                for n in range(KT):
                    t = first_tile(B_YATT) + n
                    dve.wait_ge(gate_tanh, nth(L, 2 * KT, KT + n))
                    dve.wait_ge(tile_done, nth(L, LAYER_TILES, t))
                    nc.vector.scalar_tensor_tensor(g[:, n, :], g[:, n, :], 1.0, ps[t % 4][:, :], ALU.add, ALU.mult
                                                   ).then_inc(bank_free[t % 4], 1)
                    dve.drain()
                    tt(g[:, n, :], g[:, n, :], yc[:, n, :], ALU.add).then_inc(merged_ready, 1)
                    if n > 0:
                        merged_low(n - 1)
                merged_low(KT - 1)

                def x_add(t, n, done):
                    last = tt(x[:, n, :], x[:, n, :], ps[t % 4][:, :], ALU.add)
                    last.then_inc(bank_free[t % 4], 1)
                    if done:
                        dve.drain().then_inc(x_ready, 1)

                for n in range(KT):
                    t = first_tile(B_MIX) + n
                    dve.wait_ge(tile_done, nth(L, LAYER_TILES, t))
                    x_add(t, n, True)
                    if n > 0:
                        low(L, n - 1, KT + n - 1, lp[:, LP_GMLP + n - 1:LP_GMLP + n])
                low(L, KT - 1, 2 * KT - 1, lp[:, LP_GMLP + KT - 1:LP_GMLP + KT])
                norm(L, 1)

                def chunk(c, last_chunk):
                    def h_low(n):
                        dve.wait_ge(h_hi, nth(L, 8 * CHUNKS, c * 8 + n))
                        tt(b_lo[:, n, :], g[:, 6 + n % 2, :], f32(b_hi[:, n, :]), ALU.subtract).then_inc(h_split, 1)
                        dve.drain()

                    for n in range(8):
                        dve.wait_ge(tile_done, nth(L, LAYER_TILES, c * 16 + (first_tile(B_MLP) + n)))
                        t = g[:, 4 + n % 2, :]
                        tt(t, ps[n % 4][:, :], rms[:, :], ALU.mult).then_inc(bank_free[n % 4], 1)
                        dve.drain()
                        nc.vector.scalar_tensor_tensor(g[:, 6 + n % 2, :], t, 0.0, t, ALU.max, ALU.mult
                                                       ).then_inc(h_ready, 1)
                        if n > 0:
                            h_low(n - 1)
                    h_low(7)
                    for n in range(8, 16):
                        dve.wait_ge(tile_done, nth(L, LAYER_TILES, c * 16 + (first_tile(B_MLP) + n)))
                        x_add(n, n - 8, last_chunk)
                        if last_chunk and n > 8:
                            low(L, n - 9, KT + n - 1, lp[:, LP_GNEXT + n - 9:LP_GNEXT + n - 8])
                        p = (n - 8) // 2
                        if n % 2 == 0 and p < 3:
                            dve.drain()
                            dve.wait_ge(ada_loaded, nth(L, 12, c * 3 + p, 16))
                            tt(ada_p.rearrange("p (k n) -> p k n", k=KT),
                               ada_w[:, :, :].rearrange("p a (b n) -> p (a b) n", b=2),
                               cs[:, :].unsqueeze(2).to_broadcast([P, KT, 256]), ALU.mult).then_inc(ada_used, 1)
                            dve.drain()
                            if p > 0:
                                dve.wait_ge(ada_done, nth(L, 12, c * 3 + p - 1))
                            nc.vector.tensor_reduce(out=ada_s, in_=ada_p.rearrange("p (k n) -> p n k", k=KT),
                                                    axis=AX_X, op=ALU.add).then_inc(ada_summed, 1)
                        if n % 2 and 1 <= p <= 3:
                            p -= 1
                            dve.wait_ge(ada_done, nth(L, 12, c * 3 + p))
                            col = (L * 12 + c * 3 + p) * 2
                            tt(mod[:, bass.ds(col, 2)], ps[7][:, 0:2], sp[:, bass.ds(col + SP_BADA, 2)], ALU.add
                               ).then_inc(ada_taken, 1)

                with dve.Fori(0, CHUNKS - 1) as c:
                    chunk(c, False)
                chunk(CHUNKS - 1, True)
                low(L, KT - 1, 3 * KT - 1, lp[:, LP_GNEXT + KT - 1:LP_GNEXT + KT])

            L = LAYERS
            for e, (gain, scale) in enumerate(((SP_GMIX, KT), (SP_GFFN, 4 * KT))):
                nc.vector.scalar_tensor_tensor(gs[:, e * KT:(e + 1) * KT], mod[:, scale:scale + KT], 1.0,
                                               sp[:, gain:gain + KT], ALU.add, ALU.mult)
            dve.drain()
            tt(gs[:, 0:KT], gs[:, 0:KT], sp[:, SP_GFIN:SP_GFIN + KT], ALU.mult)
            for n in range(1, KT):
                dve.wait_ge(x_sq, nth(L, 2 * KT, KT + n))
                last = tt(gained_sq[0], gained_sq[0], gained_sq[n], ALU.add)
                if n < KT - 1:
                    dve.drain()
            last.then_inc(gained_summed, 1)
            mean, root_, inverse = (qcol[:, e, 0:2 * TT] for e in range(3))
            dve.wait_ge(ss_done, nth(L, 2, 0))
            nc.vector.tensor_scalar(mean[:, 0:TT], ps[6][:, 0:TT], 1.0 / D, EPS, ALU.mult, ALU.add)
            dve.drain()
            nc.vector.reciprocal(root_[:, 0:TT], mean[:, 0:TT])
            dve.drain()
            tt(root_[:, TT:2 * TT], ps[4][:, 0:TT], root_[:, 0:TT], ALU.mult)
            dve.drain()
            nc.vector.tensor_scalar(mean[:, TT:2 * TT], root_[:, TT:2 * TT], 1.0 / D, EPS, ALU.mult, ALU.add
                                    ).then_inc(ms_ready, 1)
            dve.wait_ge(root_ready, nth(L, 2, 0))
            refine(inverse, root_, mean, root_)
            dve.drain()
            tt(inverse[:, TT:2 * TT], inverse[:, TT:2 * TT], inverse[:, 0:TT], ALU.mult)
            dve.drain()
            for tile_, c in ((2, TT), (3, 0)):
                last = nc.vector.tensor_copy(g[:, tile_, :].rearrange("p (t c) -> p t c", t=TT),
                                             inverse[:, c:c + TT].unsqueeze(2).to_broadcast([P, TT, P]))
            last.then_inc(rms_spread, 1)
            dve.wait_ge(rms_turned, nth(L, 2, 0))

            def modulated(base, e, shift):
                def xm_low(n):
                    dve.wait_ge(xm_hi, base + n + 1)
                    nc.vector.scalar_tensor_tensor(a_lo[:, n, :], g[:, 4 + n % 2, :], mod[:, shift + n:shift + n + 1],
                                                   f32(a_hi[:, n, :]), ALU.add, ALU.subtract).then_inc(xm_split, 1)
                    dve.drain()

                for n in range(KT):
                    nc.vector.scalar_tensor_tensor(g[:, 4 + n % 2, :], x[:, n, :], gs[:, e * KT + n:e * KT + n + 1],
                                                   ps[6][:, :], ALU.mult, ALU.mult).then_inc(xm_ready, 1)
                    if n > 0:
                        xm_low(n - 1)
                xm_low(KT - 1)

            modulated(0, 0, 0)
            for n in range(KT):
                nc.vector.scalar_tensor_tensor(x[:, n, :], x[:, n, :], sp[:, SP_GFIN + n:SP_GFIN + n + 1], ps[4][:, :],
                                               ALU.mult, ALU.mult)

            def qk_columns(e):
                dve.wait_ge(qn_ss, AT * (e + 1))
                nc.vector.tensor_scalar(qcol[:, 0, :], ps[6][:, 0:32], 1.0 / HD, EPS, ALU.mult, ALU.add).then_inc(qn_ms, 1)
                dve.wait_ge(qn_root, e + 1)
                refine(qcol[:, 2, :], qcol[:, 1, :], qcol[:, 0, :], qcol[:, 1, :])
                dve.drain()
                for r in range(AT):
                    nc.vector.tensor_copy(g[:, 2 + r, :].rearrange("p (t c) -> p t c", t=2 * TT),
                                          qcol[:, 2, 8 * r:8 * r + 8].unsqueeze(2).to_broadcast([P, 2 * TT, HD])
                                          ).then_inc(qn_spread, 1)

            def qk_norm(r):
                dst, gain = (q[:, r, :], SP_QG) if r < AT else (k[:, r - AT, :], SP_KG)
                dve.wait_ge(qn_turned, r + 1)
                nc.vector.scalar_tensor_tensor(dst, dst, sp[:, gain:gain + 1], ps[4 + r % 2][:, :], ALU.mult, ALU.mult
                                               ).then_inc(qk_normed, 1)

            for j in range(C_OUT):
                for u in range(2):
                    t = 2 * j + u
                    b = t % 4
                    if t in (AT, 2 * AT):
                        qk_columns(t // AT - 1)
                    for first in (AT + 1, 2 * AT + 1):
                        if t - first in (0, 1):
                            for e in range(2):
                                qk_norm(first - AT - 1 + 2 * (t - first) + e)
                            dve.drain()
                    if j == C_IF:
                        dve.wait_ge(tile_done, nth(L, LAYER_TILES, t))
                        row, col = (row_b, SP_BF) if u else (row_a, SP_BI)
                        nc.vector.tensor_scalar(row, ps[b][0:MH, :], sp[0:MH, col:col + 1], None, ALU.add
                                                ).then_inc(bank_free[b], 1)
                        dve.drain().then_inc(f_ready, 1) if u else dve.drain()
                    if t == 2 * C_IF + 2:
                        dve.wait_ge(f_log, 1)
                        nc.vector.scalar_tensor_tensor(row_g, row_b, 0.0, row_e, ALU.min, ALU.subtract)
                        dve.drain()
                        nc.vector.memset(row_e, 1.0)
                        dve.drain()
                        nc.vector.tensor_tensor_scan(row_b, row_e, row_g, 0.0, ALU.mult, ALU.add)
                        dve.drain()
                        tt(row_a, row_a, row_b, ALU.subtract)
                        dve.drain()
                        nc.vector.tensor_tensor_scan(row_g, row_a, row_a, 0.0, ALU.max, ALU.max)
                        dve.drain()
                        tt(row_b, row_b, row_g, ALU.add).then_inc(m_rows, 1)
                    h, part = divmod(t - HEAD2_SLOT, 2)
                    if part == 0 and 0 <= h < HEADS:
                        if h == 0:
                            dve.wait_ge(second_loaded, 48)
                        mask_scores(L, h, HD ** -0.5)
                    if C_QM <= j < C_VM:
                        i = t - 2 * C_QM
                        o = g[:, 4 + i % 2, :]
                        dve.wait_ge(mc_first, i + 1)
                        for back in (1, 2, 3):
                            w = SP_WCONV + 8 * (3 - back) + i
                            last = nc.vector.scalar_tensor_tensor(o[:, back:], ps[b][:, 0:S - back], sp[:, w:w + 1],
                                                                  o[:, back:], ALU.mult, ALU.add)
                            if back < 3:
                                dve.drain()
                        last.then_inc(bank_free[b], 1)
                        dve.drain().then_inc(mc_ready, 1)
                    if part == 0 and 0 <= h < HEADS:
                        normalise(L, h)
                    if C_QM <= j < C_VM:
                        dve.wait_ge(mc_tanh, i + 1)
                        dst = mq[:, i, :] if i < MH else mk[:, i - MH, :]
                        nc.vector.scalar_tensor_tensor(dst, mt[:, :], 1.0, o, ALU.add, ALU.mult
                                                       ).then_inc(mc_silu, 1)
                    if part == 0 and 2 <= h <= HEADS and h % 2 == 0:
                        y_low(L, h // 2 - 1)

            dve.wait_ge(a_turned, 1)
            nc.vector.tensor_copy(acol[:, :, :, :].rearrange("p e a b -> p (e a b)"), ps[6][:, 0:2 * TT * MH]
                                  ).then_inc(a_cols, 1)
            dve.drain()
            dve.wait_ge(og_ready, 1)

            def m_gaps(h):
                dve.wait_ge(m_bc, h + 1)
                for i in range(TT):
                    nc.vector.tensor_scalar(m_pr[h % 2][:, TRT[i]:TRT[i + 1]], m_bank[h % 2][:, i * P:],
                                            acol[:, 0, i, h:h + 1], 0.0, ALU.subtract, ALU.max)
                dve.drain().then_inc(m_gap, 1)

            def m_mask(h):
                dve.wait_ge(m_decay, h + 1)
                for i in range(TT):
                    d = m_pr[h % 2][:, TRT[i]:TRT[i] + P]
                    tt(d, d, tri, ALU.mult)
                dve.drain()

            def m_finish(h):
                num = g[:, 4 + h, :]
                dve.wait_ge(m_turned, h + 1)
                nc.vector.scalar_tensor_tensor(num, num, sp[:, SP_MG + h:SP_MG + h + 1], ps[4 + h][:, :],
                                               ALU.mult, ALU.mult)
                dve.drain()
                nc.vector.scalar_tensor_tensor(num, og[h], 1.0, num, ALU.add, ALU.mult).then_inc(m_out, 1)
                dve.wait_ge(m_hi, h + 1)
                nc.vector.scalar_tensor_tensor(a_lo[:, h, :], num, 0.5, f32(a_hi[:, h, :]), ALU.mult, ALU.subtract
                                               ).then_inc(m_split, 1)
                dve.drain()

            m_gaps(0)
            m_gaps(1)
            m_mask(0)
            for h in range(MH):
                dve.wait_ge(m_scores, h + 1)
                for i in range(TT):
                    nc.vector.scalar_tensor_tensor(pt[:, TRT[i]:TRT[i + 1]], key_bank[i], 0.25 * P ** -0.5,
                                                   m_pr[h % 2][:, TRT[i]:TRT[i + 1]], ALU.mult, ALU.mult)
                dve.drain().then_inc(m_probs, 1)
                if h + 2 < MH:
                    m_gaps(h + 2)
                if h + 1 < MH:
                    m_mask(h + 1)
            den, ms = mcol[:, 0, :, :], mcol[:, 1, :, :]
            dve.wait_ge(m_ss, MH)
            nc.vector.tensor_scalar(ms, m_cols[:, :, 0, :], -1.0, None, ALU.mult)
            dve.drain()
            tt(den, ms, m_cols[:, :, 0, :], ALU.max)
            dve.drain()
            tt(den, den, acol[:, 1, :, :].rearrange("p t h -> p h t"), ALU.max)
            dve.drain()
            nc.vector.scalar_tensor_tensor(den, den, EPS, den, ALU.mult, ALU.mult)
            dve.drain()
            nc.vector.scalar_tensor_tensor(ms, m_cols[:, :, 1, :], 1.0 / P, den, ALU.mult, ALU.add).then_inc(m_ms, 1)
            dve.wait_ge(m_root, 1)
            refine(mcol[:, 3, :, :], mcol[:, 2, :, :], ms, mcol[:, 2, :, :])
            dve.drain()
            for h in range(MH):
                nc.vector.tensor_copy(k[:, h, :].rearrange("p (t c) -> p t c", t=TT),
                                      mcol[:, 3, h, :].unsqueeze(2).to_broadcast([P, TT, P])).then_inc(m_spread, 1)
            for h in range(MH):
                m_finish(h)

            for n in range(KT):
                t = 2 * C_OUT + n
                dve.wait_ge(tile_done, nth(L, LAYER_TILES, t))
                nc.vector.scalar_tensor_tensor(x[:, n, :], ps[t % 4][:, :], mod[:, 2 * KT + n:2 * KT + n + 1],
                                               x[:, n, :], ALU.mult, ALU.add).then_inc(bank_free[t % 4], 1)
                dve.drain().then_inc(x_ready, 1)
                if n > 0:
                    squares(L, n - 1, 2 * KT + n - 1)
            squares(L, KT - 1, 3 * KT - 1)
            norm(L, 1, copy=False)
            modulated(KT, 1, 3 * KT)
            j, hid = C_FF, 0
            for nt in FF_TILES:
                def h_low(n):
                    dve.wait_ge(h_hi, nth(L, 8 * CHUNKS, n))
                    tt(b_lo[:, n - hid, :], g[:, 6 + n % 2, :], f32(b_hi[:, n - hid, :]), ALU.subtract
                       ).then_inc(h_split, 1)

                for b in range(nt):
                    if b % 2:
                        for u in range(2):
                            t, n = 2 * j + u, hid + b - 1 + u
                            dve.wait_ge(tile_done, nth(L, LAYER_TILES, t))
                            dve.wait_ge(silu_done, n + 1)
                            tt(g[:, 6 + u, :], ps[t % 4][:, :], g[:, 4 + u, :], ALU.mult).then_inc(bank_free[t % 4], 1)
                            dve.drain().then_inc(h_ready, 1)
                        for u in range(2):
                            h_low(hid + b - 1 + u)
                        dve.drain()
                    j += 1
                for n in range(KT):
                    t = 2 * j + n
                    dve.wait_ge(tile_done, nth(L, LAYER_TILES, t))
                    last = nc.vector.scalar_tensor_tensor(x[:, n, :], ps[t % 4][:, :],
                                                          mod[:, 5 * KT + n:5 * KT + n + 1], x[:, n, :],
                                                          ALU.mult, ALU.add)
                    last.then_inc(bank_free[t % 4], 1)
                    if nt == FF_TILES[-1]:
                        dve.drain().then_inc(x_final, 1)
                j += 4
                hid += nt


def rope_constants():
    half = HD // 8
    inv = (1.0 / (np.float32(500000.0) ** (np.arange(0, 2 * half, 2, dtype=np.float32) / np.float32(2 * half)))).astype(np.float32)
    ang = np.arange(S, dtype=np.float32)[:, None] * inv[None, :]
    c = np.zeros((P, 2, S), np.float32)
    for f in range(P):
        c[f, 0, :] = np.cos(ang[:, f % half])
        c[f, 1, :] = np.sin(ang[:, f % half])
    return c


def constant_matrices():
    half = ROTARY // 2
    m = np.zeros((P, K_N), np.float32)
    for base in range(0, P, ROTARY):
        for i in range(half):
            m[base + half + i, K_ROT + base + i] = -1.0
            m[base + i, K_ROT + base + half + i] = 1.0
    for base in (0, HD):
        m[base:base + HD, K_HALF + base:K_HALF + base + HD] = 1.0
    m[:, K_ID:K_ID + P] = np.eye(P, dtype=np.float32)
    m[:, K_ONES:K_ONES + P] = 1.0
    return m


def key_biases():
    t = np.arange(P)
    near = np.where(t[None, :] < (t[:, None] // 64 + 1) * 64, 0.0, NEG).astype(np.float32)
    many = np.zeros((P, TRI[TT]), np.float32)
    for i in range(TT):
        rel = (i * P + t[:, None]) - np.arange((i + 1) * P)[None, :]
        n = sum(((rel >= 0) & (rel % d == 0) & (rel <= w)).astype(np.float32) for w, d in ((128, 1), (512, 4), (2048, 16)))
        many[:, TRI[i]:TRI[i + 1]] = np.where(n > 0, 8.0 * np.log(np.maximum(n, 1.0)), NEG)
    return near, many


def kernel(**inputs):
    import concourse.bacc as bacc
    from concourse.bass_utils import run_bass_kernel_spmd

    a = {n: np.asarray(v) for n, v in inputs.items()}

    def blocks(w):
        depth, cols = w.shape
        wide = BLK * P // depth if depth in (512, 1024) else 256
        n = -(-cols // wide)
        full = np.zeros((max(depth, 512) if depth == 512 else 1024, n * wide), w.dtype)
        full[:depth, :cols] = w
        return full.reshape(-1, P, n, wide).transpose(2, 1, 0, 3).reshape(n, P, BLK)

    parts = []
    for l in range(LAYERS):
        w = a["w_in"][l]
        cut = np.split(w, np.cumsum([512, 512, 512, 256, 64, 4, 512, 512, 512, 1024]), axis=1)
        wq, wk, wv, wiq, wik, wiw, wb, wc, wh, wg0, wg1 = cut
        parts += [blocks(wiq), blocks(np.concatenate([wik, wik, wiw], axis=1)), blocks(wq), blocks(wk), blocks(wv)]
        for pair in range(2):
            parts += [blocks(m[:, 256 * pair:256 * pair + 256]) for m in (wc, wh, wb)]
        parts += [blocks(a["w_conv_out"][l]), blocks(wg1), blocks(wg0), blocks(a["w_attn_out"][l]),
                  blocks(a["w_mix_out"][l])]
        for c in range(CHUNKS):
            parts += [blocks(a["w_mlp_up"][l][:, 1024 * c:1024 * c + 1024]),
                      blocks(a["w_mlp_down"][l][1024 * c:1024 * c + 1024])]
    w = a["w_in_2"][0]
    parts += [blocks(w[:, c:d]) for c, d in ((0, 512), (512, 1024), (1024, 1536), (3584, 3592), (1536, 2048), (2048, 2560),
                                             (2560, 3072), (3072, 3584))]
    parts += [blocks(a["w_out_2"][0])]
    at = 0
    for nt in FF_TILES:
        for i in range(0, nt, 2):
            parts += [blocks(a[m][0][:, at + P * i:at + P * i + 256]) for m in ("w_gate_2", "w_up_2")]
        parts += [blocks(a["w_down_2"][0][at:at + P * nt])]
        at += P * nt
    weights = np.concatenate(parts)
    assert weights.shape[0] == BLOCKS

    def cols(vec):
        return vec.reshape(-1, P).T

    layer_params = np.stack([np.concatenate(
        [cols(a["norm_mlp"][l])] + [cols(a["conv_w"][l][t]) for t in range(3)]
        + [cols(a["norm_mix"][l + 1] if l + 1 < LAYERS else a["norm_final"])], axis=1) for l in range(LAYERS)])

    def rows4(vec):
        full = np.zeros((P, 1), vec.dtype)
        full[:MH, 0] = vec
        return full

    params = np.concatenate(
        [cols(a["g_mix_2"][0]), cols(a["g_ffn_2"][0]), cols(a["norm_final"]), cols(a["b_conv_2"][0])]
        + [cols(a["w_conv_2"][0][t]) for t in range(4)]
        + [np.tile(a["q_norm_g_2"][0], 2)[:, None], np.tile(a["k_norm_g_2"][0], 2)[:, None],
           cols(a["mlstm_norm_g_2"][0]), cols(a["b_ada_2"][0]), cols(a["c_2"][0]),
           rows4(a["b_igate_2"][0]), rows4(a["b_fgate_2"][0]), cols(a["norm_mix"][0])], axis=1)
    near, many = key_biases()
    t = np.arange(P)
    selectors = np.zeros((MH, MH * P), np.float32)
    for h in range(MH):
        selectors[h, h * P:(h + 1) * P] = 1.0
    arrays = {
        "weights": weights,
        "ada": blocks(a["w_ada_2"][0]),
        "consts": constant_matrices(),
        "rope": rope_constants(),
        "tri_bias": near,
        "mult_bias": many,
        "tri_mask": (t[:, None] <= t[None, :]).astype(np.float32),
        "layer_params": layer_params,
        "params": params,
        "x_in": a["x"][0].T,
        "selectors": selectors,
    }
    arrays = {f"in_{n}": np.ascontiguousarray(v) for n, v in arrays.items()}
    nc = bacc.Bacc("TRN2", target_bir_lowering=False, num_devices=1)
    args = [nc.dram_tensor(n, v.shape, mybir.dt.from_np(v.dtype), kind="ExternalInput").ap() for n, v in arrays.items()]
    args.append(nc.dram_tensor("out", (D, S), F32, kind="ExternalOutput").ap())
    two_blocks(nc, *args)
    r = run_bass_kernel_spmd(nc, [arrays], core_ids=[0])
    return np.ascontiguousarray(r.results[0]["out"].T)[None]
```
